# Optimizing a Trainium2 kernel written in Bass

```python
import jax, jax.numpy as jnp
from jax import lax
import numpy as np

D_MODEL = 1024
BATCH = 1
SEQ = 256
DEPTH = 2
DEC_BATCH = 8
DEC_SEQ = 4
PAST_LEN = 1024
PAGE_SIZE = 128

N_EVEN = (DEPTH + 1) // 2
N_ODD = DEPTH // 2

HEAD_DIM = 64
N_Q_HEADS = 8
N_KV_HEADS = 2
Q_PER_KV = N_Q_HEADS // N_KV_HEADS
ROT_DIM = HEAD_DIM // 4
ROPE_THETA = 500000.0
N_IDX_HEADS = 4
IDX_DIM = 64
TOPK_MAX = 256
Q_BLOCK = 128
ATTN_DIM = N_Q_HEADS * HEAD_DIM
KV_DIM = N_KV_HEADS * HEAD_DIM
CONV_DIM = D_MODEL // 2
CONV_W = 3
IN_EVEN_SIZES = (ATTN_DIM, KV_DIM, KV_DIM, N_IDX_HEADS * IDX_DIM, IDX_DIM, N_IDX_HEADS, CONV_DIM, CONV_DIM, CONV_DIM)
IN_EVEN_DIM = sum(IN_EVEN_SIZES)
IN_EVEN_SPLITS = tuple(int(c) for c in np.cumsum(IN_EVEN_SIZES)[:-1])
OUT_EVEN_DIM = ATTN_DIM + CONV_DIM
RWKV_HEAD = 64
RWKV_HEADS = D_MODEL // RWKV_HEAD
LORA_W = 64
LORA_A = 64
LORA_G = 128
GN_EPS = 64e-5
D_FF = 2816
N_EXPERTS = 8
TOP_K_EXPERTS = 2
RMS_EPS = 1e-6

RWKV_NAMES = ('rwkv_mu', 'rwkv_w_rkv', 'rwkv_w0', 'rwkv_w1', 'rwkv_w2', 'rwkv_a0', 'rwkv_a1', 'rwkv_a2',
              'rwkv_g1', 'rwkv_g2', 'rwkv_k_k', 'rwkv_k_a', 'rwkv_r_k', 'rwkv_ln_w', 'rwkv_ln_b', 'rwkv_w_o')

kernel_name = 'dsa_shortconv_rwkv7_moe_step'

def rms_norm(x, g):
    xf = x.astype(jnp.float32)
    xf = xf * lax.rsqrt(jnp.mean(xf * xf, axis=-1, keepdims=True) + RMS_EPS)
    return (xf * g.astype(jnp.float32)).astype(x.dtype)

def partial_rope(x, pos):
    half = ROT_DIM // 2
    inv_freq = ROPE_THETA ** (-jnp.arange(half, dtype=jnp.float32) / half)
    ang = pos.astype(jnp.float32)[:, None] * inv_freq[None, :]
    cos = jnp.cos(ang)[:, None, :]
    sin = jnp.sin(ang)[:, None, :]
    xr = x[..., :ROT_DIM].astype(jnp.float32)
    x1, x2 = xr[..., :half], xr[..., half:]
    rot = jnp.concatenate([x1 * cos - x2 * sin, x2 * cos + x1 * sin], axis=-1)
    return jnp.concatenate([rot.astype(x.dtype), x[..., ROT_DIM:]], axis=-1)

def take_rows(rows, idx):
    return jax.vmap(lambda r, i: r[i])(rows, idx)

def project_even(xn, pos, w_in):
    B, T, _ = xn.shape
    h = xn @ w_in
    q, k, v, iq, ik, iw, cb, cc, ch = jnp.split(h, IN_EVEN_SPLITS, axis=-1)
    q = partial_rope(q.reshape(B, T, N_Q_HEADS, HEAD_DIM), pos)
    k = partial_rope(k.reshape(B, T, N_KV_HEADS, HEAD_DIM), pos)
    v = v.reshape(B, T, N_KV_HEADS, HEAD_DIM)
    iq = partial_rope(iq.reshape(B, T, N_IDX_HEADS, IDX_DIM), pos)
    ik = partial_rope(ik[:, :, None, :], pos)[:, :, 0]
    return q, k, v, iq, ik, iw, cb, cc, ch

def index_scores(iq, ik, iw):
    s = jnp.einsum('bthd,bsd->bths', iq, ik).astype(jnp.float32) * (IDX_DIM ** -0.5)
    w = iw.astype(jnp.float32) * (N_IDX_HEADS ** -0.5)
    return jnp.einsum('bths,bth->bts', jax.nn.relu(s), w)

def sparse_attend(q, k_sel, v_sel, valid):
    B, T = q.shape[:2]
    qg = q.reshape(B, T, N_KV_HEADS, Q_PER_KV, HEAD_DIM)
    s = jnp.einsum('btgrd,btkgd->btgrk', qg, k_sel).astype(jnp.float32) * (HEAD_DIM ** -0.5)
    s = jnp.where(valid[:, :, None, None, :], s, -jnp.inf)
    p = jax.nn.softmax(s, axis=-1).astype(v_sel.dtype)
    o = jnp.einsum('btgrk,btkgd->btgrd', p, v_sel)
    return o.reshape(B, T, ATTN_DIM)

def prompt_sparse_attention(q, k, v, iq, ik, iw):
    B, T = q.shape[:2]
    n_sel = min(TOPK_MAX, T // 4)
    key_pos = jnp.arange(T)

    def block(i):
        t0 = i * Q_BLOCK
        qb = lax.dynamic_slice_in_dim(q, t0, Q_BLOCK, axis=1)
        iqb = lax.dynamic_slice_in_dim(iq, t0, Q_BLOCK, axis=1)
        iwb = lax.dynamic_slice_in_dim(iw, t0, Q_BLOCK, axis=1)
        tq = t0 + jnp.arange(Q_BLOCK)
        causal = key_pos[None, :] <= tq[:, None]
        scores = jnp.where(causal[None], index_scores(iqb, ik, iwb), -jnp.inf)
        _, sel = lax.top_k(scores, n_sel)
        valid = sel <= tq[None, :, None]
        return sparse_attend(qb, take_rows(k, sel), take_rows(v, sel), valid)

    out = lax.map(block, jnp.arange(T // Q_BLOCK))
    return jnp.transpose(out, (1, 0, 2, 3)).reshape(B, T, ATTN_DIM)

def sample_sparse_attention(q, k_new, v_new, iq, ik_new, iw, cache_k, cache_v, cache_ik, page_table):
    Bd, Tn = q.shape[:2]
    past = page_table.shape[1] * PAGE_SIZE
    n_keys = past + Tn
    n_sel = min(TOPK_MAX, n_keys // 4)
    ik_past = cache_ik[page_table].reshape(Bd, past, IDX_DIM).astype(ik_new.dtype)
    ik_all = jnp.concatenate([ik_past, ik_new], axis=1)
    tq = past + jnp.arange(Tn)
    causal = jnp.arange(n_keys)[None, :] <= tq[:, None]
    scores = jnp.where(causal[None], index_scores(iq, ik_all, iw), -jnp.inf)
    _, sel = lax.top_k(scores, n_sel)
    valid = sel <= tq[None, :, None]
    in_past = (sel < past)[..., None, None]
    sp = jnp.minimum(sel, past - 1)
    phys = take_rows(page_table, sp // PAGE_SIZE) * PAGE_SIZE + sp % PAGE_SIZE
    sn = jnp.clip(sel - past, 0, Tn - 1)
    k_pool = cache_k.reshape(-1, N_KV_HEADS, HEAD_DIM)
    v_pool = cache_v.reshape(-1, N_KV_HEADS, HEAD_DIM)
    k_sel = jnp.where(in_past, k_pool[phys].astype(k_new.dtype), take_rows(k_new, sn))
    v_sel = jnp.where(in_past, v_pool[phys].astype(v_new.dtype), take_rows(v_new, sn))
    return sparse_attend(q, k_sel, v_sel, valid)

def short_conv(cb, cc, ch, conv_w, prev):
    T = cb.shape[1]
    u = jnp.concatenate([prev.astype(cb.dtype), cc * ch], axis=1)
    y = sum(conv_w[j] * u[:, j:j + T] for j in range(CONV_W))
    return cb * y, u[:, T:]

def swiglu(x, w_gate, w_up, w_down):
    return (jax.nn.silu(x @ w_gate) * (x @ w_up)) @ w_down

def moe_swiglu(x, w_router, w_gate, w_up, w_down):
    logits = (x @ w_router).astype(jnp.float32)
    top_val, top_idx = lax.top_k(logits, TOP_K_EXPERTS)
    gate = jax.nn.softmax(top_val, axis=-1)
    combine = jnp.einsum('btk,btke->bte', gate, jax.nn.one_hot(top_idx, N_EXPERTS, dtype=jnp.float32)).astype(x.dtype)
    out = jnp.zeros_like(x)
    for e in range(N_EXPERTS):
        out = out + combine[..., e:e + 1] * swiglu(x, w_gate[e], w_up[e], w_down[e])
    return out

def rwkv7_time_mix(xn, shift_prev, wkv_prev, mu, w_rkv, w0, w1, w2, a0, a1, a2, g1, g2,
                   k_k, k_a, r_k, ln_w, ln_b, w_o):
    B, T, D = xn.shape
    f32 = jnp.float32
    x_prev = jnp.concatenate([shift_prev[:, None].astype(xn.dtype), xn[:, :-1]], axis=1)
    xx = x_prev - xn
    xr, xw, xk, xv, xa, xg = [xn + xx * mu[i] for i in range(6)]
    r = xr @ w_rkv[0]
    k = xk @ w_rkv[1]
    v = xv @ w_rkv[2]
    w_log = -jax.nn.softplus(-(w0 + jnp.tanh(xw @ w1) @ w2).astype(f32)) - 0.5
    decay = jnp.exp(-jnp.exp(w_log))
    a = jax.nn.sigmoid(a0 + (xa @ a1) @ a2)
    g = jax.nn.sigmoid(xg @ g1) @ g2

    def heads(z):
        return z.reshape(B, T, RWKV_HEADS, RWKV_HEAD).astype(f32)

    kk = heads(k * k_k)
    kk = kk * lax.rsqrt(jnp.maximum(jnp.sum(kk * kk, axis=-1, keepdims=True), 1e-24))
    k = k * (1 + (a - 1) * k_a)
    rh, kh, vh, ah, wh = heads(r), heads(k), heads(v), heads(a), heads(decay)

    def step(S, inp):
        r_t, w_t, k_t, v_t, kk_t, a_t = inp
        sa = jnp.einsum('bhvk,bhk->bhv', S, -kk_t)
        S = S * w_t[:, :, None, :] + sa[..., None] * (kk_t * a_t)[:, :, None, :] + v_t[..., None] * k_t[:, :, None, :]
        return S, jnp.einsum('bhvk,bhk->bhv', S, r_t)

    seq = tuple(jnp.swapaxes(z, 0, 1) for z in (rh, wh, kh, vh, kk, ah))
    S, y = lax.scan(step, wkv_prev.astype(f32), seq)
    y = jnp.swapaxes(y, 0, 1)
    mean = jnp.mean(y, axis=-1, keepdims=True)
    var = jnp.mean(jnp.square(y - mean), axis=-1, keepdims=True)
    y = (y - mean) * lax.rsqrt(var + GN_EPS)
    y = y * ln_w.astype(f32).reshape(RWKV_HEADS, RWKV_HEAD) + ln_b.astype(f32).reshape(RWKV_HEADS, RWKV_HEAD)
    y = y + jnp.sum(rh * kh * r_k.astype(f32), axis=-1, keepdims=True) * vh
    out = (y.reshape(B, T, D).astype(xn.dtype) * g) @ w_o
    return out, xn[:, -1], S.astype(wkv_prev.dtype)

def trunk(x, pos, conv_prev, shift_prev, wkv_prev, attend, p):
    rows_k, rows_v, rows_ik, conv_new, shift_new, wkv_new = [], [], [], [], [], []
    for layer in range(DEPTH):
        i = layer // 2
        if layer % 2 == 0:
            xn = rms_norm(x, p['norm_mix_even'][i])
            q, k, v, iq, ik, iw, cb, cc, ch = project_even(xn, pos, p['w_in_even'][i])
            attn = attend(i, q, k, v, iq, ik, iw)
            conv, conv_state = short_conv(cb, cc, ch, p['conv_w'][i], conv_prev[i])
            x = x + jnp.concatenate([attn, conv], axis=-1) @ p['w_out_even'][i]
            x = x + swiglu(rms_norm(x, p['norm_ffn_even'][i]), p['ffn_gate'][i], p['ffn_up'][i], p['ffn_down'][i])
            rows_k.append(k)
            rows_v.append(v)
            rows_ik.append(ik)
            conv_new.append(conv_state)
        else:
            xn = rms_norm(x, p['norm_mix_odd'][i])
            mix, shift_state, wkv_state = rwkv7_time_mix(xn, shift_prev[i], wkv_prev[i], *(p[n][i] for n in RWKV_NAMES))
            x = x + mix
            x = x + moe_swiglu(rms_norm(x, p['norm_ffn_odd'][i]), p['moe_router'][i], p['moe_gate'][i],
                               p['moe_up'][i], p['moe_down'][i])
            shift_new.append(shift_state)
            wkv_new.append(wkv_state)
    y = rms_norm(x, p['norm_final'])
    return (y, jnp.stack(rows_k), jnp.stack(rows_v), jnp.stack(rows_ik), jnp.stack(conv_new),
            jnp.stack(shift_new), jnp.stack(wkv_new))

def setup_inputs(seed: int = 0) -> dict:
    key = jax.random.key(seed)
    ks = iter(jax.random.split(key, 64))

    def nrm(shape, scale):
        return jax.random.normal(next(ks), shape, jnp.float32) * scale

    def gain(shape):
        return 1.0 + nrm(shape, 0.05)

    n_pages = PAST_LEN // PAGE_SIZE
    used = DEC_BATCH * n_pages
    n_pool = used + max(1, used // 4)
    E, O = N_EVEN, N_ODD
    D, H, N = D_MODEL, RWKV_HEADS, RWKV_HEAD
    return {
        'x_prompt': nrm((BATCH, SEQ, D), 1.0),
        'x_sample': nrm((DEC_BATCH, DEC_SEQ, D), 1.0),
        'cache_k': nrm((E, n_pool, PAGE_SIZE, N_KV_HEADS, HEAD_DIM), 1.0),
        'cache_v': nrm((E, n_pool, PAGE_SIZE, N_KV_HEADS, HEAD_DIM), 1.0),
        'cache_idx_k': nrm((E, n_pool, PAGE_SIZE, IDX_DIM), 1.0),
        'state_conv': nrm((E, DEC_BATCH, CONV_W - 1, CONV_DIM), 1.0),
        'state_shift': nrm((O, DEC_BATCH, D), 1.0),
        'state_wkv': nrm((O, DEC_BATCH, H, N, N), 0.5),
        'page_table': jax.random.permutation(next(ks), n_pool)[:used].reshape(DEC_BATCH, n_pages).astype(jnp.int32),
        'norm_mix_even': gain((E, D)),
        'w_in_even': nrm((E, D, IN_EVEN_DIM), D ** -0.5),
        'conv_w': nrm((E, CONV_W, CONV_DIM), CONV_W ** -0.5),
        'w_out_even': nrm((E, OUT_EVEN_DIM, D), OUT_EVEN_DIM ** -0.5),
        'norm_ffn_even': gain((E, D)),
        'ffn_gate': nrm((E, D, D_FF), D ** -0.5),
        'ffn_up': nrm((E, D, D_FF), D ** -0.5),
        'ffn_down': nrm((E, D_FF, D), D_FF ** -0.5),
        'norm_mix_odd': gain((O, D)),
        'rwkv_mu': jax.random.uniform(next(ks), (O, 6, D), jnp.float32),
        'rwkv_w_rkv': nrm((O, 3, D, D), D ** -0.5),
        'rwkv_w0': nrm((O, D), 0.5),
        'rwkv_w1': nrm((O, D, LORA_W), D ** -0.5),
        'rwkv_w2': nrm((O, LORA_W, D), 0.5 * LORA_W ** -0.5),
        'rwkv_a0': nrm((O, D), 0.1),
        'rwkv_a1': nrm((O, D, LORA_A), D ** -0.5),
        'rwkv_a2': nrm((O, LORA_A, D), LORA_A ** -0.5),
        'rwkv_g1': nrm((O, D, LORA_G), D ** -0.5),
        'rwkv_g2': nrm((O, LORA_G, D), LORA_G ** -0.5),
        'rwkv_k_k': 0.85 + nrm((O, D), 0.05),
        'rwkv_k_a': gain((O, D)),
        'rwkv_r_k': nrm((O, H, N), 0.1),
        'rwkv_ln_w': gain((O, D)),
        'rwkv_ln_b': nrm((O, D), 0.02),
        'rwkv_w_o': nrm((O, D, D), D ** -0.5),
        'norm_ffn_odd': gain((O, D)),
        'moe_router': nrm((O, D, N_EXPERTS), D ** -0.5),
        'moe_gate': nrm((O, N_EXPERTS, D, D_FF), D ** -0.5),
        'moe_up': nrm((O, N_EXPERTS, D, D_FF), D ** -0.5),
        'moe_down': nrm((O, N_EXPERTS, D_FF, D), D_FF ** -0.5),
        'norm_final': gain((D,)),
    }

def reference(x_prompt, x_sample, cache_k, cache_v, cache_idx_k, state_conv, state_shift, state_wkv, page_table,
              norm_mix_even, w_in_even, conv_w, w_out_even, norm_ffn_even, ffn_gate, ffn_up, ffn_down,
              norm_mix_odd, rwkv_mu, rwkv_w_rkv, rwkv_w0, rwkv_w1, rwkv_w2, rwkv_a0, rwkv_a1, rwkv_a2,
              rwkv_g1, rwkv_g2, rwkv_k_k, rwkv_k_a, rwkv_r_k, rwkv_ln_w, rwkv_ln_b, rwkv_w_o,
              norm_ffn_odd, moe_router, moe_gate, moe_up, moe_down, norm_final):
    p = dict(norm_mix_even=norm_mix_even, w_in_even=w_in_even, conv_w=conv_w, w_out_even=w_out_even,
             norm_ffn_even=norm_ffn_even, ffn_gate=ffn_gate, ffn_up=ffn_up, ffn_down=ffn_down,
             norm_mix_odd=norm_mix_odd, rwkv_mu=rwkv_mu, rwkv_w_rkv=rwkv_w_rkv, rwkv_w0=rwkv_w0,
             rwkv_w1=rwkv_w1, rwkv_w2=rwkv_w2, rwkv_a0=rwkv_a0, rwkv_a1=rwkv_a1, rwkv_a2=rwkv_a2,
             rwkv_g1=rwkv_g1, rwkv_g2=rwkv_g2, rwkv_k_k=rwkv_k_k, rwkv_k_a=rwkv_k_a, rwkv_r_k=rwkv_r_k,
             rwkv_ln_w=rwkv_ln_w, rwkv_ln_b=rwkv_ln_b, rwkv_w_o=rwkv_w_o, norm_ffn_odd=norm_ffn_odd,
             moe_router=moe_router, moe_gate=moe_gate, moe_up=moe_up, moe_down=moe_down, norm_final=norm_final)
    B, T = x_prompt.shape[:2]
    Tn = x_sample.shape[1]
    past = page_table.shape[1] * PAGE_SIZE
    pos_prompt = jnp.arange(T, dtype=jnp.int32)
    pos_sample = past + jnp.arange(Tn, dtype=jnp.int32)

    conv0 = jnp.zeros((N_EVEN, B, CONV_W - 1, CONV_DIM), x_prompt.dtype)
    shift0 = jnp.zeros((N_ODD, B, D_MODEL), x_prompt.dtype)
    wkv0 = jnp.zeros((N_ODD, B, RWKV_HEADS, RWKV_HEAD, RWKV_HEAD), state_wkv.dtype)

    def attend_prompt(i, q, k, v, iq, ik, iw):
        return prompt_sparse_attention(q, k, v, iq, ik, iw)

    def attend_sample(i, q, k, v, iq, ik, iw):
        return sample_sparse_attention(q, k, v, iq, ik, iw, cache_k[i], cache_v[i], cache_idx_k[i], page_table)

    y_prompt, k_p, v_p, ik_p, conv_p, shift_p, wkv_p = trunk(
        x_prompt, pos_prompt, conv0, shift0, wkv0, attend_prompt, p)
    y_sample, k_s, v_s, ik_s, conv_s, shift_s, wkv_s = trunk(
        x_sample, pos_sample, state_conv, state_shift, state_wkv, attend_sample, p)
    return (y_prompt, y_sample, k_p, v_p, ik_p, k_s, v_s, ik_s, conv_p, conv_s, shift_p, shift_s, wkv_p, wkv_s)


_drawn_inputs = setup_inputs


def setup_inputs(seed=0):
    import zlib

    import numpy as np

    out = dict(_drawn_inputs(seed))
    spreads = {}
    factors = {}
    for name, (base, spread) in spreads.items():
        noise = np.random.default_rng([zlib.crc32(name.encode()), seed]).standard_normal(out[name].shape)
        drawn = base * np.exp(spread * noise) if base else spread * noise
        out[name] = __import__('jax').numpy.asarray(drawn.astype(out[name].dtype))
    for name, factor in factors.items():
        out[name] = (out[name] * factor).astype(out[name].dtype)
    return out
```

```python
from contextlib import ExitStack

import numpy as np

import concourse.bass as bass
from concourse import mybir

F32 = mybir.dt.float32
I32 = mybir.dt.int32
U32 = mybir.dt.uint32
ALU = mybir.AluOpType
ACT = mybir.ActivationFunctionType
AX = mybir.AxisListType

P = 128
D = 1024
KC = D // P
TP = 256
NB, TS = 8, 4
NS = NB * TS
T = TP + NS
TILES = ((0, 128), (128, 128), (256, NS))
HD = 64
NQ, NKV, NIH = 8, 2, 4
PAST, PAGE, NPG = 1024, 128, 8
NK = PAST + TS
SEL_P, SEL_S = 64, 256
CONV = 512
FF = 2816
FC = FF // P
NE = 8
RH = 16
CH = 64
NCH = TP // CH
CAP = 96
EPS = 1e-6
GN_EPS = 64e-5
NEG = -1.0e30
TAKEN = -3.0e38
RING = 11
SLOT = 1024

Q0, K0, V0, IQ0, IK0, IW0, CB0, CC0, CH0 = 0, 512, 640, 768, 1024, 1088, 1092, 1604, 2116

VEC_NAMES = ["norm_mix_even", "norm_ffn_even", "norm_mix_odd", "norm_ffn_odd", "mu", "rwkv_w0", "rwkv_a0",
             "rwkv_k_k", "rwkv_k_a", "rwkv_r_k", "rwkv_ln_w"]
VEC = {}
_at = 0
for _n in VEC_NAMES:
    VEC[_n] = _at
    _at += 48 if _n == "mu" else 8
VEC["rwkv_ln_b"] = 128
VEC["conv_w"] = 136
VEC["state_shift"] = 148
VEC["state_conv"] = 256


def constants():
    p = np.arange(P)
    c = {}
    c["ident"] = np.eye(P)
    c["ones"] = np.ones((P, P))
    c["headones"] = (p[:, None] // HD == p[None, :] // HD).astype(np.float32)
    rot = np.zeros((P, P))
    for h in (0, HD):
        for i in range(8):
            rot[h + 8 + i, h + i] = -1.0
            rot[h + i, h + 8 + i] = 1.0
    c["rot"] = rot
    pos = np.concatenate([np.arange(TP), np.tile(PAST + np.arange(TS), NB)]).astype(np.float32)
    inv = (np.float32(500000.0) ** (-np.arange(8, dtype=np.float32) / np.float32(8))).astype(np.float32)
    ang = inv[:, None] * pos[None, :]
    cos, sin = np.ones((P, T)), np.zeros((P, T))
    for h in (0, HD):
        for half in (0, 8):
            cos[h + half:h + half + 8] = np.cos(ang.astype(np.float64))
            sin[h + half:h + half + 8] = np.sin(ang.astype(np.float64))
    c["cos"], c["sin"] = cos, sin
    c["causal"] = np.concatenate([np.where(np.arange(TP)[None] <= (i * P + p)[:, None], 0.0, NEG)
                                  for i in range(2)], 1)
    new = np.zeros((P, TS))
    new[:NS] = np.where(np.arange(TS)[None] <= (np.arange(NS) % TS)[:, None], 0.0, NEG)
    c["causal_new"] = new
    selh = np.zeros((P, 2, NS))
    selm = np.zeros((P, 2, P))
    for g in range(2):
        for b in range(4):
            for t in range(TS):
                for h in range(NIH):
                    selh[32 * b + 4 * t + h, g, (4 * g + b) * TS + t] = 1.0
                for h in range(NQ):
                    selm[(4 * g + b) * TS + t, g, 32 * b + 4 * h + t] = 1.0
    c["sel_sum"], c["sel_spread"] = selh.reshape(P, -1), selm.reshape(P, -1)
    s, t = (p % CH)[:, None], (p % CH)[None, :]
    c["delta_mask"] = np.where(p[None, :] < CH, s < t, s <= t)
    lo = np.zeros((P, 6, CH))
    for j in range(6):
        b = 1 << j
        tt, ss = (p % CH)[:, None], np.arange(CH)[None, :]
        lo[:, j] = (tt // (2 * b) == ss // (2 * b)) & (tt % (2 * b) >= b) & (ss % (2 * b) < b)
    c["levels"] = lo.reshape(P, -1)
    c["ident64"] = np.concatenate([np.eye(CH), np.eye(CH)], 0)
    c["before"] = p[:, None] < p[None, :]
    c["slots"] = np.tile(np.arange(P)[None], (P, 1))
    return {k: np.asarray(v, np.float32) for k, v in c.items()}


CONSTS = constants()
COL = {}
_at = 0
for _n, _v in CONSTS.items():
    COL[_n] = (_at, _at + _v.shape[1])
    _at += _v.shape[1]
NCOL = _at


class Plan:

    def __init__(self):
        self.items = []

    def add(self, name, pieces, freed_by, value):
        self.items.append((name, pieces, freed_by, value))


def build(nc, I, O):
    ctx = ExitStack()
    place = [16512]

    def sbt(name, shape, dtype=F32, at=None):
        n = int(np.prod(shape[1:])) * 4
        n = (n + 31) // 32 * 32
        if at is None:
            at = place[0]
            place[0] += n
        assert at + n <= 229344, (name, at + n)
        t = nc.alloc_sbuf_tensor_at(name, list(shape), dtype, offset=at)
        ends[name] = at + n
        starts[name] = at
        return t

    ends, starts = {}, {}

    def sem(name):
        return ctx.enter_context(nc.semaphore(name))

    ring = [sbt(f"ring{i}", [P, SLOT]) for i in range(RING)]
    cst = sbt("cst", [P, NCOL])
    C = {k: cst[:, a:b] for k, (a, b) in COL.items()}
    vecT = sbt("vecT", [P, 2 * P + 64])
    xT = sbt("xT", [P, KC, T])
    ms = sbt("ms", [P, T])
    rs = sbt("rs", [P, T])
    arena = place[0]
    bk = [nc.alloc_psum_tensor(f"bk{i}", [P, 512], F32) for i in range(8)]

    x_rows = sbt("x_rows", [P, 3, D])
    sq = sbt("sq", [P, KC, T], at=starts["x_rows"])
    probsT = sbt("probsT", [P, 3, NQ, P], at=starts["x_rows"])
    xn = sbt("xn", [P, KC, T])
    raw = sbt("raw", [P, 9, T])
    rp = sbt("rp", [P, 8, T])
    ccb = sbt("ccb", [P, 3, 4, T])
    probs = sbt("probs", [P, 2, NQ, TP])
    mixT = sbt("mixT", [P, KC, T])
    rows = sbt("rows", [P, 3, 3, P])
    iw = sbt("iw", [P, 3, NIH])
    vec_rows = sbt("vec_rows", [P, 3, P])
    sc_p = sbt("sc_p", [P, 2, TP])
    tmp_p = sbt("tmp_p", [P, 4, TP])
    top8 = sbt("top8", [P, 8])
    mxp = sbt("mxp", [P, 2, NQ])
    smp = sbt("smp", [P, 2, NQ])
    pg_ids = sbt("pg_ids", [1, NB * NPG], I32)
    k_pages = sbt("k_pages", [P, NPG, P])
    ik_pages = sbt("ik_pages", [P, NPG, 2, HD])
    keysT = sbt("keysT", [P, NK])
    ikeysT = sbt("ikeysT", [P, NK])
    pS_T = sbt("pS_T", [P, 9, P], at=starts["k_pages"])
    v_pages = sbt("v_pages", [P, 2, NPG, P])
    v_new = sbt("v_new", [TS, NB, P])
    q_s = sbt("q_s", [P, NB, 32])
    iq_s = sbt("iq_s", [P, NB, 32])
    iw_s = sbt("iw_s", [P, 2])
    idx_s = sbt("idx_s", [P, 2, NK])
    att_s = sbt("att_s", [P, 2, NK])
    sc_s = sbt("sc_s", [NS, NK], at=starts["ikeysT"])
    mxs = sbt("mxs", [P, 2])
    sms = sbt("sms", [P, 2])
    u_p = sbt("u_p", [P, 4, 2 + TP], at=starts["xn"])
    u_s = sbt("u_s", [P, 4, NB, 2 + TS], at=starts["xn"] + 4 * 4 * (2 + TP))
    u_last = sbt("u_last", [P, 4, 2 + 2 * NB])
    conv_rows = sbt("conv_rows", [2 + 2 * NB, CONV])
    print("layer 0 arena ends", place[0])

    place[0] = arena
    sq1 = sbt("sq1", [P, KC, T])
    xn1 = sbt("xn1", [P, KC, T])
    hid = sbt("hid", [P, FC, T])
    sg = sbt("sg", [P, 2, T])


    place[0] = arena
    rT = sbt("rT", [P, KC, T])
    kT = sbt("kT", [P, KC, T])
    aT = sbt("aT", [P, KC, T])
    lwT = sbt("lwT", [P, KC, T])
    vT = sbt("vT", [P, KC, T])
    gT = sbt("gT", [P, KC, T])
    xn2 = sbt("xn2", [P, KC, T])
    xx = sbt("xx", [P, KC, T])
    mx = sbt("mx", [P, 2, KC, T])
    sq2 = sbt("sq2", [P, KC, T], at=starts["mx"])
    G = sbt("G", [P, 2, 2, KC, P])
    L = sbt("L", [P, 2, KC, CH])
    Cj = sbt("Cj", [P, 2, KC, CH])
    M = sbt("M", [P, 2, KC, CH])
    X = sbt("X", [P, 2, KC, CH])
    Y = sbt("Y", [P, 2, KC, CH])
    Z = sbt("Z", [P, 2, KC, 2, CH])
    s6 = sbt("s6", [P, TS, 6, HD])
    omk = sbt("omk", [P, KC])
    gst = sbt("gst", [P, RH])
    gst2 = sbt("gst2", [P, RH])
    print("rwkv arena ends", place[0])
    t1, t2, t3, t4 = (sbt(f"t{i + 1}", [P, KC, T], at=starts["G"] + 9216 * i) for i in range(4))
    bon = sbt("bon", [P, 7, T], at=starts["G"] + 4 * 9216)
    st = sbt("st", [NS, 2, D], at=starts["G"] + 4 * 9216)
    lh = sbt("lh", [P, 3, T], at=starts["G"])
    e_last = sbt("e_last", [P, KC, 1 + NB], at=starts["G"] + 4096)
    shift_rows = sbt("shift_rows", [1 + NB, D], at=starts["G"] + 5120)
    AR = sbt("AR", [P, KC, NCH, 2, CH], at=starts["xn2"])
    BK = sbt("BK", [P, KC, NCH, 2, CH], at=starts["xn2"] + 16384)
    ST = sbt("ST", [P, KC, CH], at=starts["xn2"] + 32768)
    PC = sbt("PC", [P, KC, NCH], at=starts["xn2"] + 32768 + 2048)
    S = sbt("S", [P, HD, HD], at=starts["rT"])
    y_rows = sbt("y_rows", [P, 3, D], at=starts["rT"] + 16384)
    stmp = sbt("stmp", [P, HD // 2, HD], at=starts["rT"] + 16384 + 12288)
    sa = sbt("sa", [P, HD], at=starts["xn2"] + 32768 + 2048 + 128)
    ys = sbt("ys", [P, TS, HD], at=starts["xn2"] + 32768 + 2048 + 128 + 256)
    BKt = sbt("BKt", [P, 2, KC, P], at=starts["L"])
    bonT = sbt("bonT", [P, KC, T], at=starts["G"])
    oT = sbt("oT", [P, KC, T], at=starts["xn2"])
    gsq = sbt("gsq", [P, D], at=starts["L"])
    st_rows = sbt("st_rows", [HD, RH, HD], at=starts["X"])
    q6_dram = nc.dram_tensor("q6_dram", [NS, 6, D], F32, kind="Internal").ap()
    bon_dram = nc.dram_tensor("bon_dram", [P, KC, T], F32, kind="Internal").ap()
    ys_dram = nc.dram_tensor("ys_dram", [NB, TS, RH, HD], F32, kind="Internal").ap()

    place[0] = arena
    xn3 = sbt("xn3", [P, KC, T])
    sq3 = sbt("sq3", [P, KC, T])
    acc = sbt("acc", [P, 3, D])
    xr = sbt("xr", [P, 3, D])
    w_rt = sbt("w_rt", [P, KC, NE])
    lg = sbt("lg", [P, 3, NE])
    top_v = sbt("top_v", [P, 3, NE])
    top_i = sbt("top_i", [P, 3, NE], U32)
    top_f = sbt("top_f", [P, 3, NE])
    hot1 = sbt("hot1", [P, 3, NE])
    hot2 = sbt("hot2", [P, 3, NE])
    sel = sbt("sel", [P, 3, NE])
    comb = sbt("comb", [P, 3, NE])
    gates = sbt("gates", [P, 3, 2])
    NIT = NE * (T // CAP)
    rank = sbt("rank", [P, 3, NIT + NE])
    share = sbt("share", [P, 3, NIT + NE])
    blocks_f = sbt("blocks_f", [1, 4])
    blocks = sbt("blocks", [1, 1], I32)
    pick = sbt("pick", [P, 3, CAP])
    give = sbt("give", [P, 3, CAP])
    giveT = sbt("giveT", [CAP, T])
    xg = sbt("xg", [P, KC, CAP])
    hid2 = sbt("hid2", [P, FC, CAP])
    sg2 = sbt("sg2", [P, 2, CAP])
    ye = sbt("ye", [CAP, D])
    gain_f = sbt("gain_f", [P, D])
    y_out = sbt("y_out", [P, 3, D])
    ssf = sbt("ssf", [P, 3])
    iw_dram = nc.dram_tensor("iw_dram", [NS, NIH], F32, kind="Internal").ap()
    N_POOL = I["cache_k"].shape[1]
    OUT_0 = 7
    OUT_1 = OUT_0 + 2
    N_OUT = OUT_1 + 2 + 2

    head_in = sem("head_in")
    HEAD = 16 * (3 + len(VEC_NAMES) + 4)
    slot_in = [sem(f"slot_in{i}") for i in range(RING)]
    out_done = sem("out_done")
    dve_chain, act_chain, pool_chain = sem("dve_chain"), sem("act_chain"), sem("pool_chain")
    vec_mm, vec_ok = sem("vec_mm"), sem("vec_ok")
    xT_mm, xT_ok = sem("xT_mm"), sem("xT_ok")
    sq_ok, ssq_mm, ms_ok, sd_ok, xn_ok = sem("sq_ok"), sem("ssq_mm"), sem("ms_ok"), sem("sd_ok"), sem("xn_ok")
    job_mm, job_ok = sem("job_mm"), sem("job_ok")
    iw_mm, iw_ok, iw_out, iws_in = sem("iw_mm"), sem("iw_ok"), sem("iw_out"), sem("iws_in")
    rot_mm, rope_ok, rope_pool = sem("rot_mm"), sem("rope_ok"), sem("rope_pool")
    qs_ok = sem("qs_ok")
    turn_mm, turn_ok = sem("turn_mm"), sem("turn_ok")
    temp_out, vnew_in = sem("temp_out"), sem("vnew_in")
    ids_in, page_in, new_ok = sem("ids_in"), sem("page_in"), sem("new_ok")
    kT_mm, kT_ok, qk_mm, qk_ok = sem("kT_mm"), sem("kT_ok"), sem("qk_mm"), sem("qk_ok")
    ikT_mm, ikT_ok, idx_mm, idx_ok = sem("ikT_mm"), sem("ikT_ok"), sem("idx_mm"), sem("idx_ok")
    isum_mm, sel_ok, spread_mm, att_ok = sem("isum_mm"), sem("sel_ok"), sem("spread_mm"), sem("att_ok")
    exps_ok, ps_ok, psT_mm, psT_ok = sem("exps_ok"), sem("ps_ok"), sem("psT_mm"), sem("psT_ok")
    vpage_in = [sem("vpage_in0"), sem("vpage_in1")]
    pvs_mm, pvs_ok = sem("pvs_mm"), sem("pvs_ok")
    ip_mm, ip_ok = sem("ip_mm"), sem("ip_ok")
    sp_mm, sp_ok, shift_ok, expp_ok = sem("sp_mm"), sem("sp_ok"), sem("shift_ok"), sem("expp_ok")
    pp_ok, ppT_mm, ppT_ok, pvp_mm, pvp_ok = sem("pp_ok"), sem("ppT_mm"), sem("ppT_ok"), sem("pvp_mm"), sem("pvp_ok")
    conv_ok = sem("conv_ok")
    om_mm, om_ok = sem("om_mm"), sem("om_ok")
    gu_mm, silu_ok, hid_ok, down_mm, down_ok = sem("gu_mm"), sem("silu_ok"), sem("hid_ok"), sem("down_mm"), sem("down_ok")


    xx_ok, mix_ok, lh_mm, lh_ok = (sem(n) for n in ("xx_ok", "mix_ok", "lh_mm", "lh_ok"))
    el_ok = sem("el_ok")
    t1_ok, sqk_ok, hs_mm, nk_ok, nsq_ok = (sem(n) for n in ("t1_ok", "sqk_ok", "hs_mm", "nk_ok", "nsq_ok"))
    rk_ok, bn_ok, cum_ok, e_ok = (sem(n) for n in ("rk_ok", "bn_ok", "cum_ok", "e_ok"))
    ehat_ok, arbk_ok = sem("ehat_ok"), sem("arbk_ok")
    st_mm, st_ok = sem("st_mm"), sem("st_ok")
    st_out = [sem("st_out0"), sem("st_out1")]
    s6_in, ys_ok, yrow_in = sem("s6_in"), sem("ys_ok"), sem("yrow_in")
    vt_mm, vt_ok, g_mm, g_ok, l_mm, l_ok = (sem(n) for n in ("vt_mm", "vt_ok", "g_mm", "g_ok", "l_mm", "l_ok"))
    c_ok, m_mm, m_ok, y_mm, x_mm, xy_ok = (sem(n) for n in ("c_ok", "m_mm", "m_ok", "y_mm", "x_mm", "xy_ok"))
    bt_mm, bt_ok, w1_mm, w1_ok, w2_mm, w_ok = (sem(n) for n in ("bt_mm", "bt_ok", "w1_mm", "w1_ok", "w2_mm", "w_ok"))
    u_mm, u_ok, s_mm, s_ok, yo_mm, yo_ok = (sem(n) for n in ("u_mm", "u_ok", "s_mm", "s_ok", "yo_mm", "yo_ok"))
    gn_ok, gn_act, yT_mm, oT_ok = (sem(n) for n in ("gn_ok", "gn_act", "yT_mm", "oT_ok"))
    gns_ok, gnq_ok = sem("gns_ok"), sem("gnq_ok")
    bonT_in = sem("bonT_in")

    tk_mm, tk_ok, lg_mm, gx_ok, sel2_ok = (sem(n) for n in ("tk_mm", "tk_ok", "lg_mm", "gx_ok", "sel2_ok"))
    rt_in, rank_mm, blocks_ok = sem("rt_in"), sem("rank_mm"), sem("blocks_ok")
    pick_ok, xg_mm, xg_ok, gt_mm, gt_ok = (sem(n) for n in ("pick_ok", "xg_mm", "xg_ok", "gt_mm", "gt_ok"))
    y_ok, sc_mm, sc_ok = sem("y_ok"), sem("sc_mm"), sem("sc_ok")
    fin_ok = sem("fin_ok")

    plan = Plan()

    def add_cols(name, w, cols, freed_by, value):
        n = sum(c for _, c in cols)
        pieces, at = [], 0
        for c0, c in cols:
            def dst(s, at=at, c=c, n=n):
                return s[:, 0:KC * n].rearrange("p (k n) -> p k n", k=KC)[:, :, at:at + c]
            pieces.append((dst, w[:, c0:c0 + c].rearrange("(k p) n -> p k n", p=P)))
            at += c
        plan.add(name, pieces, freed_by, value)

    w_in = I["w_in_even"][0]
    IN_JOBS = [("k", [(K0, 128)]), ("ik", [(IK0, 64), (IK0, 64)]), ("iq0", [(IQ0, 128)]), ("iq1", [(IQ0 + 128, 128)])]
    IN_JOBS += [(f"q{j}", [(Q0 + 64 * j, 64), (Q0 + 64 * (j + 4), 64)]) for j in range(4)]
    IN_JOBS += [("v", [(V0, 128)])]
    IN_JOBS += [(f"{n}{j}", [(c0 + 128 * j, 128)]) for n, c0 in (("cc", CC0), ("ch", CH0), ("cb", CB0)) for j in range(4)]
    NIN = len(IN_JOBS)
    N_ATT = 9
    for j, (n, cols) in enumerate(IN_JOBS):
        if j == N_ATT:
            add_cols("iw", w_in, [(IW0, NIH)], iw_mm, 1)
        add_cols(n, w_in, cols, job_mm, j + 1)
    w_out = I["w_out_even"][0]
    for c in range(KC):
        def slot3(s):
            return s[:, :].rearrange("p (k n) -> p k n", k=KC)
        cols = w_out[:, c * P:(c + 1) * P]
        plan.add(f"wo{c}", [
            (lambda s: slot3(s)[0:HD, 0:4, :], cols[0:256].rearrange("(j p) n -> p j n", p=HD)),
            (lambda s: slot3(s)[HD:P, 0:4, :], cols[256:512].rearrange("(j p) n -> p j n", p=HD)),
            (lambda s: slot3(s)[:, 4:8, :], cols[512:1024].rearrange("(j p) n -> p j n", p=P)),
        ], om_mm, c + 1)
    gate0, up0, down0 = I["ffn_gate"][0], I["ffn_up"][0], I["ffn_down"][0]

    def slot4(s):
        return s[:, :].rearrange("p (k n) -> p k n", k=4)

    for q in range(FC // 2):
        for w in (gate0, up0):
            for half in range(2):
                src = w[512 * half:512 * half + 512, 256 * q:256 * q + 256].rearrange("(k p) n -> p k n", p=P)
                plan.add(f"gu{q}", [(slot4, src)], gu_mm, 2 * q + 2)
    for half in range(2):
        for f2 in range(FC // 2):
            src = down0[256 * f2:256 * f2 + 256, 512 * half:512 * half + 512].rearrange("(k p) n -> p k n", p=P)
            plan.add(f"dn{half}_{f2}", [(lambda s: s[:, :].rearrange("p (k n) -> p k n", k=2), src)],
                     down_mm, half * (FC // 2) + f2 + 1)

    for n, w1_, w2_, i in (("w", "rwkv_w1", "rwkv_w2", 0), ("a", "rwkv_a1", "rwkv_a2", 1), ("g", "rwkv_g1", "rwkv_g2", 2)):
        add_cols(n + "1", I[w1_][0], [(0, I[w1_].shape[2])], lh_mm, i + 1)
    for n, w2_, i in (("w", "rwkv_w2", 0), ("a", "rwkv_a2", 1), ("g", "rwkv_g2", 2)):
        plan.add(n + "2", [(lambda s, r=I[w2_].shape[1]: s[0:r, :], I[w2_][0])], job_mm, NIN + KC * (i + 1))
    for i, m in enumerate((1, 0, 2)):
        for c in range(KC):
            add_cols(f"krv{m}{c}", I["rwkv_w_rkv"][0, m], [(c * P, P)], job_mm, NIN + 24 + KC * i + c + 1)
    for c in range(KC):
        add_cols(f"ro{c}", I["rwkv_w_o"][0], [(c * P, P)], om_mm, KC + c + 1)
    landed, _sum = [], [0] * RING
    for n, it in enumerate(plan.items):
        _sum[n % RING] += 16 * len(it[1])
        landed.append(_sum[n % RING])
    PRE = len(plan.items)

    def weights(pe, n):
        pe.wait_ge(slot_in[n % RING], landed[n])
        return ring[n % RING]

    def chained(eng, s):
        count = [0]

        def link(ins):
            count[0] += 1
            ins.then_inc(s, 1)
            eng.wait_ge(s, count[0])
        return link

    mm = nc.tensor.matmul

    def rms_act(act, n, src, square):
        for c in range(KC):
            nc.scalar.activation(square[:, c], src[:, c], ACT.Square).then_inc(sq_ok, 1)
        act.wait_ge(ms_ok, n + 1)
        nc.scalar.activation(rs[:], ms[:], ACT.Sqrt).then_inc(sd_ok, 1)

    def rms_pe(pe, n, square):
        for c in range(KC):
            pe.wait_ge(sq_ok, KC * n + c + 1)
            last = mm(bk[0][:, 0:T], C["ones"], square[:, c], start=c == 0, stop=c == KC - 1)
        last.then_inc(ssq_mm, 1)

    def rms_dve(dve, link, n, src, gain, dst):
        dve.wait_ge(ssq_mm, n + 1)
        nc.vector.tensor_scalar(ms[:], bk[0][:, 0:T], 1.0 / D, EPS, ALU.mult, ALU.add).then_inc(ms_ok, 1)
        dve.wait_ge(sd_ok, n + 1)
        link(nc.vector.reciprocal(rs[:], rs[:]))
        for c in range(KC):
            nc.vector.scalar_tensor_tensor(dst[:, c], src[:, c], vecT[:, gain + c:gain + c + 1], rs[:],
                                           ALU.mult, ALU.mult).then_inc(xn_ok, 1)

    block = ctx.enter_context(nc.Block())

    @block.sync
    def _(sp):
        sp.dma_start(x_rows[:, 0:2, :], I["x_prompt"][0].rearrange("(i p) d -> p i d", p=P)).then_inc(head_in, 16)
        sp.dma_start(x_rows[0:NS, 2, :], I["x_sample"].rearrange("b t d -> (b t) d")).then_inc(head_in, 16)
        sp.dma_start(cst[:], I["consts"]).then_inc(head_in, 16)

        def vec_load(row, src):
            r, n = row % P, src.shape[0]
            sp.dma_start(vec_rows[r:r + n, row // P, :], src).then_inc(head_in, 16)

        for n in VEC_NAMES:
            a = I["rwkv_mu" if n == "mu" else n][0]
            if n == "mu":
                vec_load(VEC[n], a.rearrange("m (c p) -> (m c) p", p=P))
            elif n == "rwkv_r_k":
                vec_load(VEC[n], a.rearrange("(c h) k -> c (h k)", h=2))
            else:
                vec_load(VEC[n], a.rearrange("(c p) -> c p", p=P))
        vec_load(VEC["rwkv_ln_b"], I["rwkv_ln_b"][0].rearrange("(c p) -> c p", p=P))
        vec_load(VEC["conv_w"], I["conv_w"][0].rearrange("j (c p) -> (j c) p", p=P))
        vec_load(VEC["state_shift"], I["state_shift"][0].rearrange("b (c p) -> (b c) p", p=P))
        vec_load(VEC["state_conv"], I["state_conv"][0].rearrange("b j (c p) -> (b j c) p", p=P))
        for n, (name, pieces, freed_by, value) in enumerate(plan.items):
            if n >= RING:
                old = plan.items[n - RING]
                sp.wait_ge(old[2], old[3])
            for view, src in pieces:
                sp.dma_start(view(ring[n % RING]), src).then_inc(slot_in[n % RING], 16)

        sp.wait_ge(om_mm, KC + KC)
        sp.dma_start(w_rt[:], I["moe_router"][0].rearrange("(k p) e -> p k e", p=P)).then_inc(rt_in, 16)
        sp.dma_start(gain_f[:], I["norm_final"].partition_broadcast(P)).then_inc(rt_in, 16)

        def load(s, view, src):
            n = PRE + s
            sp.dma_start(view(ring[n % RING]), src).then_inc(slot_in[n % RING], 16)

        def expert_load(it, e):
            for s in range(3 * FC):
                if s < RING:
                    sp.wait_ge(down_mm, FC * it + s + FC - RING + 1)
                elif s - RING < 2 * FC:
                    sp.wait_ge(gu_mm, FC + FC * it + 2 * ((s - RING) // 4) + 2)
                else:
                    sp.wait_ge(down_mm, FC * it + FC + s - RING - 2 * FC + 1)
                if s < 2 * FC:
                    q, m, half = s // 4, s // 2 % 2, s % 2
                    w = I["moe_gate" if m == 0 else "moe_up"][0, bass.ds(e, 1)].rearrange("o d f -> (o d) f")
                    load(s, slot4, w[512 * half:512 * half + 512, 256 * q:256 * q + 256].rearrange(
                        "(k p) n -> p k n", p=P))
                else:
                    f = s - 2 * FC
                    w = I["moe_down"][0, bass.ds(e, 1)].rearrange("o f d -> (o f) d")
                    load(s, lambda t: t[:, :], w[f * P:(f + 1) * P, :])

        sp.wait_ge(blocks_ok, 1)
        n_blocks = sp.value_load(blocks[0:1, 0:1], min_val=1, max_val=T // CAP)
        with sp.Fori(0, n_blocks) as blk:
            with sp.Fori(0, NE) as e:
                expert_load(blk * NE + e, e)
        sp.wait_ge(fin_ok, 3)
        sp.dma_start(O["y_prompt"][0].rearrange("(i p) d -> p i d", p=P), y_out[:, 0:2, :]).then_inc(out_done, 16)
        sp.dma_start(O["y_sample"].rearrange("b t d -> (b t) d"), y_out[0:NS, 2, :]).then_inc(out_done, 16)
        sp.wait_ge(out_done, 16 * N_OUT)

    @block.tensor
    def _(pe):
        item = [0]

        def project(pe, weights_n, rhs, out):
            w = weights(pe, weights_n)[:, :].rearrange("p (k n) -> p k n", k=KC)
            for k in range(KC):
                last = mm(out, w[:, k], rhs[:, k], start=k == 0, stop=k == KC - 1)
            return last

        pe.wait_ge(head_in, HEAD)
        nc.tensor.transpose(bk[0][:, 0:P], vec_rows[:, 0, :], C["ident"])
        nc.tensor.transpose(bk[0][:, P:P + 84], vec_rows[0:84, 1, :], C["ident"][0:84, 0:84])
        nc.tensor.transpose(bk[0][:, 2 * P:2 * P + 64], vec_rows[0:64, 2, :],
                            C["ident"][0:64, 0:64]).then_inc(vec_mm, 1)
        for c in range(KC):
            if c >= 4:
                pe.wait_ge(xT_ok, c - 3)
            for i, (t0, tn) in enumerate(TILES):
                last = nc.tensor.transpose(bk[1 + c % 4][:, t0:t0 + tn], x_rows[0:tn, i, c * P:(c + 1) * P],
                                           C["ident"][0:tn, 0:tn])
            last.then_inc(xT_mm, 1)
        pe.wait_ge(vec_ok, 1)
        rms_pe(pe, 0, sq)

        pe.wait_ge(xn_ok, KC)

        def in_job(j):
            if j >= 4:
                pe.wait_ge(job_ok, j - 3)
            n = j if j < N_ATT else j + 1
            project(pe, n, xn, bk[1 + j % 4][:, 0:T]).then_inc(job_mm, 1)

        for j in range(N_ATT):
            in_job(j)
        w = weights(pe, N_ATT)[:, 0:KC * NIH].rearrange("p (k n) -> p k n", k=KC)
        for i, (t0, tn) in enumerate(TILES):
            for k in range(KC):
                last = mm(bk[5][0:tn, 8 * i:8 * i + NIH], xn[:, k, t0:t0 + tn], w[:, k],
                          start=k == 0, stop=k == KC - 1)
        last.then_inc(iw_mm, 1)
        for j in range(8):
            pe.wait_ge(job_ok, j + 1)
            if j >= 2:
                pe.wait_ge(rope_ok, j - 1)
            mm(bk[6 + j % 2][:, 0:T], C["rot"], raw[:, j], start=True, stop=True).then_inc(rot_mm, 1)
        pe.wait_ge(job_ok, 9)
        for i, (t0, tn) in enumerate(TILES):
            for m, src in enumerate((rp[:, 0], raw[:, 8], rp[:, 1])):
                pe.wait_ge(rope_ok, 2)
                last = nc.tensor.transpose(bk[i][0:tn, m * P:(m + 1) * P], src[:, t0:t0 + tn], C["ident"])
        last.then_inc(turn_mm, 1)
        for i in range(2):
            pe.wait_ge(rope_ok, 4)
            for h in range(NIH):
                pe.wait_ge(rope_ok, 8)
                pe.wait_ge(turn_ok, 1)
                if i == 1:
                    pe.wait_ge(ip_ok, h + 1)
                a = HD * (h % 2)
                mm(bk[h][:, 0:TP], rp[a:a + HD, 2 + h // 2, i * P:(i + 1) * P], rp[a:a + HD, 1, 0:TP],
                   start=True, stop=True).then_inc(ip_mm, 1)
        pe.wait_ge(ip_ok, 2 * NIH)
        for i in range(2):
            n = P * (i + 1)
            for j in range(4):
                for g in range(2):
                    o = NQ * i + 2 * j + g
                    if o >= 4:
                        pe.wait_ge(sp_ok, o - 3)
                    a = HD * g
                    mm(bk[o % 4][:, 0:n], rp[a:a + HD, 4 + j, i * P:(i + 1) * P], rp[a:a + HD, 0, 0:n],
                       start=True, stop=True).then_inc(sp_mm, 1)
        for b in range(NB):
            pe.wait_ge(page_in, 16 * 3 * NPG * (b + 1))
            pe.wait_ge(sp_ok, 2 * NQ)
            if b >= 1:
                pe.wait_ge(ikT_ok, b)
            for g in range(NPG):
                last = nc.tensor.transpose(bk[g // 4][:, (g % 4) * P:(g % 4 + 1) * P], k_pages[:, g], C["ident"])
            last.then_inc(kT_mm, 1)
            pe.wait_ge(kT_ok, b + 1)
            pe.wait_ge(new_ok, 2 * b + 1)
            pe.wait_ge(qs_ok, 4)
            if b >= 1:
                pe.wait_ge(qk_ok, b)
            else:
                pe.wait_ge(iw_ok, 1)
            a = 32 * (b % 4)
            mm(bk[4][a:a + 32, :], q_s[:, b], keysT[:, 0:512], start=True, stop=True)
            mm(bk[5][a:a + 32, :], q_s[:, b], keysT[:, 512:1024], start=True, stop=True)
            mm(bk[3][a:a + 32, 0:TS], q_s[:, b], keysT[:, 1024:NK], start=True, stop=True).then_inc(qk_mm, 1)
            for g in range(NPG):
                last = nc.tensor.transpose(bk[g // 4][:, (g % 4) * P:(g % 4 + 1) * P],
                                           ik_pages[:, g].rearrange("p a d -> p (a d)"), C["ident"])
            last.then_inc(ikT_mm, 1)
            pe.wait_ge(ikT_ok, b + 1)
            pe.wait_ge(new_ok, 2 * b + 2)
            if b >= 1:
                pe.wait_ge(idx_ok, b)
            mm(bk[6][a:a + 32, :], iq_s[:, b], ikeysT[:, 0:512], start=True, stop=True)
            mm(bk[7][a:a + 32, :], iq_s[:, b], ikeysT[:, 512:1024], start=True, stop=True)
            mm(bk[2][a:a + 32, 0:TS], iq_s[:, b], ikeysT[:, 1024:NK], start=True, stop=True).then_inc(idx_mm, 1)
        pe.wait_ge(idx_ok, NB)
        for cols, o in (((0, 512), 6), ((512, 1024), 7), ((1024, NK), 2)):
            for g in range(2):
                last = mm(bk[o][0:NS, 0:cols[1] - cols[0]], C["sel_sum"][:, g * NS:(g + 1) * NS],
                          idx_s[:, g, cols[0]:cols[1]], start=g == 0, stop=g == 1)
        last.then_inc(isum_mm, 1)
        pe.wait_ge(qk_ok, NB)
        for j in range(N_ATT, len(IN_JOBS)):
            if j == N_ATT:
                pe.wait_ge(sel_ok, 1)
            in_job(j)
        for o in range(2):
            pe.wait_ge(pp_ok, o + 1)
            pe.wait_ge(job_ok, len(IN_JOBS))
            for s in range(o + 1):
                for h in range(NQ):
                    n = 8 * (o + s) + h
                    if n % 4 == 0 and n >= 16:
                        pe.wait_ge(ppT_ok, n // 4 - 3)
                    last = nc.tensor.transpose(bk[(n // 4) % 4][:, (n % 4) * P:(n % 4 + 1) * P],
                                               probs[:, o, h, s * P:(s + 1) * P], C["ident"])
                    if n % 4 == 3:
                        last.then_inc(ppT_mm, 1)
        pe.wait_ge(ppT_ok, 6)
        for o in range(2):
            for j in range(4):
                for g in range(2):
                    for s in range(o + 1):
                        last = mm(bk[4 + j][HD * g:HD * g + HD, o * P:(o + 1) * P], rows[:, s, 1, HD * g:HD * g + HD],
                                  probsT[:, o + s, 2 * j + g], start=s == 0, stop=s == o)
                if o == 1:
                    last.then_inc(pvp_mm, 1)
        pe.wait_ge(conv_ok, 1)
        for c in range(4):
            last = nc.tensor.transpose(bk[0][0:2 + 2 * NB, c * P:(c + 1) * P], u_last[:, c], C["ident"])
        last.then_inc(turn_mm, 1)
        pe.wait_ge(sel_ok, 3)
        for g in range(2):
            banks = (1, 2, 3)
            if g == 1:
                pe.wait_ge(att_ok, 1)
            for o, (c0, c1) in zip(banks, ((0, 512), (512, 1024), (1024, NK))):
                last = mm(bk[o][:, 0:c1 - c0], C["sel_spread"][0:NS, g * P:(g + 1) * P], sc_s[:, c0:c1],
                          start=True, stop=True)
            last.then_inc(spread_mm, 1)
        pe.wait_ge(pvp_ok, 4)
        for g in range(2):
            pe.wait_ge(ps_ok, g + 1)
            if g == 1:
                pe.wait_ge(psT_ok, 1)
            for n in range(9):
                o = 4 + n // 4
                w_ = P if n < 8 else TS
                last = nc.tensor.transpose(bk[o][0:w_, (n % 4) * P:(n % 4 + 1) * P], att_s[:, g, n * P:n * P + w_],
                                           C["ident"])
            last.then_inc(psT_mm, 1)
            pe.wait_ge(psT_ok, g + 1)
            pe.wait_ge(vnew_in, 16)
            for b in range(4 * g, 4 * g + 4):
                pe.wait_ge(vpage_in[b % 2], 16 * NPG * (b // 2 + 1))
                for n in range(9):
                    k = P if n < 8 else TS
                    lhs = v_pages[:, b % 2, n] if n < 8 else v_new[:, b]
                    last = mm(bk[7][:, 32 * b:32 * b + 32], lhs, pS_T[0:k, n, 32 * (b % 4):32 * (b % 4) + 32],
                              start=n == 0, stop=n == 8)
                last.then_inc(pvs_mm, 1)
        pe.wait_ge(pvs_ok, 1)
        pe.wait_ge(conv_ok, 2)
        pe.wait_ge(turn_ok, 2)
        n0 = len(IN_JOBS) + 1
        for c in range(KC):
            if c >= 4:
                pe.wait_ge(om_ok, c - 3)
            project(pe, n0 + c, mixT, bk[1 + c % 4][:, 0:T]).then_inc(om_mm, 1)
        rms_pe(pe, 1, sq1)
        pe.wait_ge(xn_ok, 2 * KC)
        n0 += KC
        for q in range(FC // 2):
            slots = [weights(pe, n0 + 4 * q + i)[:, :].rearrange("p (k n) -> p k n", k=4) for i in range(4)]
            for f in (2 * q, 2 * q + 1):
                if f >= 2:
                    pe.wait_ge(hid_ok, f - 1)
                for m in range(2):
                    for k in range(KC):
                        last = mm(bk[2 * m + f % 2][:, 0:T], slots[2 * m + k // 4][:, k % 4, (f % 2) * P:(f % 2 + 1) * P],
                                  xn1[:, k], start=k == 0, stop=k == KC - 1)
                last.then_inc(gu_mm, 1)
        n0 += 2 * FC
        for half in range(2):
            banks = (4, 5, 6, 7) if half == 0 else (0, 1, 2, 3)
            for f in range(FC):
                if f % 2 == 0:
                    w = weights(pe, n0 + half * (FC // 2) + f // 2)[:, :].rearrange("p (k n) -> p k n", k=2)
                pe.wait_ge(hid_ok, FC if half else f + 1)
                for c in range(4):
                    last = mm(bk[banks[c]][:, 0:T], w[:, f % 2, c * P:(c + 1) * P], hid[:, f],
                              start=f == 0, stop=f == FC - 1)
                if f % 2 == 1:
                    last.then_inc(down_mm, 1)
        n0 += FC

        pe.wait_ge(down_ok, 8)
        rms_pe(pe, 2, sq2)
        h_in = [(0, HD), (1, HD), (2, P)]
        for i, r in h_in:
            pe.wait_ge(mix_ok, KC * (i + 1))
            w = weights(pe, n0 + i)[:, 0:KC * r].rearrange("p (k n) -> p k n", k=KC)
            for k in range(KC):
                last = mm(bk[5 + i][0:r, 0:T], w[:, k], mx[:, i % 2, k], start=k == 0, stop=k == KC - 1)
            last.then_inc(lh_mm, 1)
        n0 += 3
        for j in range(48):
            i, c = j // KC, j % KC
            if j >= 4:
                pe.wait_ge(job_ok, NIN + j - 3)
            out = bk[1 + j % 4][:, 0:T]
            if i < 3:
                pe.wait_ge(lh_ok, i + 1)
                r = h_in[i][1]
                w = weights(pe, n0 + i)
                mm(out, w[0:r, c * P:(c + 1) * P], lh[0:r, i], start=True, stop=True).then_inc(job_mm, 1)
            else:
                pe.wait_ge(mix_ok, KC * (i + 1))
                project(pe, n0 + 3 + j - 24, mx[:, i % 2], out).then_inc(job_mm, 1)
        n0 += 3 + 24
        pe.wait_ge(el_ok, 2)
        for c in range(KC):
            last = nc.tensor.transpose(bk[5 + c // 4][0:1 + NB, (c % 4) * P:(c % 4 + 1) * P], e_last[:, c], C["ident"])
        last.then_inc(turn_mm, 1)
        pe.wait_ge(job_ok, NIN + 48)
        pe.wait_ge(turn_ok, 3)
        pe.wait_ge(sqk_ok, 1)
        for c in range(KC):
            last = mm(bk[c][:, 0:T], C["headones"], t2[:, c], start=True, stop=True)
        last.then_inc(hs_mm, 1)
        pe.wait_ge(nk_ok, 1)
        pe.wait_ge(rk_ok, 1)
        for c in range(KC):
            last = mm(bk[c][:, 0:T], C["headones"], t2[:, c], start=True, stop=True)
        last.then_inc(hs_mm, 1)
        pe.wait_ge(bn_ok, 1)
        pe.wait_ge(e_ok, 3)
        pe.wait_ge(arbk_ok, 1)
        for q, src in enumerate((rT, lwT, kT, vT, t1, aT)):
            if q >= 4:
                pe.wait_ge(st_ok, q - 3)
            for c in range(KC):
                last = nc.tensor.transpose(bk[2 * (q % 4) + c // 4][0:NS, (c % 4) * P:(c % 4 + 1) * P],
                                           src[:, c, TP:T], C["ident"])
            last.then_inc(st_mm, 1)
        pe.wait_ge(st_ok, 6)
        for p2 in range(2):
            if p2:
                pe.wait_ge(yo_ok, 2)
                pe.wait_ge(s_ok, 2)
            for c in range(KC):
                last = nc.tensor.transpose(bk[c // 4][:, (c % 4) * P:(c % 4 + 1) * P], vT[:, c, P * p2:P * (p2 + 1)],
                                           C["ident"])
            last.then_inc(vt_mm, 1)
            for gi in range(8):
                cc, par, half = gi // 4, gi // 2 % 2, gi % 2
                if gi < 2:
                    pe.wait_ge(vt_ok, p2 + 1)
                r = slice(HD * par, HD * par + HD)
                for i in range(4):
                    hp = 4 * half + i
                    last = mm(bk[gi][:, i * P:(i + 1) * P],
                              BK[r, hp, 2 * p2 + cc].rearrange("p a t -> p (a t)"),
                              AR[r, hp, 2 * p2 + cc].rearrange("p a t -> p (a t)"), start=True, stop=True)
                last.then_inc(g_mm, 1)
            pe.wait_ge(g_ok, 8 * (p2 + 1))
            for cc in range(2):
                for par in range(2):
                    r = slice(HD * par, HD * par + HD)
                    for hp in range(KC):
                        last = mm(bk[4 + 2 * cc + par][CH * cc:CH * cc + CH, hp * CH:(hp + 1) * CH],
                                  AR[r, hp, 2 * p2 + cc, 0], BK[r, hp, 2 * p2 + cc, 0], start=True, stop=True)
            last.then_inc(l_mm, 1)
            def each(fn, first):
                for cc in range(2):
                    r = slice(CH * cc, CH * cc + CH)
                    for par in range(2):
                        for hp in range(KC):
                            lhs, rhs = fn(r, par, hp)
                            last = mm(bk[first + 2 * cc + par][r, hp * CH:(hp + 1) * CH], lhs, rhs, start=True, stop=True)
                return last

            for j in range(6):
                pe.wait_ge(c_ok, 6 * p2 + j + 1)
                if j:
                    pe.wait_ge(xy_ok, 6 * p2 + j)
                    each(lambda r, par, hp: (Cj[r, par, hp], Y[r, par, hp]), 0).then_inc(m_mm, 1)
                    pe.wait_ge(m_ok, 5 * p2 + j)
                    each(lambda r, par, hp: (X[r, par, hp], M[r, par, hp]), 4).then_inc(y_mm, 1)
                    if j < 5:
                        each(lambda r, par, hp: (M[r, par, hp], X[r, par, hp]), 0).then_inc(x_mm, 1)
                else:
                    each(lambda r, par, hp: (Cj[r, par, hp], C["ident64"][r]), 0).then_inc(m_mm, 1)
            pe.wait_ge(m_ok, 5 * (p2 + 1))
            for cc in range(2):
                for hp in range(KC):
                    last = nc.tensor.transpose(bk[2 * cc + hp // 4][:, (hp % 4) * P:(hp % 4 + 1) * P],
                                               BK[:, hp, 2 * p2 + cc].rearrange("p a t -> p (a t)"), C["ident"])
            last.then_inc(bt_mm, 1)
            pe.wait_ge(xy_ok, 6 * (p2 + 1))
            for cc in range(2):
                r = slice(CH * cc, CH * cc + CH)
                for par in range(2):
                    for hp in range(KC):
                        last = mm(bk[4 + 2 * cc + par][r, hp * CH:(hp + 1) * CH], G[CH:P, cc, par, hp, 0:CH],
                                  Z[CH:P, cc, hp, par], start=True, stop=True)
            last.then_inc(w1_mm, 1)
            pe.wait_ge(bt_ok, p2 + 1)
            pe.wait_ge(w1_ok, p2 + 1)
            for cc in range(2):
                c = 2 * p2 + cc
                r = slice(CH * cc, CH * cc + CH)
                if c:
                    pe.wait_ge(s_ok, c)
                    pe.wait_ge(yo_ok, c)
                    for par in range(2):
                        for hp in range(KC):
                            q = slice(HD * par, HD * par + HD)
                            last = mm(bk[par][r, hp * CH:(hp + 1) * CH], AR[q, hp, c, 0], ST[q, hp],
                                      start=True, stop=True)
                    last.then_inc(w2_mm, 1)
                    pe.wait_ge(w_ok, c)
                for par in range(2):
                    for hp in range(KC):
                        last = mm(bk[2 + par][0:CH, hp * CH:(hp + 1) * CH], Y[r, par, hp], X[r, par, hp],
                                  start=True, stop=True)
                last.then_inc(u_mm, 1)
                pe.wait_ge(u_ok, c + 1)
                for hp in range(KC):
                    for par in range(2):
                        last = mm(bk[6][HD * par:HD * par + HD, hp * CH:(hp + 1) * CH],
                                  BKt[:, cc, hp, HD * par:HD * par + HD], Z[:, cc, hp, par], start=True, stop=True)
                last.then_inc(s_mm, 1)
                for par in range(2):
                    for hp in range(KC):
                        q = slice(HD * par, HD * par + HD)
                        out = bk[4 + par][r, hp * CH:(hp + 1) * CH]
                        last = mm(out, G[:, cc, par, hp, CH:P], Z[:, cc, hp, par], start=True, stop=c == 0)
                        if c:
                            last = mm(out, AR[q, hp, c, 1], ST[q, hp], start=False, stop=True)
                last.then_inc(yo_mm, 1)
        pe.wait_ge(s_ok, NCH)
        for hp in range(KC):
            last = nc.tensor.transpose(bk[hp // 4][0:HD, (hp % 4) * P:(hp % 4 + 1) * P], ST[:, hp], C["ident"])
        last.then_inc(turn_mm, 1)
        pe.wait_ge(gn_ok, 3)
        pe.wait_ge(turn_ok, 4)
        for c in range(KC):
            if c >= 4:
                pe.wait_ge(oT_ok, c - 3)
            for i, (t0, tn) in enumerate(TILES):
                last = nc.tensor.transpose(bk[2 + c % 4][:, t0:t0 + tn], y_rows[0:tn, i, c * P:(c + 1) * P],
                                           C["ident"][0:tn, 0:tn])
            last.then_inc(yT_mm, 1)
        pe.wait_ge(oT_ok, KC)
        for c in range(KC):
            if c >= 4:
                pe.wait_ge(om_ok, KC + c - 3)
            project(pe, n0 + c, oT, bk[2 + c % 4][:, 0:T]).then_inc(om_mm, 1)
        n0 += KC

        pe.wait_ge(om_ok, KC + KC)
        rms_pe(pe, 3, sq3)
        pe.wait_ge(xn_ok, 4 * KC)
        pe.wait_ge(rt_in, 32)
        for i, (t0, tn) in enumerate(TILES):
            for k in range(KC):
                last = mm(bk[1][0:tn, NE * i:NE * i + NE], xn3[:, k, t0:t0 + tn], w_rt[:, k], start=k == 0, stop=k == KC - 1)
        last.then_inc(lg_mm, 1)
        for m in range(12):
            src, i, half = (xn3, xT)[m // 6], m // 2 % 3, m % 2
            t0, tn = TILES[i]
            if m >= 4:
                pe.wait_ge(tk_ok, m - 3)
            for c in range(4):
                last = nc.tensor.transpose(bk[4 + m % 4][0:tn, c * P:(c + 1) * P], src[:, 4 * half + c, t0:t0 + tn],
                                           C["ident"])
            last.then_inc(tk_mm, 1)
        pe.wait_ge(sel2_ok, 1)
        for i, (t0, tn) in enumerate(TILES):
            for j in range(i + 1):
                jn = TILES[j][1]
                last = mm(bk[2][0:tn, NE * i:NE * i + NE], C["before" if j == i else "ones"][0:jn, 0:tn], sel[0:jn, j],
                          start=j == 0, stop=j == i)
        for j in range(3):
            jn = TILES[j][1]
            last = mm(bk[2][0:1, 4 * NE:5 * NE], C["ones"][0:jn, 0:1], sel[0:jn, j], start=j == 0, stop=j == 2)
        last.then_inc(rank_mm, 1)

        def gather():
            for c in range(KC):
                for i, (t0, tn) in enumerate(TILES):
                    last = mm(bk[6 + c // 4][:, (c % 4) * CAP:(c % 4 + 1) * CAP], xr[0:tn, i, c * P:(c + 1) * P],
                              pick[0:tn, i], start=i == 0, stop=i == 2)
            last.then_inc(xg_mm, 1)

        pe.wait_ge(tk_ok, 12)
        pe.wait_ge(pick_ok, 1)
        gather()

        def slot(it, s):
            n = PRE + s
            pe.wait_ge(slot_in[n % RING], it * (16 * 3 * FC // RING) + _sum[n % RING] + 16 * (s // RING + 1))
            return ring[n % RING]

        def expert(it):
            pe.wait_ge(xg_ok, it + 1)
            pe.wait_ge(hid_ok, FC + FC * it)
            pe.wait_ge(sc_ok, 6 * it + 1)
            for q in range(FC // 2):
                w = [slot(it, 4 * q + i)[:, :].rearrange("p (k n) -> p k n", k=4) for i in range(4)]
                for f in (2 * q, 2 * q + 1):
                    if f >= 2:
                        pe.wait_ge(hid_ok, FC + FC * it + f - 1)
                    for m in range(2):
                        for k in range(KC):
                            last = mm(bk[f % 2][:, m * CAP:(m + 1) * CAP], w[2 * m + k // 4][:, k % 4, (f % 2) * P:(f % 2 + 1) * P],
                                      xg[:, k], start=k == 0, stop=k == KC - 1)
                    last.then_inc(gu_mm, 1)
            pe.wait_ge(pick_ok, it + 2)
            gather()
            for i, (t0, tn) in enumerate(TILES):
                last = nc.tensor.transpose(bk[5][0:CAP, t0:t0 + tn], give[0:tn, i], C["ident"][0:tn, 0:tn])
            last.then_inc(gt_mm, 1)
            pe.wait_ge(hid_ok, FC + FC * it + FC)
            for f in range(FC):
                w = slot(it, 2 * FC + f)
                for half in range(2):
                    last = mm(bk[2 + half][0:CAP, :], hid2[:, f], w[:, 512 * half:512 * half + 512],
                              start=f == 0, stop=f == FC - 1)
                last.then_inc(down_mm, 1)
            pe.wait_ge(gt_ok, it + 1)
            pe.wait_ge(y_ok, it + 1)
            for g in range(6):
                i, half = g // 2, g % 2
                t0, tn = TILES[i]
                if g >= 4:
                    pe.wait_ge(sc_ok, 6 * it + 1 + g - 3)
                mm(bk[(4, 5, 0, 1)[g % 4]][0:tn, :], giveT[:, t0:t0 + tn], ye[:, 512 * half:512 * half + 512],
                   start=True, stop=True).then_inc(sc_mm, 1)

        pe.wait_ge(blocks_ok, 1)
        n_blocks = pe.value_load(blocks[0:1, 0:1], min_val=1, max_val=T // CAP)
        with pe.Fori(0, n_blocks) as blk:
            with pe.Fori(0, NE) as e:
                expert(blk * NE + e)

    @block.scalar
    def _(act):
        link = chained(act, act_chain)
        for c in range(KC):
            act.wait_ge(xT_mm, c + 1)
            nc.scalar.copy(xT[:, c], bk[1 + c % 4][:, 0:T]).then_inc(xT_ok, 1)
        act.wait_ge(xT_ok, KC)
        rms_act(act, 0, xT, sq)
        for j in range(N_ATT):
            act.wait_ge(job_mm, j + 1)
            nc.scalar.copy(raw[:, j], bk[1 + j % 4][:, 0:T]).then_inc(job_ok, 1)
        act.wait_ge(iw_mm, 1)
        for i, (t0, tn) in enumerate(TILES):
            last = nc.scalar.mul(iw[0:tn, i, :], bk[5][0:tn, 8 * i:8 * i + NIH], 1.0 / 16)
        last.then_inc(iw_ok, 1)
        act.wait_ge(turn_mm, 1)
        for i, (t0, tn) in enumerate(TILES):
            last = nc.scalar.copy(rows[0:tn, i].rearrange("p m d -> p (m d)"), bk[i][0:tn, 0:3 * P])
        last.then_inc(turn_ok, 1)
        act.wait_ge(iw_ok, 1)
        act.dma_start(iw_dram[:], iw[0:NS, 2, :]).then_inc(iw_out, 16)
        act.wait_ge(turn_ok, 1)
        for name, m, w_ in (("k", 0, P), ("v", 1, P), ("idx_k", 2, HD)):
            flat_p = O[name + "_prompt"][0, 0].rearrange("(i p) g d -> p i (g d)", p=P) if m < 2 \
                else O[name + "_prompt"][0, 0].rearrange("(i p) d -> p i d", p=P)
            flat_s = O[name + "_sample"][0].rearrange("b t g d -> (b t) (g d)") if m < 2 \
                else O[name + "_sample"][0].rearrange("b t d -> (b t) d")
            act.dma_start(flat_p, rows[:, 0:2, m, 0:w_]).then_inc(out_done, 16)
            if m == 1:
                act.dma_start(flat_s, rows[0:NS, 2, m, 0:w_]).then_inc(temp_out, 16)
            else:
                act.dma_start(flat_s, rows[0:NS, 2, m, 0:w_]).then_inc(out_done, 16)
        act.wait_ge(iw_out, 16)
        for b in range(NB):
            act.dma_start(iw_s[32 * (b % 4):32 * (b % 4) + 16, b // 4:b // 4 + 1],
                          iw_dram[TS * b:TS * b + TS, :].rearrange("t (h o) -> (t h) o", o=1)).then_inc(iws_in, 16)
        act.wait_ge(temp_out, 16)
        act.dma_start(v_new[:], O["v_sample"][0].rearrange("b t g d -> t b (g d)")).then_inc(vnew_in, 16)
        for i in range(2):
            n = P * (i + 1)
            act.wait_ge(shift_ok, i + 1)
            nc.scalar.activation(probs[:, i, :, 0:n], probs[:, i, :, 0:n], ACT.Exp).then_inc(expp_ok, 1)
        for b in range(NB):
            a, g = 32 * (b % 4), b // 4
            act.wait_ge(kT_mm, b + 1)
            if b >= 1:
                act.wait_ge(qk_mm, b)
            nc.scalar.copy(keysT[:, 0:512], bk[0][:])
            nc.scalar.copy(keysT[:, 512:1024], bk[1][:]).then_inc(kT_ok, 1)
            act.wait_ge(qk_mm, b + 1)
            nc.scalar.copy(att_s[a:a + 32, g, 0:512], bk[4][a:a + 32, :])
            nc.scalar.copy(att_s[a:a + 32, g, 512:1024], bk[5][a:a + 32, :])
            nc.scalar.copy(att_s[a:a + 32, g, 1024:NK], bk[3][a:a + 32, 0:TS]).then_inc(qk_ok, 1)
        for j in range(N_ATT, len(IN_JOBS)):
            act.wait_ge(job_mm, j + 1)
            m = j - N_ATT
            nc.scalar.copy(ccb[:, m // 4, m % 4], bk[1 + j % 4][:, 0:T]).then_inc(job_ok, 1)
        for n in range(6):
            act.wait_ge(ppT_mm, n + 1)
            nc.scalar.copy(probsT[:, n // 2, 4 * (n % 2):4 * (n % 2) + 4].rearrange("p h t -> p (h t)"),
                           bk[n % 4][:]).then_inc(ppT_ok, 1)
        for j in range(4):
            act.wait_ge(pvp_mm, j + 1)
            nc.scalar.copy(mixT[:, j, 0:TP], bk[4 + j][:, 0:TP]).then_inc(pvp_ok, 1)
        act.wait_ge(turn_mm, 2)
        nc.scalar.copy(conv_rows[:], bk[0][0:2 + 2 * NB, :]).then_inc(turn_ok, 1)
        act.wait_ge(turn_ok, 2)
        act.dma_start(O["conv_prompt"][0, 0], conv_rows[0:2, :]).then_inc(out_done, 16)
        act.dma_start(O["conv_sample"][0].rearrange("b j c -> (b j) c"), conv_rows[2:2 + 2 * NB, :]).then_inc(out_done, 16)
        for g in range(2):
            act.wait_ge(att_ok, 2 * (g + 1))
            nc.scalar.activation(att_s[:, g], att_s[:, g], ACT.Exp, bias=mxs[:, g:g + 1],
                                 accum_out=sms[:, g:g + 1]).then_inc(exps_ok, 1)
        for g in range(2):
            act.wait_ge(psT_mm, g + 1)
            if g == 1:
                act.wait_ge(pvs_mm, 4)
            nc.scalar.copy(pS_T[:, 0:4].rearrange("p n t -> p (n t)"), bk[4][:])
            nc.scalar.copy(pS_T[:, 4:8].rearrange("p n t -> p (n t)"), bk[5][:])
            nc.scalar.copy(pS_T[0:TS, 8], bk[6][0:TS, 0:P]).then_inc(psT_ok, 1)
        act.wait_ge(om_ok, KC)
        act.wait_ge(out_done, 16 * OUT_0)
        rms_act(act, 1, xT, sq1)
        for f in range(FC):
            act.wait_ge(gu_mm, f + 1)
            if f >= 2:
                act.wait_ge(hid_ok, f - 1)
            nc.scalar.activation(sg[:, f % 2], bk[f % 2][:, 0:T], ACT.Silu).then_inc(silu_ok, 1)

        act.wait_ge(down_ok, 8)
        rms_act(act, 2, xT, sq2)
        for i, (r, f) in enumerate(((HD, ACT.Tanh), (HD, ACT.Copy), (P, ACT.Sigmoid))):
            act.wait_ge(lh_mm, i + 1)
            nc.scalar.activation(lh[0:r, i], bk[5 + i][0:r, 0:T], f).then_inc(lh_ok, 1)
        for j in range(48):
            i, c = j // KC, j % KC
            act.wait_ge(job_mm, NIN + j + 1)
            src = bk[1 + j % 4][:, 0:T]
            if i < 2:
                v_ = VEC["rwkv_w0" if i == 0 else "rwkv_a0"] + c
                nc.scalar.activation((lwT, aT)[i][:, c], src, ACT.Sigmoid, bias=vecT[:, v_:v_ + 1]).then_inc(job_ok, 1)
            else:
                nc.scalar.copy((gT, kT, rT, vT)[i - 2][:, c], src).then_inc(job_ok, 1)
        act.wait_ge(turn_mm, 3)
        nc.scalar.copy(shift_rows[:, 0:512], bk[5][0:1 + NB, :])
        nc.scalar.copy(shift_rows[:, 512:1024], bk[6][0:1 + NB, :]).then_inc(turn_ok, 1)
        act.wait_ge(turn_ok, 3)
        act.dma_start(O["shift_prompt"][0], shift_rows[0:1, :]).then_inc(out_done, 16)
        act.dma_start(O["shift_sample"][0], shift_rows[1:1 + NB, :]).then_inc(out_done, 16)
        act.wait_ge(out_done, 16 * OUT_1)
        act.wait_ge(t1_ok, 1)
        nc.scalar.activation(t2[:], t1[:], ACT.Square).then_inc(sqk_ok, 1)
        act.wait_ge(nk_ok, 1)
        nc.scalar.activation(t2[:], t2[:], ACT.Sqrt).then_inc(nsq_ok, 1)
        pr = slice(0, TP)
        act.wait_ge(cum_ok, 1)
        nc.scalar.activation(t4[:, :, pr], t3[:, :, pr], ACT.Exp).then_inc(e_ok, 1)
        act.wait_ge(cum_ok, 2)
        nc.scalar.activation(t2[:, :, pr], t2[:, :, pr], ACT.Exp).then_inc(e_ok, 1)
        nc.scalar.activation(lwT[:, :, TP:T], lwT[:, :, TP:T], ACT.Exp).then_inc(e_ok, 1)
        act.wait_ge(ehat_ok, 1)
        nc.scalar.activation(t4[:, :, pr], t3[:, :, pr], ACT.Exp, scale=-1.0).then_inc(e_ok, 1)
        act.wait_ge(bn_ok, 1)
        act.dma_start(bon_dram[:, 0:7], bon[:]).then_inc(temp_out, 16)
        act.dma_start(bon_dram[:, 7], ms[:]).then_inc(temp_out, 16)
        act.wait_ge(temp_out, 48)
        for q in range(6):
            act.wait_ge(st_mm, q + 1)
            if q >= 2:
                act.wait_ge(st_out[q % 2], 16 * (q // 2))
            for i in range(2):
                last = nc.scalar.copy(st[:, q % 2, 512 * i:512 * i + 512], bk[2 * (q % 4) + i][0:NS, :])
            last.then_inc(st_ok, 1)
            act.wait_ge(st_ok, q + 1)
            act.dma_start(q6_dram[:, q], st[:, q % 2]).then_inc(st_out[q % 2], 16)
        for i in range(2):
            act.wait_ge(st_out[i], 48)
        for b in range(NB):
            act.dma_start(s6[RH * b:RH * b + RH].rearrange("p t q d -> p (t q) d"), q6_dram[TS * b:TS * b + TS].rearrange(
                "t q (h d) -> h (t q) d", h=RH)).then_inc(s6_in, 16)
        act.dma_start(S[:].rearrange("p v k -> p (v k)"),
                      I["state_wkv"][0].rearrange("b h v k -> (b h) (v k)")).then_inc(s6_in, 16)
        for p2 in range(2):
            act.wait_ge(vt_mm, p2 + 1)
            for cc in range(2):
                for i in range(2):
                    last = nc.scalar.copy(Z[CH:P, cc, 4 * i:4 * i + 4].rearrange("p h a v -> p (h a v)"),
                                          bk[i][CH * cc:CH * cc + CH, :])
            last.then_inc(vt_ok, 1)
            act.wait_ge(l_mm, p2 + 1)
            for cc in range(2):
                r = slice(CH * cc, CH * cc + CH)
                for par in range(2):
                    last = nc.scalar.copy(L[r, par].rearrange("p h s -> p (h s)"), bk[4 + 2 * cc + par][r, :])
            last.then_inc(l_ok, 1)
            for j in range(1, 6):
                act.wait_ge(m_mm, 6 * p2 + j + 1)
                for cc in range(2):
                    r = slice(CH * cc, CH * cc + CH)
                    for par in range(2):
                        last = nc.scalar.copy(M[r, par].rearrange("p h s -> p (h s)"), bk[2 * cc + par][r, :])
                last.then_inc(m_ok, 1)
            act.wait_ge(bt_mm, p2 + 1)
            for cc in range(2):
                for i in range(2):
                    last = nc.scalar.copy(BKt[:, cc, 4 * i:4 * i + 4].rearrange("p h d -> p (h d)"), bk[2 * cc + i][:])
            last.then_inc(bt_ok, 1)
            act.wait_ge(w1_mm, p2 + 1)
            for cc in range(2):
                r = slice(CH * cc, CH * cc + CH)
                for par in range(2):
                    last = nc.scalar.copy(X[r, par].rearrange("p h s -> p (h s)"), bk[4 + 2 * cc + par][r, :])
            last.then_inc(w1_ok, 1)
            for cc in range(2):
                c = 2 * p2 + cc
                act.wait_ge(u_mm, c + 1)
                for par in range(2):
                    last = nc.scalar.copy(Z[0:CH, cc, :, par], bk[2 + par][0:CH, :].rearrange("p (h v) -> p h v", h=KC))
                last.then_inc(u_ok, 1)
                act.wait_ge(yo_mm, c + 1)
                r = slice(CH * cc, CH * cc + CH)
                for par in range(2):
                    last = nc.scalar.copy(y_rows[r, p2].rearrange("p (h a v) -> p h a v", h=KC, a=2)[:, :, par],
                                          bk[4 + par][r, :].rearrange("p (h v) -> p h v", h=KC))
                last.then_inc(yo_ok, 1)
        act.wait_ge(turn_mm, 4)
        for i in range(2):
            last = nc.scalar.copy(st_rows[:, 8 * i:8 * i + 8].rearrange("p h k -> p (h k)"), bk[i][0:HD, :])
        last.then_inc(turn_ok, 1)
        act.wait_ge(turn_ok, 4)
        act.dma_start(O["wkv_prompt"][0, 0].rearrange("h v k -> v h k"), st_rows[:]).then_inc(out_done, 16)
        act.dma_start(bonT[:], bon_dram).then_inc(bonT_in, 16)
        act.wait_ge(ys_ok, TS)
        act.dma_start(O["wkv_sample"][0].rearrange("b h v k -> (b h) (v k)"),
                      S[:].rearrange("p v k -> p (v k)")).then_inc(out_done, 16)
        for b in range(NB):
            act.dma_start(ys_dram[b].rearrange("t h v -> h t v"), ys[RH * b:RH * b + RH]).then_inc(temp_out, 16)
        act.wait_ge(temp_out, 48 + 16 * NB)
        act.dma_start(y_rows[0:NS, 2], ys_dram.rearrange("b t h v -> (b t) (h v)")).then_inc(yrow_in, 16)
        for i, (t0, tn) in enumerate(TILES):
            act.wait_ge(gn_act, 2 * i + 1)
            nc.scalar.activation(gsq[0:tn], y_rows[0:tn, i], ACT.Square).then_inc(gn_act, 1)
            act.wait_ge(gns_ok, i + 1)
            nc.scalar.activation(gst2[0:tn], gst2[0:tn], ACT.Sqrt).then_inc(gnq_ok, 1)

        act.wait_ge(om_ok, KC + KC)
        act.wait_ge(out_done, 16 * (OUT_1 + 2))
        rms_act(act, 3, xT, sq3)
        for m in range(12):
            dst, i, half = (xr, acc)[m // 6], m // 2 % 3, m % 2
            tn = TILES[i][1]
            act.wait_ge(tk_mm, m + 1)
            nc.scalar.copy(dst[0:tn, i, 512 * half:512 * half + 512], bk[4 + m % 4][0:tn, :]).then_inc(tk_ok, 1)
        act.wait_ge(gx_ok, 1)
        for i, (t0, tn) in enumerate(TILES):
            last = nc.scalar.activation(gates[0:tn, i, 1:2], gates[0:tn, i, 1:2], ACT.Exp)
        last.then_inc(gx_ok, 1)

        def rows_in():
            for i in range(2):
                last = nc.scalar.copy(xg[:, 4 * i:4 * i + 4].rearrange("p k c -> p (k c)"), bk[6 + i][:, 0:4 * CAP])
            last.then_inc(xg_ok, 1)

        act.wait_ge(xg_mm, 1)
        rows_in()

        def expert(it):
            act.wait_ge(hid_ok, FC + FC * it)
            for f in range(FC):
                act.wait_ge(gu_mm, FC + FC * it + f + 1)
                if f >= 2:
                    act.wait_ge(hid_ok, FC + FC * it + f - 1)
                nc.scalar.activation(sg2[:, f % 2], bk[f % 2][:, 0:CAP], ACT.Silu).then_inc(silu_ok, 1)
            act.wait_ge(xg_mm, it + 2)
            rows_in()
            act.wait_ge(down_mm, FC * it + 2 * FC)
            act.wait_ge(sc_ok, 6 * it + 1)
            for half in range(2):
                last = nc.scalar.copy(ye[:, 512 * half:512 * half + 512], bk[2 + half][0:CAP, :])
            last.then_inc(y_ok, 1)

        act.wait_ge(blocks_ok, 1)
        n_blocks = act.value_load(blocks[0:1, 0:1], min_val=1, max_val=T // CAP)
        with act.Fori(0, n_blocks) as blk:
            with act.Fori(0, NE) as e:
                expert(blk * NE + e)
        act.wait_ge(sc_ok, n_blocks * (6 * NE) + 1)
        for i, (t0, tn) in enumerate(TILES):
            last = nc.scalar.activation(y_out[0:tn, i], acc[0:tn, i], ACT.Square, accum_out=ssf[0:tn, i:i + 1])
        last.then_inc(sq_ok, 1)
        act.wait_ge(ms_ok, 5)
        nc.scalar.activation(ssf[:], ssf[:], ACT.Sqrt).then_inc(sd_ok, 1)

    @block.vector
    def _(dve):
        link = chained(dve, dve_chain)
        V = nc.vector
        dve.wait_ge(vec_mm, 1)
        V.tensor_copy(vecT[:, 0:P + 84], bk[0][:, 0:P + 84])
        V.tensor_copy(vecT[:, 2 * P:2 * P + 64], bk[0][:, 2 * P:2 * P + 64]).then_inc(vec_ok, 1)
        dve.wait_ge(vec_ok, 1)
        rms_dve(dve, link, 0, xT, VEC["norm_mix_even"], xn)
        for j in range(8):
            dve.wait_ge(rot_mm, j + 1)
            link(V.tensor_tensor(ms[:], bk[6 + j % 2][:, 0:T], C["sin"], ALU.mult))
            dve.wait_ge(rope_pool, j + 1)
            V.tensor_tensor(rp[:, j], rp[:, j], ms[:], ALU.add).then_inc(rope_ok, 1)
            dve.wait_ge(rope_ok, j + 1)
        dve.wait_ge(iw_ok, 1)
        for i in range(2):
            for h in range(NIH):
                dve.wait_ge(ip_mm, NIH * i + h + 1)
                dst = sc_p[:, i] if h == 0 else tmp_p[:, h]
                ins = V.tensor_scalar(dst, bk[h][:, 0:TP], 0.0, iw[:, i, h:h + 1], ALU.max, ALU.mult)
                ins.then_inc(ip_ok, 1)
                dve.wait_ge(ip_ok, NIH * i + h + 1)
                if h:
                    link(V.tensor_tensor(sc_p[:, i], sc_p[:, i], tmp_p[:, h], ALU.add))
            link(V.tensor_tensor(sc_p[:, i], sc_p[:, i], C["causal"][:, i * TP:(i + 1) * TP], ALU.add))
            for r in range(SEL_P // 8):
                link(V.max(top8[:], sc_p[:, i]))
                link(V.match_replace(sc_p[:, i], top8[:], sc_p[:, i], TAKEN))
            link(V.tensor_scalar(sc_p[:, i], sc_p[:, i], -2.0e38, NEG, ALU.is_gt, ALU.mult))
            link(V.tensor_tensor(sc_p[:, i], sc_p[:, i], C["causal"][:, i * TP:(i + 1) * TP], ALU.add))
        for i in range(2):
            n = P * (i + 1)
            for h in range(NQ):
                dve.wait_ge(sp_mm, NQ * i + h + 1)
                V.scalar_tensor_tensor(probs[:, i, h, 0:n], bk[(NQ * i + h) % 4][:, 0:n], HD ** -0.5,
                                       sc_p[:, i, 0:n], ALU.mult, ALU.add).then_inc(sp_ok, 1)
            dve.wait_ge(sp_ok, NQ * (i + 1))
            link(V.tensor_reduce(mxp[:, i], probs[:, i, :, 0:n], AX.X, ALU.max))
            V.tensor_tensor(probs[:, i, :, 0:n], probs[:, i, :, 0:n],
                            mxp[:, i].unsqueeze(2).broadcast_to([P, NQ, n]), ALU.subtract).then_inc(shift_ok, 1)
        for i in range(2):
            n = P * (i + 1)
            dve.wait_ge(expp_ok, i + 1)
            link(V.tensor_reduce(smp[:, i], probs[:, i, :, 0:n], AX.X, ALU.add))
            link(V.reciprocal(smp[:, i], smp[:, i]))
            V.tensor_tensor(probs[:, i, :, 0:n], probs[:, i, :, 0:n],
                            smp[:, i].unsqueeze(2).broadcast_to([P, NQ, n]), ALU.mult).then_inc(pp_ok, 1)
        dve.wait_ge(iws_in, 16 * NB)
        for b in range(NB):
            a, g = 32 * (b % 4), b // 4
            dve.wait_ge(ikT_mm, b + 1)
            if b >= 1:
                dve.wait_ge(idx_mm, b)
            V.tensor_copy(ikeysT[:, 0:512], bk[0][:])
            V.tensor_copy(ikeysT[:, 512:1024], bk[1][:]).then_inc(ikT_ok, 1)
            dve.wait_ge(idx_mm, b + 1)
            w_ = iw_s[a:a + 32, g:g + 1]
            V.tensor_scalar(idx_s[a:a + 32, g, 0:512], bk[6][a:a + 32, :], 0.0, w_, ALU.max, ALU.mult)
            V.tensor_scalar(idx_s[a:a + 32, g, 512:1024], bk[7][a:a + 32, :], 0.0, w_, ALU.max, ALU.mult)
            V.tensor_scalar(idx_s[a:a + 32, g, 1024:NK], bk[2][a:a + 32, 0:TS], 0.0, w_, ALU.max,
                            ALU.mult).then_inc(idx_ok, 1)
        dve.wait_ge(isum_mm, 1)
        V.tensor_copy(sc_s[:, 0:512], bk[6][0:NS, :])
        V.tensor_copy(sc_s[:, 512:1024], bk[7][0:NS, :])
        V.tensor_tensor(sc_s[:, 1024:NK], bk[2][0:NS, 0:TS], C["causal_new"][0:NS], ALU.add).then_inc(sel_ok, 1)
        dve.wait_ge(sel_ok, 1)
        for r in range(SEL_S // 8):
            link(V.max(top8[0:NS], sc_s[:]))
            link(V.match_replace(sc_s[:], top8[0:NS], sc_s[:], TAKEN))
        V.tensor_scalar(sc_s[:], sc_s[:], -2.0e38, NEG, ALU.is_gt, ALU.mult).then_inc(sel_ok, 2)
        for g in range(2):
            dve.wait_ge(spread_mm, g + 1)
            dve.wait_ge(qk_ok, NB)
            for o, (c0, c1) in zip((1, 2, 3), ((0, 512), (512, 1024), (1024, NK))):
                last = V.scalar_tensor_tensor(att_s[:, g, c0:c1], att_s[:, g, c0:c1], HD ** -0.5, bk[o][:, 0:c1 - c0],
                                              ALU.mult, ALU.add)
            last.then_inc(att_ok, 1)
            dve.wait_ge(att_ok, 2 * g + 1)
            link(V.tensor_reduce(mxs[:, g:g + 1], att_s[:, g], AX.X, ALU.max))
            V.tensor_scalar(mxs[:, g:g + 1], mxs[:, g:g + 1], -1.0, None, ALU.mult).then_inc(att_ok, 1)
        for g in range(2):
            dve.wait_ge(exps_ok, g + 1)
            link(V.reciprocal(sms[:, g:g + 1], sms[:, g:g + 1]))
            V.tensor_scalar(att_s[:, g], att_s[:, g], sms[:, g:g + 1], None, ALU.mult).then_inc(ps_ok, 1)
        dve.wait_ge(pvs_mm, NB)
        o_s = bk[7][:, 0:256].rearrange("p (b h t) -> p h b t", b=NB, h=NQ)
        for g in range(2):
            last = V.tensor_copy(mixT[HD * g:HD * g + HD, 0:4, TP:T].rearrange("p j (b t) -> p j b t", b=NB),
                                 o_s[HD * g:HD * g + HD, 4 * g:4 * g + 4])
        last.then_inc(pvs_ok, 1)
        for c in range(KC):
            dve.wait_ge(om_mm, c + 1)
            V.tensor_tensor(xT[:, c], xT[:, c], bk[1 + c % 4][:, 0:T], ALU.add).then_inc(om_ok, 1)
        dve.wait_ge(om_ok, KC)
        rms_dve(dve, link, 1, xT, VEC["norm_ffn_even"], xn1)
        for f in range(FC):
            dve.wait_ge(silu_ok, f + 1)
            V.tensor_tensor(hid[:, f], sg[:, f % 2], bk[2 + f % 2][:, 0:T], ALU.mult).then_inc(hid_ok, 1)
        for half in range(2):
            dve.wait_ge(down_mm, (half + 1) * (FC // 2))
            for c in range(4):
                o = (4, 5, 6, 7)[c] if half == 0 else c
                V.tensor_tensor(xT[:, 4 * half + c], xT[:, 4 * half + c], bk[o][:, 0:T], ALU.add).then_inc(down_ok, 1)

        dve.wait_ge(down_ok, 8)
        rms_dve(dve, link, 2, xT, VEC["norm_mix_odd"], xn2)
        dve.wait_ge(xn_ok, 3 * KC)
        xs = xn2[:, :, TP:T].rearrange("p c (b t) -> p c b t", b=NB)
        ds_ = xx[:, :, TP:T].rearrange("p c (b t) -> p c b t", b=NB)
        shiftT = vecT[:, VEC["state_shift"]:VEC["state_shift"] + 64].rearrange("p (b c) -> p c b", b=NB)
        V.tensor_tensor(xx[:, :, 1:TP], xn2[:, :, 0:TP - 1], xn2[:, :, 1:TP], ALU.subtract)
        V.tensor_scalar(xx[:, :, 0:1], xn2[:, :, 0:1], -1.0, None, ALU.mult)
        for c in range(KC):
            V.tensor_tensor(ds_[:, c, :, 1:TS], xs[:, c, :, 0:TS - 1], xs[:, c, :, 1:TS], ALU.subtract)
        V.tensor_tensor(ds_[:, :, :, 0], shiftT, xs[:, :, :, 0], ALU.subtract).then_inc(xx_ok, 1)
        dve.wait_ge(xx_ok, 1)
        for i, m in enumerate((1, 4, 5, 2, 0, 3)):
            if i == 5:
                dve.wait_ge(job_mm, NIN + 32)
            elif i >= 2:
                dve.wait_ge(lh_mm, i - 1)
            for c in range(KC):
                v_ = VEC["mu"] + KC * m + c
                V.scalar_tensor_tensor(mx[:, i % 2, c], xx[:, c], vecT[:, v_:v_ + 1], xn2[:, c],
                                       ALU.mult, ALU.add).then_inc(mix_ok, 1)
        ka = VEC["rwkv_k_a"]
        pr = slice(0, TP)
        link(V.tensor_scalar(omk[:], vecT[:, ka:ka + KC], -1.0, 1.0, ALU.mult, ALU.add))
        dve.wait_ge(hs_mm, 1)
        for c in range(KC):
            last = V.tensor_scalar(t2[:, c], bk[c][:, 0:T], 1.0e-24, None, ALU.max)
        last.then_inc(nk_ok, 1)
        dve.wait_ge(nsq_ok, 1)
        link(V.reciprocal(t2[:], t2[:]))
        link(V.tensor_tensor(t1[:], t1[:], t2[:], ALU.mult))
        for c in range(KC):
            last = V.tensor_scalar(t3[:, c], aT[:, c], vecT[:, ka + c:ka + c + 1], omk[:, c:c + 1], ALU.mult, ALU.add)
        link(last)
        link(V.tensor_tensor(kT[:], kT[:], t3[:], ALU.mult))
        for c in range(KC):
            v_ = VEC["rwkv_r_k"] + c
            last = V.scalar_tensor_tensor(t2[:, c], rT[:, c], vecT[:, v_:v_ + 1], kT[:, c], ALU.mult, ALU.mult)
        last.then_inc(rk_ok, 1)
        V.tensor_tensor(aT[:], t1[:], aT[:], ALU.mult)
        link(V.tensor_scalar(lwT[:], lwT[:], -float(np.exp(np.float64(-0.5))), None, ALU.mult))
        for c in range(KC):
            for k in range(NCH):
                s_ = slice(k * CH, k * CH + CH)
                last = V.tensor_tensor_scan(t3[:, c, s_], C["ones"][:, 0:CH], lwT[:, c, s_], 0.0, ALU.mult, ALU.add)
        last.then_inc(cum_ok, 1)
        dve.wait_ge(cum_ok, 1)
        dve.wait_ge(hs_mm, 2)
        for c in range(KC):
            last = V.tensor_copy(bon[:, c] if c < 7 else ms[:], bk[c][:, 0:T])
        last.then_inc(bn_ok, 1)
        V.tensor_tensor(t2[:, :, pr], t3[:, :, pr], lwT[:, :, pr], ALU.subtract).then_inc(cum_ok, 1)
        dve.wait_ge(e_ok, 1)

        def tok(t):
            return t[:, :, pr].rearrange("p c (k t) -> p c k t", k=NCH)

        V.tensor_copy(PC[:], tok(t4)[:, :, :, CH - 1])
        V.tensor_tensor(AR[:, :, :, 1], tok(rT), tok(t4), ALU.mult).then_inc(ehat_ok, 1)
        dve.wait_ge(e_ok, 2)
        for c in range(KC):
            V.scalar_tensor_tensor(AR[:, c, :, 0], t1[:, c, pr].rearrange("p (k t) -> p k t", k=NCH), -1.0,
                                   t2[:, c, pr].rearrange("p (k t) -> p k t", k=NCH), ALU.mult, ALU.mult)
        dve.wait_ge(e_ok, 4)
        V.tensor_tensor(BK[:, :, :, 0], tok(aT), tok(t4), ALU.mult)
        V.tensor_tensor(BK[:, :, :, 1], tok(kT), tok(t4), ALU.mult).then_inc(arbk_ok, 1)
        for p2 in range(2):
            for gi in range(8):
                cc, par, half = gi // 4, gi // 2 % 2, gi % 2
                dve.wait_ge(g_mm, 8 * p2 + gi + 1)
                V.tensor_tensor(G[:, cc, par, 4 * half:4 * half + 4], bk[gi][:].rearrange("p (h t) -> p h t", h=4),
                                C["delta_mask"].unsqueeze(1).broadcast_to([P, 4, P]), ALU.mult).then_inc(g_ok, 1)

            def add_to(dst, first, other):
                for cc in range(2):
                    r = slice(CH * cc, CH * cc + CH)
                    for par in range(2):
                        last = V.tensor_tensor(dst[r, par], bk[first + 2 * cc + par][r, :].rearrange(
                            "p (h s) -> p h s", h=KC), other(r, par), ALU.add)
                return last

            eye = lambda r, par: C["ident64"][r].unsqueeze(1).broadcast_to([CH, KC, CH])
            def masked(j):
                mask = C["levels"][:, j * CH:(j + 1) * CH].unsqueeze(1).broadcast_to([P, KC, CH])
                for par in range(2):
                    last = V.tensor_tensor(Cj[:, par], L[:, par], mask, ALU.mult)
                last.then_inc(c_ok, 1)

            dve.wait_ge(l_ok, p2 + 1)
            masked(0)
            for j in range(6):
                if j == 0:
                    dve.wait_ge(c_ok, 6 * p2 + 1)
                    for par in range(2):
                        V.tensor_tensor(X[:, par], Cj[:, par], C["ident64"].unsqueeze(1).broadcast_to([P, KC, CH]), ALU.add)
                    dve.wait_ge(m_mm, 6 * p2 + 1)
                    add_to(Y, 0, eye).then_inc(xy_ok, 1)
                    dve.wait_ge(xy_ok, 6 * p2 + 1)
                    masked(1)
                else:
                    if j < 5:
                        dve.wait_ge(m_mm, 6 * p2 + j + 1)
                        masked(j + 1)
                    dve.wait_ge(xy_ok, 6 * p2 + j)
                    dve.wait_ge(y_mm, 5 * p2 + j)
                    last = add_to(Y, 4, lambda r, par: Y[r, par])
                    if j < 5:
                        dve.wait_ge(x_mm, 4 * p2 + j)
                        last = add_to(X, 0, lambda r, par: X[r, par])
                    last.then_inc(xy_ok, 1)
            for cc in range(2):
                c = 2 * p2 + cc
                r = slice(CH * cc, CH * cc + CH)
                if c:
                    dve.wait_ge(w1_ok, p2 + 1)
                    dve.wait_ge(w2_mm, c)
                    for par in range(2):
                        last = V.tensor_tensor(X[r, par], bk[par][r, :].rearrange("p (h s) -> p h s", h=KC),
                                               X[r, par], ALU.add)
                    last.then_inc(w_ok, 1)
                dve.wait_ge(s_mm, c + 1)
                dve.wait_ge(yo_mm, c + 1)
                upd = bk[6][:].rearrange("p (h v) -> p h v", h=KC)
                if c:
                    link(V.tensor_tensor(ST[:], upd, ST[:], ALU.add))
                    upd = ST[:]
                V.tensor_tensor(ST[:], upd, PC[:, :, c:c + 1].broadcast_to([P, KC, CH]), ALU.mult).then_inc(s_ok, 1)
        for i, (t0, tn) in enumerate(TILES):
            if i < 2:
                dve.wait_ge(yo_ok, 2 * (i + 1))
            else:
                dve.wait_ge(yrow_in, 16)
            y_ = y_rows[0:tn, i].rearrange("p (h v) -> p h v", h=RH)
            if i:
                dve.wait_ge(gn_ok, i)
            link(V.tensor_reduce(gst[0:tn], y_, AX.X, ALU.add))
            link(V.tensor_scalar(gst[0:tn], gst[0:tn], 1.0 / HD, None, ALU.mult))
            V.tensor_tensor(y_, y_, gst[0:tn].unsqueeze(2).broadcast_to([tn, RH, HD]),
                            ALU.subtract).then_inc(gn_act, 1)
            dve.wait_ge(gn_act, 2 * i + 2)
            link(V.tensor_reduce(gst2[0:tn], gsq[0:tn].rearrange("p (h v) -> p h v", h=RH), AX.X, ALU.add))
            V.tensor_scalar(gst2[0:tn], gst2[0:tn], 1.0 / HD, GN_EPS, ALU.mult, ALU.add).then_inc(gns_ok, 1)
            dve.wait_ge(gnq_ok, i + 1)
            link(V.reciprocal(gst2[0:tn], gst2[0:tn]))
            V.tensor_tensor(y_, y_, gst2[0:tn].unsqueeze(2).broadcast_to([tn, RH, HD]), ALU.mult).then_inc(gn_ok, 1)
        dve.wait_ge(bonT_in, 16)
        link(V.tensor_tensor(bonT[:], bonT[:], vT[:], ALU.mult))
        for c in range(KC):
            dve.wait_ge(yT_mm, c + 1)
            w_, b_ = VEC["rwkv_ln_w"] + c, VEC["rwkv_ln_b"] + c
            link(V.tensor_scalar(oT[:, c], bk[2 + c % 4][:, 0:T], vecT[:, w_:w_ + 1], vecT[:, b_:b_ + 1],
                                 ALU.mult, ALU.add))
            link(V.tensor_tensor(oT[:, c], oT[:, c], bonT[:, c], ALU.add))
            V.tensor_tensor(oT[:, c], oT[:, c], gT[:, c], ALU.mult).then_inc(oT_ok, 1)
        for c in range(KC):
            dve.wait_ge(om_mm, KC + c + 1)
            V.tensor_tensor(xT[:, c], xT[:, c], bk[2 + c % 4][:, 0:T], ALU.add).then_inc(om_ok, 1)

        dve.wait_ge(om_ok, KC + KC)
        rms_dve(dve, link, 3, xT, VEC["norm_ffn_odd"], xn3)
        V.memset(rank[:], -1.0)
        V.memset(share[:], 0.0)
        link(V.memset(ssf[:], 1.0))
        dve.wait_ge(lg_mm, 1)
        for i, (t0, tn) in enumerate(TILES):
            r = slice(0, tn)
            link(V.tensor_copy(lg[r, i], bk[1][r, NE * i:NE * i + NE]))
            link(V.max(top_v[r, i], lg[r, i]))
            link(V.max_index(top_i[r, i], top_v[r, i], lg[r, i]))
            link(V.tensor_copy(top_f[r, i], top_i[r, i]))
            V.tensor_scalar(hot1[r, i], C["slots"][r, 0:NE], top_f[r, i, 0:1], None, ALU.is_equal)
            V.tensor_scalar(hot2[r, i], C["slots"][r, 0:NE], top_f[r, i, 1:2], None, ALU.is_equal)
            link(V.tensor_tensor(gates[r, i, 1:2], top_v[r, i, 1:2], top_v[r, i, 0:1], ALU.subtract))
            last = V.tensor_tensor(sel[r, i], hot1[r, i], hot2[r, i], ALU.add)
        last.then_inc(sel2_ok, 1)
        dve.wait_ge(sel2_ok, 1)
        V.tensor_copy(blocks_f[0:1, 0:1], gates[0:1, 0, 1:2]).then_inc(gx_ok, 1)
        dve.wait_ge(gx_ok, 2)
        for i, (t0, tn) in enumerate(TILES):
            r = slice(0, tn)
            link(V.tensor_scalar(gates[r, i, 0:1], gates[r, i, 1:2], 1.0, None, ALU.add))
            link(V.reciprocal(gates[r, i, 0:1], gates[r, i, 0:1]))
            link(V.tensor_tensor(gates[r, i, 1:2], gates[r, i, 1:2], gates[r, i, 0:1], ALU.mult))
            link(V.tensor_scalar(comb[r, i], hot1[r, i], gates[r, i, 0:1], None, ALU.mult))
            link(V.scalar_tensor_tensor(comb[r, i], hot2[r, i], gates[r, i, 1:2], comb[r, i], ALU.mult, ALU.add))
        dve.wait_ge(rank_mm, 1)
        for i, (t0, tn) in enumerate(TILES):
            r = slice(0, tn)
            link(V.scalar_tensor_tensor(rank[r, i, 0:NE], bk[2][r, NE * i:NE * i + NE], 1.0, sel[r, i], ALU.add, ALU.mult))
            link(V.tensor_scalar(rank[r, i, 0:NE], rank[r, i, 0:NE], -1.0, None, ALU.add))
            for b in range(T // CAP):
                if b:
                    V.tensor_scalar(rank[r, i, NE * b:NE * b + NE], rank[r, i, 0:NE], -float(CAP * b), None, ALU.add)
                link(V.tensor_copy(share[r, i, NE * b:NE * b + NE], comb[r, i]))
        link(V.tensor_reduce(blocks_f[0:1, 0:1], bk[2][0:1, 4 * NE:5 * NE], AX.X, ALU.max))
        link(V.tensor_scalar(blocks_f[0:1, 1:2], blocks_f[0:1, 0:1], float(CAP), 1.0, ALU.is_gt, ALU.add))
        for b in range(2, T // CAP):
            link(V.tensor_scalar(blocks_f[0:1, 2:3], blocks_f[0:1, 0:1], float(CAP * b), None, ALU.is_gt))
            link(V.tensor_tensor(blocks_f[0:1, 1:2], blocks_f[0:1, 1:2], blocks_f[0:1, 2:3], ALU.add))
        V.tensor_copy(blocks[:], blocks_f[0:1, 1:2]).then_inc(blocks_ok, 1)
        for i, (t0, tn) in enumerate(TILES):
            last = V.tensor_scalar(pick[0:tn, i], C["slots"][0:tn, 0:CAP], rank[0:tn, i, 0:1], None, ALU.is_equal)
        last.then_inc(pick_ok, 1)

        def expert(it):
            dve.wait_ge(xg_mm, it + 1)
            dve.wait_ge(down_mm, FC * it + FC)
            for i, (t0, tn) in enumerate(TILES):
                r = slice(0, tn)
                V.tensor_scalar(give[r, i], C["slots"][r, 0:CAP], rank[r, i, bass.ds(it, 1)],
                                share[r, i, bass.ds(it, 1)], ALU.is_equal, ALU.mult)
                last = V.tensor_scalar(pick[r, i], C["slots"][r, 0:CAP], rank[r, i, bass.ds(it + 1, 1)], None,
                                       ALU.is_equal)
            last.then_inc(pick_ok, 1)
            for f in range(FC):
                dve.wait_ge(silu_ok, FC + FC * it + f + 1)
                V.tensor_tensor(hid2[:, f], sg2[:, f % 2], bk[f % 2][:, CAP:2 * CAP], ALU.mult).then_inc(hid_ok, 1)
            dve.wait_ge(gt_mm, it + 1)
            dve.wait_ge(sc_ok, 6 * it + 1)
            V.tensor_copy(giveT[:], bk[5][0:CAP, 0:T]).then_inc(gt_ok, 1)
            for g in range(6):
                i, half = g // 2, g % 2
                tn = TILES[i][1]
                dve.wait_ge(sc_mm, 6 * it + g + 1)
                a = acc[0:tn, i, 512 * half:512 * half + 512]
                V.tensor_tensor(a, a, bk[(4, 5, 0, 1)[g % 4]][0:tn, :], ALU.add).then_inc(sc_ok, 1)

        dve.wait_ge(tk_ok, 12)
        V.tensor_copy(blocks_f[0:1, 3:4], blocks_f[0:1, 1:2]).then_inc(sc_ok, 1)
        dve.wait_ge(blocks_ok, 1)
        n_blocks = dve.value_load(blocks[0:1, 0:1], min_val=1, max_val=T // CAP)
        with dve.Fori(0, n_blocks) as blk:
            with dve.Fori(0, NE) as e:
                expert(blk * NE + e)
        dve.wait_ge(sc_ok, n_blocks * (6 * NE) + 1)
        dve.wait_ge(sq_ok, 4 * KC + 1)
        V.tensor_scalar(ssf[:], ssf[:], 1.0 / D, EPS, ALU.mult, ALU.add).then_inc(ms_ok, 1)
        dve.wait_ge(sd_ok, 5)
        link(V.reciprocal(ssf[:], ssf[:]))
        dve.wait_ge(rt_in, 32)
        for i, (t0, tn) in enumerate(TILES):
            V.scalar_tensor_tensor(y_out[0:tn, i], acc[0:tn, i], ssf[0:tn, i:i + 1], gain_f[0:tn], ALU.mult,
                                   ALU.mult).then_inc(fin_ok, 1)

    @block.gpsimd
    def _(pool):
        link = chained(pool, pool_chain)
        G = nc.gpsimd
        pool.dma_start(pg_ids[:], I["page_table"].rearrange("b n -> (b n)").unsqueeze(0)).then_inc(ids_in, 16)
        for t in (q_s, iq_s, iw_s):
            link(pool.memset(t[:], 0.0))
        pool.wait_ge(ids_in, 16)

        def load_pages(b):
            with pool.Fori(0, NPG) as g:
                page = pool.value_load(pg_ids[0:1, bass.ds(g + NPG * b, 1)], min_val=0, max_val=N_POOL - 1)
                k_src = I["cache_k"][0, bass.ds(page, 1)].rearrange("o p g d -> p (o g d)")
                ik_src = I["cache_idx_k"][0, bass.ds(page, 1)].rearrange("o p d -> p (o d)")
                pool.dma_start(k_pages[:, bass.ds(g, 1)].rearrange("p o d -> p (o d)"), k_src).then_inc(page_in, 16)
                for a in range(2):
                    pool.dma_start(ik_pages[:, bass.ds(g, 1), a].rearrange("p o d -> p (o d)"),
                                   ik_src).then_inc(page_in, 16)

        def load_values(b):
            with pool.Fori(0, NPG) as g:
                page = pool.value_load(pg_ids[0:1, bass.ds(g + NPG * b, 1)], min_val=0, max_val=N_POOL - 1)
                src = I["cache_v"][0, bass.ds(page, 1)].rearrange("o p g d -> p (o g d)")
                pool.dma_start(v_pages[:, b % 2, bass.ds(g, 1)].rearrange("p o d -> p (o d)"),
                               src).then_inc(vpage_in[b % 2], 16)

        load_pages(0)
        load_values(0)
        load_values(1)
        pool.wait_ge(head_in, HEAD)
        for j in range(8):
            pool.wait_ge(job_ok, j + 1)
            G.tensor_tensor(rp[:, j], raw[:, j], C["cos"], ALU.mult).then_inc(rope_pool, 1)
        pool.wait_ge(rope_ok, 8)
        for g in range(2):
            r = slice(HD * g, HD * g + HD)
            src = rp[r, 4:8, TP:T].rearrange("p j (b t) -> p b j t", b=NB)
            dst = q_s[r, :, 16 * g:16 * g + 16].rearrange("p b (j t) -> p b j t", j=4)
            for b in range(NB):
                G.tensor_copy(dst[:, b], src[:, b])
            G.tensor_copy(iq_s[r, :, 0:16].rearrange("p b (t h) -> p b t h", h=NIH)[:, :, :, g],
                          rp[r, 2, TP:T].rearrange("p (b t) -> p b t", b=NB)).then_inc(qs_ok, 1)
            G.tensor_copy(iq_s[r, :, 0:16].rearrange("p b (t h) -> p b t h", h=NIH)[:, :, :, 2 + g],
                          rp[r, 3, TP:T].rearrange("p (b t) -> p b t", b=NB)).then_inc(qs_ok, 1)
            pool.wait_ge(qs_ok, 2 * (g + 1))
        for b in range(NB):
            if b >= 1:
                pool.wait_ge(qk_mm, b)
            G.tensor_copy(keysT[:, 1024:NK], rp[:, 0, TP + TS * b:TP + TS * b + TS]).then_inc(new_ok, 1)
            if b >= 1:
                pool.wait_ge(idx_mm, b)
            G.tensor_copy(ikeysT[:, 1024:NK], rp[:, 1, TP + TS * b:TP + TS * b + TS]).then_inc(new_ok, 1)
            if b + 1 < NB:
                pool.wait_ge(ikT_mm, b + 1)
                load_pages(b + 1)
        pool.wait_ge(vec_ok, 1)
        pool.wait_ge(job_ok, len(IN_JOBS))
        link(G.memset(u_p[:, :, 0:2], 0.0))
        conv_prev = vecT[:, 256:320].rearrange("p (b j c) -> p c b j", b=NB, j=2)
        for c in range(4):
            G.tensor_copy(u_s[:, c, :, 0:2], conv_prev[:, c])
            G.tensor_tensor(u_p[:, c, 2:2 + TP], ccb[:, 0, c, 0:TP], ccb[:, 1, c, 0:TP], ALU.mult)
            link(G.tensor_tensor(u_s[:, c, :, 2:2 + TS], ccb[:, 0, c, TP:T].rearrange("p (b t) -> p b t", b=NB),
                                 ccb[:, 1, c, TP:T].rearrange("p (b t) -> p b t", b=NB), ALU.mult))
        G.tensor_copy(u_last[:, :, 0:2], u_p[:, :, TP:TP + 2])
        for c in range(4):
            last = G.tensor_copy(u_last[:, c, 2:2 + 2 * NB].rearrange("p (b j) -> p b j", j=2), u_s[:, c, :, TS:TS + 2])
        last.then_inc(conv_ok, 1)
        for c in range(4):
            y_p = mixT[:, 4 + c, 0:TP]
            y_s = mixT[:, 4 + c, TP:T].rearrange("p (b t) -> p b t", b=NB)
            for j in range(3):
                w_ = vecT[:, VEC["conv_w"] + 4 * j + c:VEC["conv_w"] + 4 * j + c + 1]
                if j == 0:
                    G.tensor_scalar(y_p, u_p[:, c, 0:TP], w_, None, ALU.mult)
                    link(G.tensor_scalar(y_s, u_s[:, c, :, 0:TS], w_, None, ALU.mult))
                else:
                    t_p = ccb[:, 0, c, 0:TP]
                    t_s = ccb[:, 0, c, TP:T].rearrange("p (b t) -> p b t", b=NB)
                    G.tensor_scalar(t_p, u_p[:, c, j:j + TP], w_, None, ALU.mult)
                    link(G.tensor_scalar(t_s, u_s[:, c, :, j:j + TS], w_, None, ALU.mult))
                    G.tensor_tensor(y_p, y_p, t_p, ALU.add)
                    link(G.tensor_tensor(y_s, y_s, t_s, ALU.add))
            last = G.tensor_tensor(mixT[:, 4 + c], mixT[:, 4 + c], ccb[:, 2, c], ALU.mult)
        last.then_inc(conv_ok, 1)
        for b in range(2, NB):
            pool.wait_ge(pvs_mm, b - 1)
            load_values(b)

        G_ = nc.gpsimd
        pool.wait_ge(xn_ok, 3 * KC)
        pool.wait_ge(lh_mm, 3)
        pool.wait_ge(job_mm, NIN + 24)
        G_.tensor_copy(e_last[:, :, 0], xn2[:, :, TP - 1]).then_inc(el_ok, 1)
        G_.tensor_copy(e_last[:, :, 1:1 + NB], xn2[:, :, TP:T].rearrange("p c (b t) -> p c b t", b=NB)[:, :, :, TS - 1]
                       ).then_inc(el_ok, 1)
        pool.wait_ge(job_ok, NIN + 32)
        pool.wait_ge(out_done, 16 * OUT_1)
        for c in range(KC):
            v_ = VEC["rwkv_k_k"] + c
            last = G_.tensor_scalar(t1[:, c], kT[:, c], vecT[:, v_:v_ + 1], None, ALU.mult)
        last.then_inc(t1_ok, 1)

        def key_sum(out):
            w = HD // 2
            while w > 1:
                link(G_.tensor_tensor(stmp[:, :, 0:w], stmp[:, :, 0:w], stmp[:, :, w:2 * w], ALU.add))
                w //= 2
            return G_.tensor_tensor(out, stmp[:, :, 0], stmp[:, :, 1], ALU.add)

        def sample_step(t):
            r_, w_, k_, v_, kk_, b_ = (s6[:, t, q] for q in range(6))
            n = HD // 2
            key = lambda x: x.unsqueeze(1).broadcast_to([P, n, HD])
            for half in range(2):
                rows_ = slice(n * half, n * half + n)
                Sh = S[:, rows_]
                val = lambda x: x[:, rows_].unsqueeze(2).broadcast_to([P, n, HD])
                link(G_.tensor_tensor(stmp[:], Sh, key(kk_), ALU.mult))
                link(key_sum(sa[:, rows_]))
                link(G_.tensor_tensor(Sh, Sh, key(w_), ALU.mult))
                link(G_.tensor_tensor(stmp[:], val(sa), key(b_), ALU.mult))
                link(G_.tensor_tensor(Sh, Sh, stmp[:], ALU.subtract))
                link(G_.tensor_tensor(stmp[:], val(v_), key(k_), ALU.mult))
                link(G_.tensor_tensor(Sh, Sh, stmp[:], ALU.add))
                link(G_.tensor_tensor(stmp[:], Sh, key(r_), ALU.mult))
                last = key_sum(ys[:, t, rows_])
                if half:
                    last.then_inc(ys_ok, 1)
                    pool.wait_ge(ys_ok, t + 1)
                else:
                    link(last)

        pool.wait_ge(s6_in, 16 * (NB + 1))
        for t in range(TS):
            sample_step(t)

    ctx.close()


INPUTS = ["x_prompt", "x_sample", "cache_k", "cache_v", "cache_idx_k", "state_conv", "state_shift", "state_wkv",
          "page_table", "norm_mix_even", "w_in_even", "conv_w", "w_out_even", "norm_ffn_even", "ffn_gate", "ffn_up",
          "ffn_down", "norm_mix_odd", "rwkv_mu", "rwkv_w_rkv", "rwkv_w0", "rwkv_w1", "rwkv_w2", "rwkv_a0",
          "rwkv_a1", "rwkv_a2", "rwkv_g1", "rwkv_g2", "rwkv_k_k", "rwkv_k_a", "rwkv_r_k", "rwkv_ln_w", "rwkv_ln_b",
          "rwkv_w_o", "norm_ffn_odd", "moe_router", "moe_gate", "moe_up", "moe_down", "norm_final"]
OUTPUTS = [("y_prompt", (1, TP, D)), ("y_sample", (NB, TS, D)), ("k_prompt", (1, 1, TP, NKV, HD)),
           ("v_prompt", (1, 1, TP, NKV, HD)), ("idx_k_prompt", (1, 1, TP, HD)), ("k_sample", (1, NB, TS, NKV, HD)),
           ("v_sample", (1, NB, TS, NKV, HD)), ("idx_k_sample", (1, NB, TS, HD)), ("conv_prompt", (1, 1, 2, CONV)),
           ("conv_sample", (1, NB, 2, CONV)), ("shift_prompt", (1, 1, D)), ("shift_sample", (1, NB, D)),
           ("wkv_prompt", (1, 1, RH, HD, HD)), ("wkv_sample", (1, NB, RH, HD, HD))]


def kernel(**inputs):
    import concourse.bacc as bacc
    from concourse.bass_utils import run_bass_kernel_spmd

    nc = bacc.Bacc("TRN2", target_bir_lowering=False, num_devices=1)
    arrays, I, O = {}, {}, {}
    for name in INPUTS:
        a = np.ascontiguousarray(inputs[name])
        arrays[f"in_{name}"] = a
        I[name] = nc.dram_tensor(f"in_{name}", a.shape, mybir.dt.from_np(a.dtype), kind="ExternalInput").ap()
    arrays["in_consts"] = np.concatenate([CONSTS[k] for k in COL], 1)
    I["consts"] = nc.dram_tensor("in_consts", arrays["in_consts"].shape, F32, kind="ExternalInput").ap()
    for name, shape in OUTPUTS:
        O[name] = nc.dram_tensor(f"out_{name}", shape, F32, kind="ExternalOutput").ap()
    build(nc, I, O)
    r = run_bass_kernel_spmd(nc, [arrays], core_ids=[0])
    return tuple(r.results[0][f"out_{name}"] for name, _ in OUTPUTS)
```

```python
from contextlib import ExitStack

import numpy as np

import concourse.bass as bass
from concourse import mybir

F32 = mybir.dt.float32
I32 = mybir.dt.int32
U32 = mybir.dt.uint32
ALU = mybir.AluOpType
ACT = mybir.ActivationFunctionType
AX = mybir.AxisListType

P = 128
D = 1024
KC = D // P
TP = 256
NB, TS = 8, 4
NS = NB * TS
T = TP + NS
TILES = ((0, 128), (128, 128), (256, NS))
HD = 64
NQ, NKV, NIH = 8, 2, 4
PAST, PAGE, NPG = 1024, 128, 8
NK = PAST + TS
SEL_P, SEL_S = 64, 256
CONV = 512
FF = 2816
FC = FF // P
NE = 8
RH = 16
POOL_ROWS = 48
CH = 64
NCH = TP // CH
CAP = 96
EPS = 1e-6
GN_EPS = 64e-5
NEG = -1.0e30
TAKEN = -3.0e38
SP_PAGES = 4
SP_IK_PAGES = 2
RING = 11
SLOT = 1024

Q0, K0, V0, IQ0, IK0, IW0, CB0, CC0, CH0 = 0, 512, 640, 768, 1024, 1088, 1092, 1604, 2116

VEC_NAMES = ["norm_mix_even", "norm_ffn_even", "norm_mix_odd", "norm_ffn_odd", "mu", "rwkv_w0", "rwkv_a0",
             "rwkv_k_k", "rwkv_k_a", "rwkv_r_k", "rwkv_ln_w"]
VEC = {}
_at = 0
for _n in VEC_NAMES:
    VEC[_n] = _at
    _at += 48 if _n == "mu" else 8
VEC["rwkv_ln_b"] = 128
VEC["conv_w"] = 136
VEC["state_shift"] = 148
VEC["state_conv"] = 256


def constants():
    p = np.arange(P)
    c = {}
    c["ident"] = np.eye(P)
    c["ones"] = np.ones((P, P))
    c["headones"] = (p[:, None] // HD == p[None, :] // HD).astype(np.float32)
    rot = np.zeros((P, P))
    for h in (0, HD):
        for i in range(8):
            rot[h + 8 + i, h + i] = -1.0
            rot[h + i, h + 8 + i] = 1.0
    c["rot"] = rot
    pos = np.concatenate([np.arange(TP), np.tile(PAST + np.arange(TS), NB)]).astype(np.float32)
    inv = (np.float32(500000.0) ** (-np.arange(8, dtype=np.float32) / np.float32(8))).astype(np.float32)
    ang = inv[:, None] * pos[None, :]
    cos, sin = np.ones((P, T)), np.zeros((P, T))
    for h in (0, HD):
        for half in (0, 8):
            cos[h + half:h + half + 8] = np.cos(ang.astype(np.float64))
            sin[h + half:h + half + 8] = np.sin(ang.astype(np.float64))
    c["cos"], c["sin"] = cos, sin
    c["causal"] = np.concatenate([np.where(np.arange(TP)[None] <= (i * P + p)[:, None], 0.0, NEG)
                                  for i in range(2)], 1)
    new = np.zeros((P, TS))
    new[:NS] = np.where(np.arange(TS)[None] <= (np.arange(NS) % TS)[:, None], 0.0, NEG)
    c["causal_new"] = new
    selh = np.zeros((P, 2, NS))
    selm = np.zeros((P, 2, P))
    for g in range(2):
        for b in range(4):
            for t in range(TS):
                for h in range(NIH):
                    selh[32 * b + 4 * t + h, g, (4 * g + b) * TS + t] = 1.0
                for h in range(NQ):
                    selm[(4 * g + b) * TS + t, g, 32 * b + 4 * h + t] = 1.0
    c["sel_sum"], c["sel_spread"] = selh.reshape(P, -1), selm.reshape(P, -1)
    s, t = (p % CH)[:, None], (p % CH)[None, :]
    c["delta_mask"] = np.where(p[None, :] < CH, s < t, s <= t)
    lo = np.zeros((P, 6, CH))
    for j in range(6):
        b = 1 << j
        tt, ss = (p % CH)[:, None], np.arange(CH)[None, :]
        lo[:, j] = (tt // (2 * b) == ss // (2 * b)) & (tt % (2 * b) >= b) & (ss % (2 * b) < b)
    c["levels"] = lo.reshape(P, -1)
    c["ident64"] = np.concatenate([np.eye(CH), np.eye(CH)], 0)
    c["before"] = p[:, None] < p[None, :]
    c["slots"] = np.tile(np.arange(P)[None], (P, 1))
    return {k: np.asarray(v, np.float32) for k, v in c.items()}


CONSTS = constants()
COL = {}
_at = 0
for _n, _v in CONSTS.items():
    COL[_n] = (_at, _at + _v.shape[1])
    _at += _v.shape[1]
NCOL = _at


class Plan:

    def __init__(self):
        self.items = []

    def add(self, name, pieces, freed_by, value):
        self.items.append((name, pieces, freed_by, value))


def build(nc, I, O):
    ctx = ExitStack()
    place = [16512]

    def sbt(name, shape, dtype=F32, at=None):
        n = int(np.prod(shape[1:])) * 4
        n = (n + 31) // 32 * 32
        if at is None:
            at = place[0]
            place[0] += n
        assert at + n <= 229344, (name, at + n)
        t = nc.alloc_sbuf_tensor_at(name, list(shape), dtype, offset=at)
        ends[name] = at + n
        starts[name] = at
        return t

    ends, starts = {}, {}

    def sem(name):
        return ctx.enter_context(nc.semaphore(name))

    ring = [sbt(f"ring{i}", [P, SLOT]) for i in range(RING)]
    cst = sbt("cst", [P, NCOL])
    C = {k: cst[:, a:b] for k, (a, b) in COL.items()}
    vecT = sbt("vecT", [P, 2 * P + 64])
    xT = sbt("xT", [P, KC, T])
    ms = sbt("ms", [P, T])
    rs = sbt("rs", [P, T])
    arena = place[0]
    bk = [nc.alloc_psum_tensor(f"bk{i}", [P, 512], F32) for i in range(8)]

    x_rows = sbt("x_rows", [P, 3, D])
    sq = sbt("sq", [P, KC, T], at=starts["x_rows"])
    probsT = sbt("probsT", [P, 3, NQ, P], at=starts["x_rows"])
    xn = sbt("xn", [P, KC, T])
    raw = sbt("raw", [P, 9, T])
    rp = sbt("rp", [P, 8, T])
    ccb = sbt("ccb", [P, 3, 4, T])
    probs = sbt("probs", [P, 2, NQ, TP])
    mixT = sbt("mixT", [P, KC, T])
    rows = sbt("rows", [P, 3, 3, P])
    iw = sbt("iw", [P, 3, NIH])
    vec_rows = sbt("vec_rows", [P, 3, P], at=starts["probs"])
    sc_p = sbt("sc_p", [P, 2, TP])
    tmp_p = sbt("tmp_p", [P, 4, TP])
    top8 = sbt("top8", [P, 8])
    mxp = sbt("mxp", [P, 2, NQ])
    smp = sbt("smp", [P, 2, NQ])
    pg_ids = sbt("pg_ids", [1, NB * NPG], I32)
    k_pages = sbt("k_pages", [P, 2, NPG, P])
    ik_pages = sbt("ik_pages", [P, 2, NPG, HD])
    keysT = sbt("keysT", [P, NK])
    ikeysT = sbt("ikeysT", [P, 4 * P + TS])
    pS_T = sbt("pS_T", [P, 9, P], at=starts["k_pages"])
    v_new = sbt("v_new", [TS, NB, P])
    q_s = sbt("q_s", [P, NB, 32])
    iq_s = sbt("iq_s", [P, NB, 32])
    iw_s = sbt("iw_s", [P, 2])
    idx_s = sbt("idx_s", [P, 2, NK])
    att_s = sbt("att_s", [P, 2, NK])
    sc_s = sbt("sc_s", [NS, NK], at=starts["k_pages"] + 4 * 9 * P)
    v_pages = [sbt(f"v_pages{b}", [P, NPG, P]) for b in range(2)]
    v_at = (-(-(starts["sc_s"] + 4 * NK) // 32) * 32, starts["idx_s"], starts["probs"])
    for b in range(2, NB):
        v_pages.append(sbt(f"v_pages{b}", [P, NPG, P], at=v_at[b // 2 - 1] + (b % 2) * 4 * NPG * P))
    mxs = sbt("mxs", [P, 2])
    sms = sbt("sms", [P, 2])
    u_p = sbt("u_p", [P, 4, 2 + TP], at=starts["raw"])
    u_s = sbt("u_s", [P, 4, NB, 2 + TS], at=starts["raw"] + 4 * 4 * (2 + TP))
    u_last = sbt("u_last", [P, 4, 2 + 2 * NB])
    conv_rows = sbt("conv_rows", [2 + 2 * NB, CONV])

    place[0] = arena
    sq1 = sbt("sq1", [P, KC, T])
    xn1 = sbt("xn1", [P, KC, T])
    hid = sbt("hid", [P, FC, T])
    sg = sbt("sg", [P, 2, T])


    place[0] = arena
    rT = sbt("rT", [P, KC, T])
    kT = sbt("kT", [P, KC, T])
    aT = sbt("aT", [P, KC, T])
    lwT = sbt("lwT", [P, KC, T])
    vT = sbt("vT", [P, KC, T])
    gT = sbt("gT", [P, KC, T])
    xn2 = sbt("xn2", [P, KC, T])
    xx = sbt("xx", [P, KC, T])
    mx = sbt("mx", [P, 2, KC, T])
    sq2 = sbt("sq2", [P, KC, T], at=starts["mx"])
    G = sbt("G", [P, 2, 2, KC, P])
    L = sbt("L", [P, 2, KC, CH])
    Cj = sbt("Cj", [P, 2, KC, CH])
    M = sbt("M", [P, 2, KC, CH])
    X = sbt("X", [P, 2, KC, CH])
    Y = sbt("Y", [P, 2, KC, CH])
    Z = sbt("Z", [P, 2, KC, 2, CH])
    s6 = sbt("s6", [P, TS, 6, HD])
    omk = sbt("omk", [P, KC])
    gst = sbt("gst", [P, 3, RH])
    gst2 = sbt("gst2", [P, 3, RH])
    t1, t2, t3, t4 = (sbt(f"t{i + 1}", [P, KC, T], at=starts["G"] + 9216 * i) for i in range(4))
    bon = sbt("bon", [P, 7, T], at=starts["G"] + 4 * 9216)
    st = sbt("st", [NS, 6, D], at=starts["t2"])
    lh = sbt("lh", [P, 3, T], at=starts["G"])
    e_last = sbt("e_last", [P, KC, 1 + NB], at=starts["G"] + 4096)
    shift_rows = sbt("shift_rows", [1 + NB, D], at=starts["G"] + 5120)
    AR = sbt("AR", [P, KC, NCH, 2, CH], at=starts["xn2"])
    BK = sbt("BK", [P, KC, NCH, 2, CH], at=starts["xn2"] + 16384)
    ST = sbt("ST", [P, KC, CH], at=starts["xn2"] + 32768)
    PC = sbt("PC", [P, KC, NCH], at=starts["xn2"] + 32768 + 2048)
    S = sbt("S", [P, HD, HD], at=starts["rT"])
    y_rows = sbt("y_rows", [P, 3, D], at=starts["rT"] + 16384)
    stmp = sbt("stmp", [P, POOL_ROWS // 2, HD], at=starts["rT"] + 16384 + 12288)
    sa = sbt("sa", [P, HD], at=starts["xn2"] + 32768 + 2048 + 128)
    ys = sbt("ys", [P, TS, HD], at=starts["xn2"] + 32768 + 2048 + 128 + 256)
    BKt = sbt("BKt", [P, 2, KC, P], at=starts["L"])
    bonT = sbt("bonT", [P, KC, T], at=starts["G"])
    oT = sbt("oT", [P, KC, T], at=starts["xn2"])
    gsq = sbt("gsq", [P, 3, D], at=starts["L"])
    st_rows = sbt("st_rows", [HD, RH, HD], at=starts["X"])
    q6_dram = nc.dram_tensor("q6_dram", [NS, 6, D], F32, kind="Internal").ap()
    bon_dram = nc.dram_tensor("bon_dram", [P, KC, T], F32, kind="Internal").ap()
    ys_dram = nc.dram_tensor("ys_dram", [NB, TS, RH, HD], F32, kind="Internal").ap()

    place[0] = arena
    xn3 = sbt("xn3", [P, KC, T])
    sq3 = sbt("sq3", [P, KC, T])
    acc = sbt("acc", [P, 3, D])
    xr = sbt("xr", [P, 3, D])
    w_rt = sbt("w_rt", [P, KC, NE])
    lg = sbt("lg", [P, 3, NE])
    top_v = sbt("top_v", [P, 3, NE])
    top_i = sbt("top_i", [P, 3, NE], U32)
    top_f = sbt("top_f", [P, 3, NE])
    hot1 = sbt("hot1", [P, 3, NE])
    hot2 = sbt("hot2", [P, 3, NE])
    sel = sbt("sel", [P, 3, NE])
    comb = sbt("comb", [P, 3, NE])
    gates = sbt("gates", [P, 3, 2])
    NIT = NE * (T // CAP)
    rank = sbt("rank", [P, 3, NIT + NE])
    share = sbt("share", [P, 3, NIT + NE])
    blocks_f = sbt("blocks_f", [1, 4])
    blocks = sbt("blocks", [1, 1], I32)
    pick = sbt("pick", [P, 3, CAP])
    give = sbt("give", [P, 3, CAP])
    giveT = sbt("giveT", [CAP, T])
    xg = sbt("xg", [P, KC, CAP])
    hid2 = sbt("hid2", [P, FC, CAP])
    sg2 = sbt("sg2", [P, 2, CAP])
    yT = sbt("yT", [P, KC, CAP])
    ye = sbt("ye", [CAP, D])
    ring2 = [sbt(f"ring2_{i}", [P, SLOT]) for i in range(RING)]
    gain_f = sbt("gain_f", [P, D])
    y_out = sbt("y_out", [P, 3, D])
    ssf = sbt("ssf", [P, 3])
    iw_dram = nc.dram_tensor("iw_dram", [NS, NIH], F32, kind="Internal").ap()
    N_POOL = I["cache_k"].shape[1]
    OUT_0 = 7
    OUT_1 = OUT_0 + 2
    N_OUT = OUT_1 + 2 + 2

    head_in = sem("head_in")
    HEAD = 16 * (3 + len(VEC_NAMES) + 4)
    slot_in = [sem(f"slot_in{i}") for i in range(RING)]
    out_done = sem("out_done")
    dve_chain, pool_chain = sem("dve_chain"), sem("pool_chain")
    vec_mm, vec_ok = sem("vec_mm"), sem("vec_ok")
    xT_mm, xT_ok = sem("xT_mm"), sem("xT_ok")
    sq_ok, ssq_mm, ms_ok, sd_ok, xn_ok = sem("sq_ok"), sem("ssq_mm"), sem("ms_ok"), sem("sd_ok"), sem("xn_ok")
    job_mm, job_ok = sem("job_mm"), sem("job_ok")
    iw_mm, iw_ok, iws_in = sem("iw_mm"), sem("iw_ok"), sem("iws_in")
    rot_mm, rope_ok, rope_pool = sem("rot_mm"), sem("rope_ok"), sem("rope_pool")
    qs_ok = sem("qs_ok")
    turn_mm, turn_ok = sem("turn_mm"), sem("turn_ok")
    temp_out, vnew_in = sem("temp_out"), sem("vnew_in")
    ids_in, new_ok = sem("ids_in"), sem("new_ok")
    page_in = [sem("page_in0"), sem("page_in1")]
    ik_page_in = [sem("ik_page_in0"), sem("ik_page_in1")]
    kT_mm, kT_ok, qk_mm, qk_ok = sem("kT_mm"), sem("kT_ok"), sem("qk_mm"), sem("qk_ok")
    ikT_mm, ikT_ok, idx_mm, idx_ok = sem("ikT_mm"), sem("ikT_ok"), sem("idx_mm"), sem("idx_ok")
    isum_mm, sel_ok, spread_mm, att_ok = sem("isum_mm"), sem("sel_ok"), sem("spread_mm"), sem("att_ok")
    exps_ok, ps_ok, psT_mm, psT_ok = sem("exps_ok"), sem("ps_ok"), sem("psT_mm"), sem("psT_ok")
    vpage_in = [sem("vpage_in0"), sem("vpage_in1")]
    pvs_mm, pvs_ok = sem("pvs_mm"), sem("pvs_ok")
    ip_mm, ip_ok = sem("ip_mm"), sem("ip_ok")
    sp_mm, sp_ok, shift_ok, expp_ok = sem("sp_mm"), sem("sp_ok"), sem("shift_ok"), sem("expp_ok")
    pp_ok, ppT_mm, ppT_ok, pvp_mm, pvp_ok = sem("pp_ok"), sem("ppT_mm"), sem("ppT_ok"), sem("pvp_mm"), sem("pvp_ok")
    conv_ok = sem("conv_ok")
    omp_mm, omp_ok = sem("omp_mm"), sem("omp_ok")
    om_mm, om_ok = sem("om_mm"), sem("om_ok")
    gu_mm, silu_ok, hid_ok, down_mm, down_ok = sem("gu_mm"), sem("silu_ok"), sem("hid_ok"), sem("down_mm"), sem("down_ok")


    xx_ok, mix_ok, lh_mm, lh_ok = (sem(n) for n in ("xx_ok", "mix_ok", "lh_mm", "lh_ok"))
    el_ok = sem("el_ok")
    t1_ok, sqk_ok, hs_mm, nk_ok, nsq_ok = (sem(n) for n in ("t1_ok", "sqk_ok", "hs_mm", "nk_ok", "nsq_ok"))
    rk_ok, bn_ok, cum_ok, e_ok = (sem(n) for n in ("rk_ok", "bn_ok", "cum_ok", "e_ok"))
    ehat_ok, arbk_ok = sem("ehat_ok"), sem("arbk_ok")
    st_mm, st_ok = sem("st_mm"), sem("st_ok")
    st_out = sem("st_out")
    s6_in, ys_ok, yrow_in = sem("s6_in"), sem("ys_ok"), sem("yrow_in")
    vt_mm, vt_ok, g_mm, g_ok, l_mm, l_ok = (sem(n) for n in ("vt_mm", "vt_ok", "g_mm", "g_ok", "l_mm", "l_ok"))
    c_ok, m_mm, m_ok, y_mm, x_mm, xy_ok = (sem(n) for n in ("c_ok", "m_mm", "m_ok", "y_mm", "x_mm", "xy_ok"))
    bt_mm, bt_ok, w1_mm, w1_ok, w2_mm, w_ok = (sem(n) for n in ("bt_mm", "bt_ok", "w1_mm", "w1_ok", "w2_mm", "w_ok"))
    u_mm, u_ok, s_mm, s_ok, yo_mm, yo_ok = (sem(n) for n in ("u_mm", "u_ok", "s_mm", "s_ok", "yo_mm", "yo_ok"))
    gn_ok, gn_act, yT_mm, oT_ok = (sem(n) for n in ("gn_ok", "gn_act", "yT_mm", "oT_ok"))
    gns_ok, gnq_ok = sem("gns_ok"), sem("gnq_ok")
    bonT_in = sem("bonT_in")

    tk_mm, tk_ok, lg_mm, gx_ok, sel2_ok = (sem(n) for n in ("tk_mm", "tk_ok", "lg_mm", "gx_ok", "sel2_ok"))
    rt_in, rank_mm, blocks_ok = sem("rt_in"), sem("rank_mm"), sem("blocks_ok")
    pick_ok, xg_mm, xg_ok, gt_mm, gt_ok = (sem(n) for n in ("pick_ok", "xg_mm", "xg_ok", "gt_mm", "gt_ok"))
    y_ok, yt_mm, ye_ok, sc_mm, sc_ok = (sem(n) for n in ("y_ok", "yt_mm", "ye_ok", "sc_mm", "sc_ok"))
    fin_ok = sem("fin_ok")

    plan = Plan()

    def add_cols(name, w, cols, freed_by, value):
        n = sum(c for _, c in cols)
        pieces, at = [], 0
        for c0, c in cols:
            def dst(s, at=at, c=c, n=n):
                return s[:, 0:KC * n].rearrange("p (k n) -> p k n", k=KC)[:, :, at:at + c]
            pieces.append((dst, w[:, c0:c0 + c].rearrange("(k p) n -> p k n", p=P)))
            at += c
        plan.add(name, pieces, freed_by, value)

    w_in = I["w_in_even"][0]
    IN_JOBS = [("k", [(K0, 128)]), ("ik", [(IK0, 64), (IK0, 64)]), ("iq0", [(IQ0, 128)]), ("iq1", [(IQ0 + 128, 128)])]
    IN_JOBS += [(f"q{j}", [(Q0 + 64 * j, 64), (Q0 + 64 * (j + 4), 64)]) for j in range(4)]
    IN_JOBS += [("v", [(V0, 128)])]
    IN_JOBS += [(f"{n}{j}", [(c0 + 128 * j, 128)]) for n, c0 in (("cc", CC0), ("ch", CH0), ("cb", CB0)) for j in range(4)]
    NIN = len(IN_JOBS)
    N_ATT = 9
    for j, (n, cols) in enumerate(IN_JOBS):
        if j == N_ATT:
            add_cols("iw", w_in, [(IW0, NIH)], iw_mm, 1)
        add_cols(n, w_in, cols, job_mm, j + 1)
    w_out = I["w_out_even"][0]
    for c in range(KC):
        def slot3(s):
            return s[:, :].rearrange("p (k n) -> p k n", k=KC)
        cols = w_out[:, c * P:(c + 1) * P]
        plan.add(f"wo{c}", [
            (lambda s: slot3(s)[0:HD, 0:4, :], cols[0:256].rearrange("(j p) n -> p j n", p=HD)),
            (lambda s: slot3(s)[HD:P, 0:4, :], cols[256:512].rearrange("(j p) n -> p j n", p=HD)),
            (lambda s: slot3(s)[:, 4:8, :], cols[512:1024].rearrange("(j p) n -> p j n", p=P)),
        ], om_mm, c + 1)
    gate0, up0, down0 = I["ffn_gate"][0], I["ffn_up"][0], I["ffn_down"][0]

    def slot4(s):
        return s[:, :].rearrange("p (k n) -> p k n", k=4)

    for q in range(FC // 2):
        for w in (gate0, up0):
            for half in range(2):
                src = w[512 * half:512 * half + 512, 256 * q:256 * q + 256].rearrange("(k p) n -> p k n", p=P)
                plan.add(f"gu{q}", [(slot4, src)], gu_mm, 2 * q + 2)
    for half in range(2):
        for f2 in range(FC // 2):
            src = down0[256 * f2:256 * f2 + 256, 512 * half:512 * half + 512].rearrange("(k p) n -> p k n", p=P)
            plan.add(f"dn{half}_{f2}", [(lambda s: s[:, :].rearrange("p (k n) -> p k n", k=2), src)],
                     down_mm, half * (FC // 2) + f2 + 1)

    for n, w1_, w2_, i in (("w", "rwkv_w1", "rwkv_w2", 0), ("a", "rwkv_a1", "rwkv_a2", 1), ("g", "rwkv_g1", "rwkv_g2", 2)):
        add_cols(n + "1", I[w1_][0], [(0, I[w1_].shape[2])], lh_mm, i + 1)
    for n, w2_, i in (("w", "rwkv_w2", 0), ("a", "rwkv_a2", 1), ("g", "rwkv_g2", 2)):
        plan.add(n + "2", [(lambda s, r=I[w2_].shape[1]: s[0:r, :], I[w2_][0])], job_mm, NIN + KC * (i + 1))
    for i, m in enumerate((1, 0, 2)):
        for c in range(KC):
            add_cols(f"krv{m}{c}", I["rwkv_w_rkv"][0, m], [(c * P, P)], job_mm, NIN + 24 + KC * i + c + 1)
    for c in range(KC):
        add_cols(f"ro{c}", I["rwkv_w_o"][0], [(c * P, P)], om_mm, KC + c + 1)
    dtmp = sbt("dtmp", [P, HD - POOL_ROWS, HD], at=starts[f"ring{len(plan.items) % RING}"])
    landed, _sum = [], [0] * RING
    for n, it in enumerate(plan.items):
        _sum[n % RING] += 16 * len(it[1])
        landed.append(_sum[n % RING])
    USES = 3 * FC // 2

    def weights(pe, n):
        pe.wait_ge(slot_in[n % RING], landed[n])
        return ring[n % RING]

    def chained(eng, s):
        count = [0]

        def link(ins):
            count[0] += 1
            ins.then_inc(s, 1)
            eng.wait_ge(s, count[0])
        return link

    mm = nc.tensor.matmul

    def rms_act(act, n, src, square):
        for c in range(KC):
            nc.scalar.activation(square[:, c], src[:, c], ACT.Square).then_inc(sq_ok, 1)
        act.wait_ge(ms_ok, n + 1)
        nc.scalar.activation(rs[:], ms[:], ACT.Sqrt).then_inc(sd_ok, 1)

    def rms_pe(pe, n, square):
        for c in range(KC):
            pe.wait_ge(sq_ok, KC * n + c + 1)
            last = mm(bk[0][:, 0:T], C["ones"], square[:, c], start=c == 0, stop=c == KC - 1)
        last.then_inc(ssq_mm, 1)

    def rms_dve(dve, link, n, src, gain, dst):
        dve.wait_ge(ssq_mm, n + 1)
        nc.vector.tensor_scalar(ms[:], bk[0][:, 0:T], 1.0 / D, EPS, ALU.mult, ALU.add).then_inc(ms_ok, 1)
        dve.wait_ge(sd_ok, n + 1)
        link(nc.vector.reciprocal(rs[:], rs[:]))
        for c in range(KC):
            nc.vector.scalar_tensor_tensor(dst[:, c], src[:, c], vecT[:, gain + c:gain + c + 1], rs[:],
                                           ALU.mult, ALU.mult).then_inc(xn_ok, 1)

    block = ctx.enter_context(nc.Block())

    def load_page(eng, b, g, table, dst, landed):
        page = eng.value_load(pg_ids[0:1, bass.ds(g + NPG * b, 1)], min_val=0, max_val=N_POOL - 1)
        src = I[table][0, bass.ds(page, 1)].rearrange("o p g d -> p (o g d)" if table != "cache_idx_k" else
                                                      "o p d -> p (o d)")
        eng.dma_start(dst.rearrange("p o d -> p (o d)"), src).then_inc(landed, 16)

    @block.sync
    def _(sp):
        sp.dma_start(x_rows[:, 0:2, :], I["x_prompt"][0].rearrange("(i p) d -> p i d", p=P)).then_inc(head_in, 16)
        sp.dma_start(x_rows[0:NS, 2, :], I["x_sample"].rearrange("b t d -> (b t) d")).then_inc(head_in, 16)
        sp.dma_start(cst[:], I["consts"]).then_inc(head_in, 16)

        def vec_load(row, src):
            r, n = row % P, src.shape[0]
            sp.dma_start(vec_rows[r:r + n, row // P, :], src).then_inc(head_in, 16)

        for n in VEC_NAMES:
            a = I["rwkv_mu" if n == "mu" else n][0]
            if n == "mu":
                vec_load(VEC[n], a.rearrange("m (c p) -> (m c) p", p=P))
            elif n == "rwkv_r_k":
                vec_load(VEC[n], a.rearrange("(c h) k -> c (h k)", h=2))
            else:
                vec_load(VEC[n], a.rearrange("(c p) -> c p", p=P))
        vec_load(VEC["rwkv_ln_b"], I["rwkv_ln_b"][0].rearrange("(c p) -> c p", p=P))
        vec_load(VEC["conv_w"], I["conv_w"][0].rearrange("j (c p) -> (j c) p", p=P))
        vec_load(VEC["state_shift"], I["state_shift"][0].rearrange("b (c p) -> (b c) p", p=P))
        vec_load(VEC["state_conv"], I["state_conv"][0].rearrange("b j (c p) -> (b j c) p", p=P))
        sp.wait_ge(ids_in, 16)

        def load_pages(b):
            if b >= 2:
                sp.wait_ge(kT_mm, b - 1)
            with sp.Fori(0, SP_PAGES) as g:
                load_page(sp, b, g, "cache_k", k_pages[:, b % 2, bass.ds(g, 1)], page_in[b % 2])
            if b >= 2:
                sp.wait_ge(ikT_mm, b - 1)
            with sp.Fori(0, SP_IK_PAGES) as g:
                load_page(sp, b, g, "cache_idx_k", ik_pages[:, b % 2, bass.ds(g, 1)], page_in[b % 2])

        def load_values(b):
            with sp.Fori(0, NPG) as g:
                load_page(sp, b, g, "cache_v", v_pages[b][:, bass.ds(g, 1)], vpage_in[b // 4])

        for n, (name, pieces, freed_by, value) in enumerate(plan.items):
            if n == RING:
                load_pages(0)
                load_pages(1)
            if n == N_ATT + 1 + RING:
                for b in range(2, NB):
                    load_pages(b)
                load_values(0)
                load_values(1)
            if n == len(IN_JOBS) + 1:
                sp.wait_ge(qk_mm, NB)
                sp.wait_ge(idx_mm, NB)
                load_values(2)
                load_values(3)
            if n == len(IN_JOBS) + 1 + KC:
                sp.wait_ge(isum_mm, 1)
                load_values(4)
                load_values(5)
                sp.wait_ge(ppT_mm, 6)
                load_values(6)
                load_values(7)
            if n >= RING:
                old = plan.items[n - RING]
                sp.wait_ge(old[2], old[3])
            for view, src in pieces:
                sp.dma_start(view(ring[n % RING]), src).then_inc(slot_in[n % RING], 16)

        for q in range(6):
            sp.wait_ge(st_ok, q + 1)
            sp.dma_start(q6_dram[:, q], st[:, q]).then_inc(st_out, 16)
        sp.wait_ge(st_out, 16 * 6)
        for b in range(NB):
            sp.dma_start(s6[RH * b:RH * b + RH].rearrange("p t q d -> p (t q) d"), q6_dram[TS * b:TS * b + TS].rearrange(
                "t q (h d) -> h (t q) d", h=RH)).then_inc(s6_in, 16)
        sp.dma_start(S[:].rearrange("p v k -> p (v k)"),
                     I["state_wkv"][0].rearrange("b h v k -> (b h) (v k)")).then_inc(s6_in, 16)
        sp.wait_ge(ys_ok, 2)
        for b in range(NB):
            sp.dma_start(ys_dram[b].rearrange("t h v -> h t v"), ys[RH * b:RH * b + RH]).then_inc(temp_out, 16)
        sp.wait_ge(temp_out, 64 + 16 * NB)
        sp.dma_start(y_rows[0:NS, 2], ys_dram.rearrange("b t h v -> (b t) (h v)")).then_inc(yrow_in, 16)
        sp.dma_start(O["wkv_sample"][0].rearrange("b h v k -> (b h) (v k)"),
                     S[:].rearrange("p v k -> p (v k)")).then_inc(out_done, 16)
        sp.wait_ge(yo_mm, NCH)
        sp.dma_start(bonT[:], bon_dram).then_inc(bonT_in, 16)
        sp.wait_ge(om_mm, KC + KC)
        sp.dma_start(w_rt[:], I["moe_router"][0].rearrange("(k p) e -> p k e", p=P)).then_inc(rt_in, 16)
        sp.dma_start(gain_f[:], I["norm_final"].partition_broadcast(P)).then_inc(rt_in, 16)

        sp.wait_ge(out_done, 16 * (OUT_1 + 2))

        def expert_load(it, e):
            for u in range(USES):
                if u < RING:
                    sp.wait_ge(down_mm, FC * it + 2 * u + 2)
                elif u - RING < FC:
                    sp.wait_ge(gu_mm, FC + FC * it + 2 * ((u - RING) // 2) + 2)
                else:
                    sp.wait_ge(down_mm, FC + FC * it + 2 * (u - RING - FC) + 2)
                for half, part in enumerate((ring, ring2)):
                    if u < FC:
                        q, m = u // 2, u % 2
                        w = I["moe_gate" if m == 0 else "moe_up"][0, bass.ds(e, 1)].rearrange("o d f -> (o d) f")
                        src = w[512 * half:512 * half + 512, 256 * q:256 * q + 256].rearrange("(k p) n -> p k n", p=P)
                        dst = slot4(part[u % RING])
                    else:
                        f = 2 * (u - FC) + half
                        src = I["moe_down"][0, bass.ds(e, 1)].rearrange("o f d -> (o f) d")[f * P:(f + 1) * P, :]
                        dst = part[u % RING][:, :]
                    sp.dma_start(dst, src).then_inc(slot_in[u % RING], 16)

        sp.wait_ge(blocks_ok, 1)
        n_blocks = sp.value_load(blocks[0:1, 0:1], min_val=1, max_val=T // CAP)
        with sp.Fori(0, n_blocks) as blk:
            with sp.Fori(0, NE) as e:
                expert_load(blk * NE + e, e)
        sp.wait_ge(fin_ok, 3)
        sp.dma_start(O["y_prompt"][0].rearrange("(i p) d -> p i d", p=P), y_out[:, 0:2, :]).then_inc(out_done, 16)
        sp.dma_start(O["y_sample"].rearrange("b t d -> (b t) d"), y_out[0:NS, 2, :]).then_inc(out_done, 16)
        sp.wait_ge(out_done, 16 * N_OUT)

    @block.tensor
    def _(pe):
        def project(pe, weights_n, rhs, out):
            w = weights(pe, weights_n)[:, :].rearrange("p (k n) -> p k n", k=KC)
            for k in range(KC):
                last = mm(out, w[:, k], rhs[:, k], start=k == 0, stop=k == KC - 1)
            return last

        pe.wait_ge(head_in, HEAD)
        nc.tensor.transpose(bk[0][:, 0:P], vec_rows[:, 0, :], C["ident"])
        nc.tensor.transpose(bk[0][:, P:P + 84], vec_rows[0:84, 1, :], C["ident"][0:84, 0:84])
        nc.tensor.transpose(bk[0][:, 2 * P:2 * P + 64], vec_rows[0:64, 2, :],
                            C["ident"][0:64, 0:64]).then_inc(vec_mm, 1)
        for c in range(KC):
            if c >= 4:
                pe.wait_ge(xT_ok, c - 3)
            for i, (t0, tn) in enumerate(TILES):
                last = nc.tensor.transpose(bk[1 + c % 4][:, t0:t0 + tn], x_rows[0:tn, i, c * P:(c + 1) * P],
                                           C["ident"][0:tn, 0:tn])
            last.then_inc(xT_mm, 1)
        pe.wait_ge(vec_ok, 1)
        rms_pe(pe, 0, sq)

        pe.wait_ge(xn_ok, KC)

        def in_job(j):
            if j >= 4:
                pe.wait_ge(job_ok, j - 3)
            n = j if j < N_ATT else j + 1
            project(pe, n, xn, bk[1 + j % 4][:, 0:T]).then_inc(job_mm, 1)

        for j in range(N_ATT):
            in_job(j)
        w = weights(pe, N_ATT)[:, 0:KC * NIH].rearrange("p (k n) -> p k n", k=KC)
        for i, (t0, tn) in enumerate(TILES):
            for k in range(KC):
                last = mm(bk[5][0:tn, 8 * i:8 * i + NIH], xn[:, k, t0:t0 + tn], w[:, k],
                          start=k == 0, stop=k == KC - 1)
        last.then_inc(iw_mm, 1)
        for j in range(8):
            pe.wait_ge(job_ok, j + 1)
            if j >= 2:
                pe.wait_ge(rope_ok, j - 1)
            mm(bk[6 + j % 2][:, 0:T], C["rot"], raw[:, j], start=True, stop=True).then_inc(rot_mm, 1)
        pe.wait_ge(job_ok, 9)
        for i, (t0, tn) in enumerate(TILES):
            for m, src in enumerate((rp[:, 0], raw[:, 8], rp[:, 1])):
                pe.wait_ge(rope_ok, 2)
                last = nc.tensor.transpose(bk[i][0:tn, m * P:(m + 1) * P], src[:, t0:t0 + tn], C["ident"])
        last.then_inc(turn_mm, 1)
        for i in range(2):
            pe.wait_ge(rope_ok, 4)
            for h in range(NIH):
                pe.wait_ge(rope_ok, 8)
                pe.wait_ge(turn_ok, 1)
                if i == 1:
                    pe.wait_ge(ip_ok, h + 1)
                a = HD * (h % 2)
                mm(bk[h][:, 0:TP], rp[a:a + HD, 2 + h // 2, i * P:(i + 1) * P], rp[a:a + HD, 1, 0:TP],
                   start=True, stop=True).then_inc(ip_mm, 1)
        pe.wait_ge(ip_ok, 2 * NIH)
        for b in range(NB):
            pe.wait_ge(page_in[b % 2], 16 * (NPG + SP_IK_PAGES) * (b // 2 + 1))
            if b >= 1:
                pe.wait_ge(ikT_ok, b)
            for g in range(NPG):
                last = nc.tensor.transpose(bk[g // 4][:, (g % 4) * P:(g % 4 + 1) * P], k_pages[:, b % 2, g], C["ident"])
            last.then_inc(kT_mm, 1)
            pe.wait_ge(kT_ok, b + 1)
            pe.wait_ge(new_ok, 2 * b + 1)
            pe.wait_ge(qs_ok, 4)
            if b >= 1:
                pe.wait_ge(qk_ok, b)
            else:
                pe.wait_ge(iw_ok, 1)
            a = 32 * (b % 4)
            mm(bk[4][a:a + 32, :], q_s[:, b], keysT[:, 0:512], start=True, stop=True)
            mm(bk[5][a:a + 32, :], q_s[:, b], keysT[:, 512:1024], start=True, stop=True)
            mm(bk[3][a:a + 32, 0:TS], q_s[:, b], keysT[:, 1024:NK], start=True, stop=True).then_inc(qk_mm, 1)
            pe.wait_ge(ik_page_in[b % 2], 16 * (NPG - SP_IK_PAGES) * (b // 2 + 1))
            for g in range(NPG // 2):
                last = nc.tensor.transpose(bk[0][:, g * P:(g + 1) * P],
                                           ik_pages[:, b % 2, 2 * g:2 * g + 2].rearrange("p a d -> p (a d)"), C["ident"])
            last.then_inc(ikT_mm, 1)
            pe.wait_ge(ikT_ok, b + 1)
            pe.wait_ge(new_ok, 2 * b + 2)
            if b >= 1:
                pe.wait_ge(idx_ok, b)
            mm(bk[6][a:a + 32, :], iq_s[0:HD, b], ikeysT[0:HD, 0:512], start=True, stop=True)
            mm(bk[7][a:a + 32, :], iq_s[HD:P, b], ikeysT[HD:P, 0:512], start=True, stop=True)
            mm(bk[2][a:a + 32, 0:TS], iq_s[0:HD, b], ikeysT[0:HD, 512:512 + TS], start=True, stop=True).then_inc(idx_mm, 1)
        pe.wait_ge(idx_ok, NB)
        for cols, o in (((0, 512), 6), ((512, 1024), 7), ((1024, NK), 2)):
            for g in range(2):
                last = mm(bk[o][0:NS, 0:cols[1] - cols[0]], C["sel_sum"][:, g * NS:(g + 1) * NS],
                          idx_s[:, g, cols[0]:cols[1]], start=g == 0, stop=g == 1)
        last.then_inc(isum_mm, 1)
        pe.wait_ge(qk_ok, NB)
        pe.wait_ge(sel_ok, 1)
        for i in range(2):
            n = P * (i + 1)
            for j in range(4):
                for g in range(2):
                    o = NQ * i + 2 * j + g
                    if o >= 4:
                        pe.wait_ge(sp_ok, o - 3)
                    a = HD * g
                    mm(bk[o % 4][:, 0:n], rp[a:a + HD, 4 + j, i * P:(i + 1) * P], rp[a:a + HD, 0, 0:n],
                       start=True, stop=True).then_inc(sp_mm, 1)
        pe.wait_ge(sp_ok, 2 * NQ)
        for j in range(N_ATT, len(IN_JOBS)):
            in_job(j)
        for o in range(2):
            pe.wait_ge(pp_ok, o + 1)
            pe.wait_ge(job_ok, len(IN_JOBS))
            for s in range(o + 1):
                for h in range(NQ):
                    n = 8 * (o + s) + h
                    if n % 4 == 0 and n >= 16:
                        pe.wait_ge(ppT_ok, n // 4 - 3)
                    last = nc.tensor.transpose(bk[(n // 4) % 4][:, (n % 4) * P:(n % 4 + 1) * P],
                                               probs[:, o, h, s * P:(s + 1) * P], C["ident"])
                    if n % 4 == 3:
                        last.then_inc(ppT_mm, 1)
        pe.wait_ge(ppT_ok, 6)
        for o in range(2):
            for j in range(4):
                for g in range(2):
                    for s in range(o + 1):
                        last = mm(bk[4 + j][HD * g:HD * g + HD, o * P:(o + 1) * P], rows[:, s, 1, HD * g:HD * g + HD],
                                  probsT[:, o + s, 2 * j + g], start=s == 0, stop=s == o)
                if o == 1:
                    last.then_inc(pvp_mm, 1)
        pe.wait_ge(conv_ok, 1)
        for c in range(4):
            last = nc.tensor.transpose(bk[0][0:2 + 2 * NB, c * P:(c + 1) * P], u_last[:, c], C["ident"])
        last.then_inc(turn_mm, 1)
        n0 = len(IN_JOBS) + 1
        pe.wait_ge(pvp_ok, 4)
        for ks in ((0, 1, 2, 3), (4,), (5,), (6,), (7,)):
            if ks[0] >= 4:
                pe.wait_ge(conv_ok, 1 + ks[0] - 3)
            for c in range(KC):
                w = weights(pe, n0 + c)[:, :].rearrange("p (k n) -> p k n", k=KC)
                for k in ks:
                    last = nc.tensor.matmul(bk[4 + c // 2][:, TP * (c % 2):TP * (c % 2) + TP], w[:, k], mixT[:, k, 0:TP],
                                            start=k == 0 and c % 2 == 0, stop=k == KC - 1, skip_group_check=True)
        last.then_inc(omp_mm, 1)
        pe.wait_ge(sel_ok, 3)
        for g in range(2):
            banks = (1, 2, 3)
            if g == 1:
                pe.wait_ge(att_ok, 1)
            for o, (c0, c1) in zip(banks, ((0, 512), (512, 1024), (1024, NK))):
                last = mm(bk[o][:, 0:c1 - c0], C["sel_spread"][0:NS, g * P:(g + 1) * P], sc_s[:, c0:c1],
                          start=True, stop=True)
            last.then_inc(spread_mm, 1)
        pe.wait_ge(omp_ok, 1)
        for g in range(2):
            pe.wait_ge(ps_ok, g + 1)
            if g == 1:
                pe.wait_ge(psT_ok, 1)
            for n in range(9):
                o = 4 + n // 4
                w_ = P if n < 8 else TS
                last = nc.tensor.transpose(bk[o][0:w_, (n % 4) * P:(n % 4 + 1) * P], att_s[:, g, n * P:n * P + w_],
                                           C["ident"])
            last.then_inc(psT_mm, 1)
            pe.wait_ge(psT_ok, g + 1)
            pe.wait_ge(vnew_in, 16)
            for b in range(4 * g, 4 * g + 4):
                pe.wait_ge(vpage_in[g], 16 * NPG * 4)
                for n in range(9):
                    k = P if n < 8 else TS
                    lhs = v_pages[b][:, n] if n < 8 else v_new[:, b]
                    last = mm(bk[7][:, 32 * b:32 * b + 32], lhs, pS_T[0:k, n, 32 * (b % 4):32 * (b % 4) + 32],
                              start=n == 0, stop=n == 8)
                last.then_inc(pvs_mm, 1)
        pe.wait_ge(pvs_ok, 1)
        for c in range(KC):
            project(pe, n0 + c, mixT[:, :, TP:T], bk[1][:, NS * c:NS * c + NS]).then_inc(om_mm, 1)
        rms_pe(pe, 1, sq1)
        pe.wait_ge(xn_ok, 2 * KC)
        n0 += KC
        for q in range(FC // 2):
            slots = [weights(pe, n0 + 4 * q + i)[:, :].rearrange("p (k n) -> p k n", k=4) for i in range(4)]
            for f in (2 * q, 2 * q + 1):
                if f >= 2:
                    pe.wait_ge(hid_ok, f - 1)
                for m in range(2):
                    for k in range(KC):
                        last = mm(bk[2 * m + f % 2][:, 0:T], slots[2 * m + k // 4][:, k % 4, (f % 2) * P:(f % 2 + 1) * P],
                                  xn1[:, k], start=k == 0, stop=k == KC - 1)
                last.then_inc(gu_mm, 1)
        n0 += 2 * FC
        for half in range(2):
            banks = (4, 5, 6, 7) if half == 0 else (0, 1, 2, 3)
            for f in range(FC):
                if f % 2 == 0:
                    w = weights(pe, n0 + half * (FC // 2) + f // 2)[:, :].rearrange("p (k n) -> p k n", k=2)
                pe.wait_ge(hid_ok, FC if half else f + 1)
                for c in range(4):
                    last = mm(bk[banks[c]][:, 0:T], w[:, f % 2, c * P:(c + 1) * P], hid[:, f],
                              start=f == 0, stop=f == FC - 1)
                if f % 2 == 1:
                    last.then_inc(down_mm, 1)
        n0 += FC

        pe.wait_ge(down_ok, 8)
        rms_pe(pe, 2, sq2)
        h_in = [(0, HD), (1, HD), (2, P)]
        for i, r in h_in:
            pe.wait_ge(mix_ok, KC * (i + 1))
            w = weights(pe, n0 + i)[:, 0:KC * r].rearrange("p (k n) -> p k n", k=KC)
            for k in range(KC):
                last = mm(bk[5 + i][0:r, 0:T], w[:, k], mx[:, i % 2, k], start=k == 0, stop=k == KC - 1)
            last.then_inc(lh_mm, 1)
        n0 += 3
        for j in range(48):
            i, c = j // KC, j % KC
            if j >= 4:
                pe.wait_ge(job_ok, NIN + j - 3)
            out = bk[1 + j % 4][:, 0:T]
            if i < 3:
                pe.wait_ge(lh_ok, i + 1)
                r = h_in[i][1]
                w = weights(pe, n0 + i)
                mm(out, w[0:r, c * P:(c + 1) * P], lh[0:r, i], start=True, stop=True).then_inc(job_mm, 1)
            else:
                pe.wait_ge(mix_ok, KC * (i + 1))
                project(pe, n0 + 3 + j - 24, mx[:, i % 2], out).then_inc(job_mm, 1)
            if j == 26:
                pe.wait_ge(el_ok, 2)
                for c in range(KC):
                    last = nc.tensor.transpose(bk[5 + c // 4][0:1 + NB, (c % 4) * P:(c % 4 + 1) * P], e_last[:, c],
                                               C["ident"])
                last.then_inc(turn_mm, 1)
            if j in (35, 37):
                half = (j - 35) // 2
                pe.wait_ge(turn_ok, 3)
                pe.wait_ge(sqk_ok, 1)
                if half:
                    pe.wait_ge(nk_ok, 1)
                for c in range(4):
                    last = mm(bk[(0, 5, 6, 7)[c]][:, 0:T], C["headones"], t2[:, 4 * half + c], start=True, stop=True)
                last.then_inc(hs_mm, 1)
        n0 += 3 + 24
        pe.wait_ge(job_ok, NIN + 48)
        pe.wait_ge(nk_ok, 2)
        pe.wait_ge(rk_ok, 1)
        for c in range(KC):
            last = mm(bk[c][:, 0:T], C["headones"], t2[:, c], start=True, stop=True)
        last.then_inc(hs_mm, 1)
        pe.wait_ge(bn_ok, 1)
        pe.wait_ge(e_ok, 3)
        pe.wait_ge(arbk_ok, 1)
        for q, src in enumerate((rT, lwT, kT, vT, t1, aT)):
            if q >= 4:
                pe.wait_ge(st_ok, q - 3)
            for c in range(KC):
                last = nc.tensor.transpose(bk[2 * (q % 4) + c // 4][0:NS, (c % 4) * P:(c % 4 + 1) * P],
                                           src[:, c, TP:T], C["ident"])
            last.then_inc(st_mm, 1)
        pe.wait_ge(st_ok, 6)
        for p2 in range(2):
            if p2:
                pe.wait_ge(yo_ok, 2)
                pe.wait_ge(s_ok, 2)
            for c in range(KC):
                last = nc.tensor.transpose(bk[c // 4][:, (c % 4) * P:(c % 4 + 1) * P], vT[:, c, P * p2:P * (p2 + 1)],
                                           C["ident"])
            last.then_inc(vt_mm, 1)
            for gi in range(8):
                cc, par, half = gi // 4, gi // 2 % 2, gi % 2
                if gi < 2:
                    pe.wait_ge(vt_ok, p2 + 1)
                r = slice(HD * par, HD * par + HD)
                for i in range(4):
                    hp = 4 * half + i
                    last = mm(bk[gi][:, i * P:(i + 1) * P],
                              BK[r, hp, 2 * p2 + cc].rearrange("p a t -> p (a t)"),
                              AR[r, hp, 2 * p2 + cc].rearrange("p a t -> p (a t)"), start=True, stop=True)
                last.then_inc(g_mm, 1)
            pe.wait_ge(g_ok, 8 * (p2 + 1))
            for cc in range(2):
                for par in range(2):
                    r = slice(HD * par, HD * par + HD)
                    for hp in range(KC):
                        last = mm(bk[4 + 2 * cc + par][CH * cc:CH * cc + CH, hp * CH:(hp + 1) * CH],
                                  AR[r, hp, 2 * p2 + cc, 0], BK[r, hp, 2 * p2 + cc, 0], start=True, stop=True)
            last.then_inc(l_mm, 1)
            def each(fn, first, cc):
                r = slice(CH * cc, CH * cc + CH)
                for par in range(2):
                    for hp in range(KC):
                        lhs, rhs = fn(r, par, hp)
                        last = mm(bk[first + 2 * cc + par][r, hp * CH:(hp + 1) * CH], lhs, rhs, start=True, stop=True)
                return last

            pe.wait_ge(c_ok, 6 * p2 + 1)
            for cc in range(2):
                each(lambda r, par, hp: (Cj[r, par, hp], C["ident64"][r]), 0, cc).then_inc(m_mm, 1)
            for j in range(1, 6):
                pe.wait_ge(c_ok, 6 * p2 + j + 1)
                for cc in range(2):
                    pe.wait_ge(xy_ok, 12 * p2 + 2 * (j - 1) + cc + 1)
                    each(lambda r, par, hp: (Cj[r, par, hp], Y[r, par, hp]), 0, cc).then_inc(m_mm, 1)
                for cc in range(2):
                    pe.wait_ge(m_ok, 10 * p2 + 2 * (j - 1) + cc + 1)
                    each(lambda r, par, hp: (X[r, par, hp], M[r, par, hp]), 4, cc).then_inc(y_mm, 1)
                    if j < 5:
                        each(lambda r, par, hp: (M[r, par, hp], X[r, par, hp]), 0, cc).then_inc(x_mm, 1)
            pe.wait_ge(m_ok, 10 * (p2 + 1))
            for cc in range(2):
                for hp in range(KC):
                    last = nc.tensor.transpose(bk[2 * cc + hp // 4][:, (hp % 4) * P:(hp % 4 + 1) * P],
                                               BK[:, hp, 2 * p2 + cc].rearrange("p a t -> p (a t)"), C["ident"])
            last.then_inc(bt_mm, 1)
            pe.wait_ge(xy_ok, 12 * (p2 + 1))
            for cc in range(2):
                r = slice(CH * cc, CH * cc + CH)
                for par in range(2):
                    for hp in range(KC):
                        last = mm(bk[4 + 2 * cc + par][r, hp * CH:(hp + 1) * CH], G[CH:P, cc, par, hp, 0:CH],
                                  Z[CH:P, cc, hp, par], start=True, stop=True)
            last.then_inc(w1_mm, 1)
            pe.wait_ge(bt_ok, p2 + 1)
            pe.wait_ge(w1_ok, p2 + 1)
            for cc in range(2):
                c = 2 * p2 + cc
                r = slice(CH * cc, CH * cc + CH)
                if c:
                    pe.wait_ge(s_ok, c)
                    pe.wait_ge(yo_ok, c)
                    for par in range(2):
                        for hp in range(KC):
                            q = slice(HD * par, HD * par + HD)
                            last = mm(bk[par][r, hp * CH:(hp + 1) * CH], AR[q, hp, c, 0], ST[q, hp],
                                      start=True, stop=True)
                    last.then_inc(w2_mm, 1)
                    pe.wait_ge(w_ok, c)
                for par in range(2):
                    for hp in range(KC):
                        last = mm(bk[2 + par][0:CH, hp * CH:(hp + 1) * CH], Y[r, par, hp], X[r, par, hp],
                                  start=True, stop=True)
                last.then_inc(u_mm, 1)
                pe.wait_ge(u_ok, c + 1)
                for hp in range(KC):
                    for par in range(2):
                        last = mm(bk[6][HD * par:HD * par + HD, hp * CH:(hp + 1) * CH],
                                  BKt[:, cc, hp, HD * par:HD * par + HD], Z[:, cc, hp, par], start=True, stop=True)
                last.then_inc(s_mm, 1)
                for par in range(2):
                    for hp in range(KC):
                        q = slice(HD * par, HD * par + HD)
                        out = bk[4 + par][r, hp * CH:(hp + 1) * CH]
                        last = mm(out, G[:, cc, par, hp, CH:P], Z[:, cc, hp, par], start=True, stop=c == 0)
                        if c:
                            last = mm(out, AR[q, hp, c, 1], ST[q, hp], start=False, stop=True)
                last.then_inc(yo_mm, 1)
        pe.wait_ge(s_ok, NCH)
        for hp in range(KC):
            last = nc.tensor.transpose(bk[hp // 4][0:HD, (hp % 4) * P:(hp % 4 + 1) * P], ST[:, hp], C["ident"])
        last.then_inc(turn_mm, 1)
        pe.wait_ge(gn_ok, 3)
        pe.wait_ge(turn_ok, 4)
        for c in range(KC):
            if c >= 4:
                pe.wait_ge(oT_ok, c - 3)
            for i, (t0, tn) in enumerate(TILES):
                last = nc.tensor.transpose(bk[2 + c % 4][:, t0:t0 + tn], y_rows[0:tn, i, c * P:(c + 1) * P],
                                           C["ident"][0:tn, 0:tn])
            last.then_inc(yT_mm, 1)
        pe.wait_ge(oT_ok, KC)
        for c in range(KC):
            if c >= 4:
                pe.wait_ge(om_ok, KC + c - 3)
            project(pe, n0 + c, oT, bk[2 + c % 4][:, 0:T]).then_inc(om_mm, 1)
        n0 += KC

        pe.wait_ge(om_ok, KC + KC)
        rms_pe(pe, 3, sq3)
        pe.wait_ge(xn_ok, 4 * KC)
        pe.wait_ge(rt_in, 32)
        for i, (t0, tn) in enumerate(TILES):
            for k in range(KC):
                last = mm(bk[1][0:tn, NE * i:NE * i + NE], xn3[:, k, t0:t0 + tn], w_rt[:, k], start=k == 0, stop=k == KC - 1)
        last.then_inc(lg_mm, 1)
        for m in range(12):
            src, i, half = (xn3, xT)[m // 6], m // 2 % 3, m % 2
            t0, tn = TILES[i]
            if m >= 4:
                pe.wait_ge(tk_ok, m - 3)
            for c in range(4):
                last = nc.tensor.transpose(bk[4 + m % 4][0:tn, c * P:(c + 1) * P], src[:, 4 * half + c, t0:t0 + tn],
                                           C["ident"])
            last.then_inc(tk_mm, 1)
        pe.wait_ge(sel2_ok, 1)
        for i, (t0, tn) in enumerate(TILES):
            for j in range(i + 1):
                jn = TILES[j][1]
                last = mm(bk[2][0:tn, NE * i:NE * i + NE], C["before" if j == i else "ones"][0:jn, 0:tn], sel[0:jn, j],
                          start=j == 0, stop=j == i)
        for j in range(3):
            jn = TILES[j][1]
            last = mm(bk[2][0:1, 4 * NE:5 * NE], C["ones"][0:jn, 0:1], sel[0:jn, j], start=j == 0, stop=j == 2)
        last.then_inc(rank_mm, 1)

        def gather():
            for c in range(KC):
                for i, (t0, tn) in enumerate(TILES):
                    last = mm(bk[6 + c // 4][:, (c % 4) * CAP:(c % 4 + 1) * CAP], xr[0:tn, i, c * P:(c + 1) * P],
                              pick[0:tn, i], start=i == 0, stop=i == 2)
            last.then_inc(xg_mm, 1)

        pe.wait_ge(tk_ok, 12)
        pe.wait_ge(pick_ok, 1)
        gather()

        def slot(it, u):
            pe.wait_ge(slot_in[u % RING], it * (32 * USES // RING) + _sum[u % RING] + 32 * (u // RING + 1))
            return ring[u % RING], ring2[u % RING]

        def turn_y(it):
            pe.wait_ge(y_ok, it + 1)
            pe.wait_ge(gt_ok, it + 1)
            for c in range(KC):
                last = nc.tensor.transpose(bk[4 + c // 4][0:CAP, (c % 4) * P:(c % 4 + 1) * P], yT[:, c], C["ident"])
            last.then_inc(yt_mm, 1)

        def scatter(it, g):
            if g == 0:
                pe.wait_ge(ye_ok, it + 1)
            if g >= 4:
                pe.wait_ge(sc_ok, 6 * it + 1 + g - 3)
            i, half = g // 2, g % 2
            t0, tn = TILES[i]
            mm(bk[(4, 5, 2, 3)[g % 4]][0:tn, :], giveT[:, t0:t0 + tn], ye[:, 512 * half:512 * half + 512],
               start=True, stop=True).then_inc(sc_mm, 1)

        def expert(it):
            pe.wait_ge(xg_ok, it + 1)
            pe.wait_ge(hid_ok, FC + FC * it)
            for q in range(FC // 2):
                w = [h[:, :].rearrange("p (k n) -> p k n", k=4) for m in range(2) for h in slot(it, 2 * q + m)]
                for f in (2 * q, 2 * q + 1):
                    if f >= 2:
                        pe.wait_ge(hid_ok, FC + FC * it + f - 1)
                    for m in range(2):
                        for k in range(KC):
                            last = mm(bk[f % 2][:, m * CAP:(m + 1) * CAP], w[2 * m + k // 4][:, k % 4, (f % 2) * P:(f % 2 + 1) * P],
                                      xg[:, k], start=k == 0, stop=k == KC - 1)
                    last.then_inc(gu_mm, 1)
                    if f == 2:
                        turn_y(it)
                    if 5 <= f < 11:
                        scatter(it, f - 5)
            pe.wait_ge(pick_ok, it + 2)
            gather()
            pe.wait_ge(sc_ok, 6 * it + 7)
            for i, (t0, tn) in enumerate(TILES):
                last = nc.tensor.transpose(bk[4][0:CAP, t0:t0 + tn], give[0:tn, i], C["ident"][0:tn, 0:tn])
            last.then_inc(gt_mm, 1)
            for f in range(FC):
                if f % 2 == 0:
                    w = slot(it, FC + f // 2)
                if f >= FC - 2:
                    pe.wait_ge(hid_ok, FC + FC * it + f + 1)
                elif f == 0:
                    pe.wait_ge(hid_ok, FC + FC * it + FC - 2)
                for c in range(KC):
                    last = mm(bk[2 + c // 4][:, (c % 4) * CAP:(c % 4 + 1) * CAP], w[f % 2][:, c * P:(c + 1) * P], hid2[:, f],
                              start=f == 0 and c % 4 == 0, stop=f == FC - 1, skip_group_check=True)
                last.then_inc(down_mm, 1)

        pe.wait_ge(blocks_ok, 1)
        n_blocks = pe.value_load(blocks[0:1, 0:1], min_val=1, max_val=T // CAP)
        with pe.Fori(0, n_blocks) as blk:
            with pe.Fori(0, NE) as e:
                expert(blk * NE + e)
        turn_y(n_blocks * NE)
        for g in range(6):
            scatter(n_blocks * NE, g)

    @block.scalar
    def _(act):
        def load_pages(b):
            with act.Fori(SP_PAGES, NPG) as g:
                load_page(act, b, g, "cache_k", k_pages[:, b % 2, bass.ds(g, 1)], page_in[b % 2])


        for c in range(KC):
            act.wait_ge(xT_mm, c + 1)
            nc.scalar.copy(xT[:, c], bk[1 + c % 4][:, 0:T]).then_inc(xT_ok, 1)
        act.wait_ge(xT_ok, KC)
        rms_act(act, 0, xT, sq)
        act.wait_ge(ids_in, 16)
        load_pages(0)
        load_pages(1)
        for j in range(N_ATT):
            act.wait_ge(job_mm, j + 1)
            nc.scalar.copy(raw[:, j], bk[1 + j % 4][:, 0:T]).then_inc(job_ok, 1)
        act.wait_ge(iw_mm, 1)
        for i, (t0, tn) in enumerate(TILES):
            last = nc.scalar.mul(iw[0:tn, i, :], bk[5][0:tn, 8 * i:8 * i + NIH], 1.0 / 16)
        last.then_inc(iw_ok, 1)
        act.wait_ge(turn_mm, 1)
        for i, (t0, tn) in enumerate(TILES):
            last = nc.scalar.copy(rows[0:tn, i].rearrange("p m d -> p (m d)"), bk[i][0:tn, 0:3 * P])
        last.then_inc(turn_ok, 1)
        act.wait_ge(iw_ok, 1)
        act.dma_start(iw_dram[:], iw[0:NS, 2, :]).then_inc(temp_out, 16)
        act.wait_ge(turn_ok, 1)
        for name, m, w_ in (("k", 0, P), ("v", 1, P), ("idx_k", 2, HD)):
            flat_p = O[name + "_prompt"][0, 0].rearrange("(i p) g d -> p i (g d)", p=P) if m < 2 \
                else O[name + "_prompt"][0, 0].rearrange("(i p) d -> p i d", p=P)
            flat_s = O[name + "_sample"][0].rearrange("b t g d -> (b t) (g d)") if m < 2 \
                else O[name + "_sample"][0].rearrange("b t d -> (b t) d")
            act.dma_start(flat_p, rows[:, 0:2, m, 0:w_]).then_inc(out_done, 16)
            if m == 1:
                act.dma_start(flat_s, rows[0:NS, 2, m, 0:w_]).then_inc(temp_out, 16)
            else:
                act.dma_start(flat_s, rows[0:NS, 2, m, 0:w_]).then_inc(out_done, 16)

        act.wait_ge(temp_out, 32)
        for b in range(NB):
            act.dma_start(iw_s[32 * (b % 4):32 * (b % 4) + 16, b // 4:b // 4 + 1],
                          iw_dram[TS * b:TS * b + TS, :].rearrange("t (h o) -> (t h) o", o=1)).then_inc(iws_in, 16)
        act.dma_start(v_new[:], O["v_sample"][0].rearrange("b t g d -> t b (g d)")).then_inc(vnew_in, 16)
        for b in range(NB):
            a, g = 32 * (b % 4), b // 4
            act.wait_ge(kT_mm, b + 1)
            if b >= 1:
                act.wait_ge(qk_mm, b)
            nc.scalar.copy(keysT[:, 0:512], bk[0][:])
            nc.scalar.copy(keysT[:, 512:1024], bk[1][:]).then_inc(kT_ok, 1)
            act.wait_ge(qk_mm, b + 1)
            nc.scalar.copy(att_s[a:a + 32, g, 0:512], bk[4][a:a + 32, :])
            nc.scalar.copy(att_s[a:a + 32, g, 512:1024], bk[5][a:a + 32, :])
            nc.scalar.copy(att_s[a:a + 32, g, 1024:NK], bk[3][a:a + 32, 0:TS]).then_inc(qk_ok, 1)
            if b + 2 < NB:
                load_pages(b + 2)
        for i in range(2):
            n = P * (i + 1)
            act.wait_ge(shift_ok, i + 1)
            nc.scalar.activation(probs[:, i, :, 0:n], probs[:, i, :, 0:n], ACT.Exp).then_inc(expp_ok, 1)
        for j in range(N_ATT, len(IN_JOBS)):
            act.wait_ge(job_mm, j + 1)
            m = j - N_ATT
            nc.scalar.copy(ccb[:, m // 4, m % 4], bk[1 + j % 4][:, 0:T]).then_inc(job_ok, 1)
        for n in range(6):
            act.wait_ge(ppT_mm, n + 1)
            nc.scalar.copy(probsT[:, n // 2, 4 * (n % 2):4 * (n % 2) + 4].rearrange("p h t -> p (h t)"),
                           bk[n % 4][:]).then_inc(ppT_ok, 1)
        for j in range(4):
            act.wait_ge(pvp_mm, j + 1)
            nc.scalar.copy(mixT[:, j, 0:TP], bk[4 + j][:, 0:TP]).then_inc(pvp_ok, 1)
        act.wait_ge(turn_mm, 2)
        nc.scalar.copy(conv_rows[:], bk[0][0:2 + 2 * NB, :]).then_inc(turn_ok, 1)
        act.wait_ge(turn_ok, 2)
        act.dma_start(O["conv_prompt"][0, 0], conv_rows[0:2, :]).then_inc(out_done, 16)
        act.dma_start(O["conv_sample"][0].rearrange("b j c -> (b j) c"), conv_rows[2:2 + 2 * NB, :]).then_inc(out_done, 16)
        for g in range(2):
            act.wait_ge(att_ok, 2 * (g + 1))
            nc.scalar.activation(att_s[:, g], att_s[:, g], ACT.Exp, bias=mxs[:, g:g + 1],
                                 accum_out=sms[:, g:g + 1]).then_inc(exps_ok, 1)
        for g in range(2):
            act.wait_ge(psT_mm, g + 1)
            if g == 1:
                act.wait_ge(pvs_mm, 4)
            nc.scalar.copy(pS_T[:, 0:4].rearrange("p n t -> p (n t)"), bk[4][:])
            nc.scalar.copy(pS_T[:, 4:8].rearrange("p n t -> p (n t)"), bk[5][:])
            nc.scalar.copy(pS_T[0:TS, 8], bk[6][0:TS, 0:P]).then_inc(psT_ok, 1)
        act.wait_ge(om_ok, KC)
        act.wait_ge(out_done, 16 * OUT_0)
        rms_act(act, 1, xT, sq1)
        for f in range(FC):
            act.wait_ge(gu_mm, f + 1)
            if f >= 2:
                act.wait_ge(hid_ok, f - 1)
            nc.scalar.activation(sg[:, f % 2], bk[f % 2][:, 0:T], ACT.Silu).then_inc(silu_ok, 1)

        act.wait_ge(down_ok, 8)
        rms_act(act, 2, xT, sq2)
        for i, (r, f) in enumerate(((HD, ACT.Tanh), (HD, ACT.Copy), (P, ACT.Sigmoid))):
            act.wait_ge(lh_mm, i + 1)
            nc.scalar.activation(lh[0:r, i], bk[5 + i][0:r, 0:T], f).then_inc(lh_ok, 1)
        for j in range(48):
            i, c = j // KC, j % KC
            act.wait_ge(job_mm, NIN + j + 1)
            src = bk[1 + j % 4][:, 0:T]
            if i < 2:
                v_ = VEC["rwkv_w0" if i == 0 else "rwkv_a0"] + c
                nc.scalar.activation((lwT, aT)[i][:, c], src, ACT.Sigmoid, bias=vecT[:, v_:v_ + 1]).then_inc(job_ok, 1)
            else:
                nc.scalar.copy((gT, kT, rT, vT)[i - 2][:, c], src).then_inc(job_ok, 1)
            if j == 27:
                act.wait_ge(turn_mm, 3)
                nc.scalar.copy(shift_rows[:, 0:512], bk[5][0:1 + NB, :])
                nc.scalar.copy(shift_rows[:, 512:1024], bk[6][0:1 + NB, :]).then_inc(turn_ok, 1)
                act.wait_ge(turn_ok, 3)
                act.dma_start(O["shift_prompt"][0], shift_rows[0:1, :]).then_inc(out_done, 16)
                act.dma_start(O["shift_sample"][0], shift_rows[1:1 + NB, :]).then_inc(out_done, 16)
            elif j == 33:
                act.wait_ge(t1_ok, 1)
                nc.scalar.activation(t2[:], t1[:], ACT.Square).then_inc(sqk_ok, 1)
            elif j == 39:
                act.wait_ge(nk_ok, 2)
                nc.scalar.activation(t2[:], t2[:], ACT.Sqrt).then_inc(nsq_ok, 1)
        pr = slice(0, TP)
        act.wait_ge(cum_ok, 1)
        nc.scalar.activation(t4[:, :, pr], t3[:, :, pr], ACT.Exp).then_inc(e_ok, 1)
        act.wait_ge(cum_ok, 2)
        nc.scalar.activation(t2[:, :, pr], t2[:, :, pr], ACT.Exp).then_inc(e_ok, 1)
        nc.scalar.activation(lwT[:, :, TP:T], lwT[:, :, TP:T], ACT.Exp).then_inc(e_ok, 1)
        act.wait_ge(ehat_ok, 1)
        nc.scalar.activation(t4[:, :, pr], t3[:, :, pr], ACT.Exp, scale=-1.0).then_inc(e_ok, 1)
        act.wait_ge(bn_ok, 1)
        act.dma_start(bon_dram[:, 0:7], bon[:]).then_inc(temp_out, 16)
        act.dma_start(bon_dram[:, 7], ms[:]).then_inc(temp_out, 16)
        for q in range(6):
            act.wait_ge(st_mm, q + 1)
            for i in range(2):
                last = nc.scalar.copy(st[:, q, 512 * i:512 * i + 512], bk[2 * (q % 4) + i][0:NS, :])
            last.then_inc(st_ok, 1)
        act.wait_ge(temp_out, 64)
        for p2 in range(2):
            act.wait_ge(vt_mm, p2 + 1)
            for cc in range(2):
                for i in range(2):
                    last = nc.scalar.copy(Z[CH:P, cc, 4 * i:4 * i + 4].rearrange("p h a v -> p (h a v)"),
                                          bk[i][CH * cc:CH * cc + CH, :])
            last.then_inc(vt_ok, 1)
            act.wait_ge(l_mm, p2 + 1)
            for cc in range(2):
                r = slice(CH * cc, CH * cc + CH)
                for par in range(2):
                    last = nc.scalar.copy(L[r, par].rearrange("p h s -> p (h s)"), bk[4 + 2 * cc + par][r, :])
            last.then_inc(l_ok, 1)
            for j in range(1, 6):
                for cc in range(2):
                    act.wait_ge(m_mm, 12 * p2 + 2 * j + cc + 1)
                    r = slice(CH * cc, CH * cc + CH)
                    for par in range(2):
                        last = nc.scalar.copy(M[r, par].rearrange("p h s -> p (h s)"), bk[2 * cc + par][r, :])
                    last.then_inc(m_ok, 1)
            act.wait_ge(bt_mm, p2 + 1)
            for cc in range(2):
                for i in range(2):
                    last = nc.scalar.copy(BKt[:, cc, 4 * i:4 * i + 4].rearrange("p h d -> p (h d)"), bk[2 * cc + i][:])
            last.then_inc(bt_ok, 1)
            act.wait_ge(w1_mm, p2 + 1)
            for cc in range(2):
                r = slice(CH * cc, CH * cc + CH)
                for par in range(2):
                    last = nc.scalar.copy(X[r, par].rearrange("p h s -> p (h s)"), bk[4 + 2 * cc + par][r, :])
            last.then_inc(w1_ok, 1)
            for cc in range(2):
                c = 2 * p2 + cc
                act.wait_ge(u_mm, c + 1)
                for par in range(2):
                    last = nc.scalar.copy(Z[0:CH, cc, :, par], bk[2 + par][0:CH, :].rearrange("p (h v) -> p h v", h=KC))
                last.then_inc(u_ok, 1)
                act.wait_ge(yo_mm, c + 1)
                r = slice(CH * cc, CH * cc + CH)
                for par in range(2):
                    last = nc.scalar.copy(y_rows[r, p2].rearrange("p (h a v) -> p h a v", h=KC, a=2)[:, :, par],
                                          bk[4 + par][r, :].rearrange("p (h v) -> p h v", h=KC))
                last.then_inc(yo_ok, 1)
        act.wait_ge(turn_mm, 4)
        for i in range(2):
            last = nc.scalar.copy(st_rows[:, 8 * i:8 * i + 8].rearrange("p h k -> p (h k)"), bk[i][0:HD, :])
        last.then_inc(turn_ok, 1)
        act.wait_ge(turn_ok, 4)
        act.dma_start(O["wkv_prompt"][0, 0].rearrange("h v k -> v h k"), st_rows[:]).then_inc(out_done, 16)
        for i, (t0, tn) in enumerate(TILES):
            act.wait_ge(gn_act, i + 1)
            nc.scalar.activation(gsq[0:tn, i], y_rows[0:tn, i], ACT.Square).then_inc(gnq_ok, 1)
        act.wait_ge(gns_ok, 2)
        nc.scalar.activation(gst2[:, 0:2], gst2[:, 0:2], ACT.Sqrt).then_inc(gnq_ok, 1)
        act.wait_ge(gns_ok, 3)
        nc.scalar.activation(gst2[0:NS, 2], gst2[0:NS, 2], ACT.Sqrt).then_inc(gnq_ok, 1)

        act.wait_ge(om_ok, KC + KC)
        act.wait_ge(out_done, 16 * (OUT_1 + 2))
        rms_act(act, 3, xT, sq3)
        for m in range(12):
            dst, i, half = (xr, acc)[m // 6], m // 2 % 3, m % 2
            tn = TILES[i][1]
            act.wait_ge(tk_mm, m + 1)
            nc.scalar.copy(dst[0:tn, i, 512 * half:512 * half + 512], bk[4 + m % 4][0:tn, :]).then_inc(tk_ok, 1)
        act.wait_ge(gx_ok, 1)
        for i, (t0, tn) in enumerate(TILES):
            last = nc.scalar.activation(gates[0:tn, i, 1:2], gates[0:tn, i, 1:2], ACT.Exp)
        last.then_inc(gx_ok, 1)

        def rows_in():
            for i in range(2):
                last = nc.scalar.copy(xg[:, 4 * i:4 * i + 4].rearrange("p k c -> p (k c)"), bk[6 + i][:, 0:4 * CAP])
            last.then_inc(xg_ok, 1)

        act.wait_ge(xg_mm, 1)
        rows_in()

        def rows_out(it):
            act.wait_ge(yt_mm, it + 1)
            act.wait_ge(sc_ok, 6 * it + 1)
            for half in range(2):
                last = nc.scalar.copy(ye[:, 512 * half:512 * half + 512], bk[4 + half][0:CAP, :])
            last.then_inc(ye_ok, 1)

        def expert(it):
            act.wait_ge(hid_ok, FC + FC * it)
            for f in range(FC):
                act.wait_ge(gu_mm, FC + FC * it + f + 1)
                if f >= 2:
                    act.wait_ge(hid_ok, FC + FC * it + f - 1)
                nc.scalar.activation(sg2[:, f % 2], bk[f % 2][:, 0:CAP], ACT.Silu).then_inc(silu_ok, 1)
                if f == 2:
                    rows_out(it)
            act.wait_ge(xg_mm, it + 2)
            rows_in()
            act.wait_ge(down_mm, FC * it + 2 * FC)
            for half in range(2):
                last = nc.scalar.copy(yT[:, 4 * half:4 * half + 4].rearrange("p k c -> p (k c)"), bk[2 + half][:, 0:4 * CAP])
            last.then_inc(y_ok, 1)

        act.wait_ge(blocks_ok, 1)
        n_blocks = act.value_load(blocks[0:1, 0:1], min_val=1, max_val=T // CAP)
        with act.Fori(0, n_blocks) as blk:
            with act.Fori(0, NE) as e:
                expert(blk * NE + e)
        rows_out(n_blocks * NE)
        act.wait_ge(sc_ok, n_blocks * (6 * NE) + 7)
        for i, (t0, tn) in enumerate(TILES):
            last = nc.scalar.activation(y_out[0:tn, i], acc[0:tn, i], ACT.Square, accum_out=ssf[0:tn, i:i + 1])
        last.then_inc(sq_ok, 1)
        act.wait_ge(ms_ok, 5)
        nc.scalar.activation(ssf[:], ssf[:], ACT.Sqrt).then_inc(sd_ok, 1)

    @block.vector
    def _(dve):
        link = chained(dve, dve_chain)
        V = nc.vector
        dve.wait_ge(vec_mm, 1)
        V.tensor_copy(vecT[:, 0:P + 84], bk[0][:, 0:P + 84])
        V.tensor_copy(vecT[:, 2 * P:2 * P + 64], bk[0][:, 2 * P:2 * P + 64]).then_inc(vec_ok, 1)
        dve.wait_ge(vec_ok, 1)
        rms_dve(dve, link, 0, xT, VEC["norm_mix_even"], xn)
        for j in range(8):
            dve.wait_ge(rot_mm, j + 1)
            link(V.tensor_tensor(ms[:], bk[6 + j % 2][:, 0:T], C["sin"], ALU.mult))
            dve.wait_ge(rope_pool, j + 1)
            V.tensor_tensor(rp[:, j], rp[:, j], ms[:], ALU.add).then_inc(rope_ok, 1)
            dve.wait_ge(rope_ok, j + 1)
        dve.wait_ge(iw_ok, 1)
        for i in range(2):
            for h in range(NIH):
                dve.wait_ge(ip_mm, NIH * i + h + 1)
                dst = sc_p[:, i] if h == 0 else tmp_p[:, h]
                ins = V.tensor_scalar(dst, bk[h][:, 0:TP], 0.0, iw[:, i, h:h + 1], ALU.max, ALU.mult)
                ins.then_inc(ip_ok, 1)
                dve.wait_ge(ip_ok, NIH * i + h + 1)
                if h:
                    link(V.tensor_tensor(sc_p[:, i], sc_p[:, i], tmp_p[:, h], ALU.add))
            link(V.tensor_tensor(sc_p[:, i], sc_p[:, i], C["causal"][:, i * TP:(i + 1) * TP], ALU.add))
        assert SEL_P // 8 == 2 * (NB // 2)
        for b in range(NB):
            a, g = 32 * (b % 4), b // 4
            dve.wait_ge(ikT_mm, b + 1)
            if b >= 1:
                dve.wait_ge(idx_mm, b)
            V.tensor_copy(ikeysT[:, 0:512], bk[0][:]).then_inc(ikT_ok, 1)
            dve.wait_ge(idx_mm, b + 1)
            dve.wait_ge(iws_in, 16 * NB)
            w_ = iw_s[a:a + 32, g:g + 1]
            for o in range(2):
                V.tensor_scalar(idx_s[a:a + 32, g, 0:PAST].rearrange("p (j o k) -> p j o k", o=2, k=PAGE)[:, :, o],
                                bk[6 + o][a:a + 32, :].rearrange("p (j k) -> p j k", k=PAGE), 0.0, w_, ALU.max, ALU.mult)
            V.tensor_scalar(idx_s[a:a + 32, g, 1024:NK], bk[2][a:a + 32, 0:TS], 0.0, w_, ALU.max,
                            ALU.mult).then_inc(idx_ok, 1)
            i = b // 4
            for r in range(2):
                link(V.max(top8[:], sc_p[:, i]))
                link(V.match_replace(sc_p[:, i], top8[:], sc_p[:, i], TAKEN))
            if b % 4 == 3:
                link(V.tensor_scalar(sc_p[:, i], sc_p[:, i], -2.0e38, NEG, ALU.is_gt, ALU.mult))
                link(V.tensor_tensor(sc_p[:, i], sc_p[:, i], C["causal"][:, i * TP:(i + 1) * TP], ALU.add))
        dve.wait_ge(isum_mm, 1)
        V.tensor_copy(sc_s[:, 0:512], bk[6][0:NS, :])
        V.tensor_copy(sc_s[:, 512:1024], bk[7][0:NS, :])
        V.tensor_tensor(sc_s[:, 1024:NK], bk[2][0:NS, 0:TS], C["causal_new"][0:NS], ALU.add).then_inc(sel_ok, 1)
        for i in range(2):
            n = P * (i + 1)
            for h in range(NQ):
                dve.wait_ge(sp_mm, NQ * i + h + 1)
                V.scalar_tensor_tensor(probs[:, i, h, 0:n], bk[(NQ * i + h) % 4][:, 0:n], HD ** -0.5,
                                       sc_p[:, i, 0:n], ALU.mult, ALU.add).then_inc(sp_ok, 1)
            dve.wait_ge(sp_ok, NQ * (i + 1))
            link(V.tensor_reduce(mxp[:, i], probs[:, i, :, 0:n], AX.X, ALU.max))
            V.tensor_tensor(probs[:, i, :, 0:n], probs[:, i, :, 0:n],
                            mxp[:, i].unsqueeze(2).broadcast_to([P, NQ, n]), ALU.subtract).then_inc(shift_ok, 1)
        for i in range(2):
            n = P * (i + 1)
            dve.wait_ge(expp_ok, i + 1)
            link(V.tensor_reduce(smp[:, i], probs[:, i, :, 0:n], AX.X, ALU.add))
            link(V.reciprocal(smp[:, i], smp[:, i]))
            V.tensor_tensor(probs[:, i, :, 0:n], probs[:, i, :, 0:n],
                            smp[:, i].unsqueeze(2).broadcast_to([P, NQ, n]), ALU.mult).then_inc(pp_ok, 1)
        dve.wait_ge(sel_ok, 1)
        for r in range(SEL_S // 8):
            link(V.max(top8[0:NS], sc_s[:]))
            link(V.match_replace(sc_s[:], top8[0:NS], sc_s[:], TAKEN))
        V.tensor_scalar(sc_s[:], sc_s[:], -2.0e38, NEG, ALU.is_gt, ALU.mult).then_inc(sel_ok, 2)
        dve.wait_ge(omp_mm, 1)
        for i in range(4):
            last = V.tensor_tensor(xT[:, 2 * i:2 * i + 2, 0:TP], xT[:, 2 * i:2 * i + 2, 0:TP],
                                   bk[4 + i][:].rearrange("p (c t) -> p c t", c=2), ALU.add)
        last.then_inc(omp_ok, 1)
        for g in range(2):
            dve.wait_ge(spread_mm, g + 1)
            dve.wait_ge(qk_ok, NB)
            for o, (c0, c1) in zip((1, 2, 3), ((0, 512), (512, 1024), (1024, NK))):
                last = V.scalar_tensor_tensor(att_s[:, g, c0:c1], att_s[:, g, c0:c1], HD ** -0.5, bk[o][:, 0:c1 - c0],
                                              ALU.mult, ALU.add)
            last.then_inc(att_ok, 1)
            dve.wait_ge(att_ok, 2 * g + 1)
            link(V.tensor_reduce(mxs[:, g:g + 1], att_s[:, g], AX.X, ALU.max))
            V.tensor_scalar(mxs[:, g:g + 1], mxs[:, g:g + 1], -1.0, None, ALU.mult).then_inc(att_ok, 1)
        for g in range(2):
            dve.wait_ge(exps_ok, g + 1)
            link(V.reciprocal(sms[:, g:g + 1], sms[:, g:g + 1]))
            V.tensor_scalar(att_s[:, g], att_s[:, g], sms[:, g:g + 1], None, ALU.mult).then_inc(ps_ok, 1)
        dve.wait_ge(pvs_mm, NB)
        o_s = bk[7][:, 0:256].rearrange("p (b h t) -> p h b t", b=NB, h=NQ)
        for g in range(2):
            last = V.tensor_copy(mixT[HD * g:HD * g + HD, 0:4, TP:T].rearrange("p j (b t) -> p j b t", b=NB),
                                 o_s[HD * g:HD * g + HD, 4 * g:4 * g + 4])
        last.then_inc(pvs_ok, 1)
        dve.wait_ge(om_mm, KC)
        V.tensor_tensor(xT[:, :, TP:T], xT[:, :, TP:T], bk[1][:, 0:KC * NS].rearrange("p (c t) -> p c t", c=KC),
                        ALU.add).then_inc(om_ok, KC)
        dve.wait_ge(om_ok, KC)
        rms_dve(dve, link, 1, xT, VEC["norm_ffn_even"], xn1)
        for f in range(FC):
            dve.wait_ge(silu_ok, f + 1)
            V.tensor_tensor(hid[:, f], sg[:, f % 2], bk[2 + f % 2][:, 0:T], ALU.mult).then_inc(hid_ok, 1)
        for half in range(2):
            dve.wait_ge(down_mm, (half + 1) * (FC // 2))
            for c in range(4):
                o = (4, 5, 6, 7)[c] if half == 0 else c
                V.tensor_tensor(xT[:, 4 * half + c], xT[:, 4 * half + c], bk[o][:, 0:T], ALU.add).then_inc(down_ok, 1)

        dve.wait_ge(down_ok, 8)
        rms_dve(dve, link, 2, xT, VEC["norm_mix_odd"], xn2)
        dve.wait_ge(xn_ok, 3 * KC)
        xs = xn2[:, :, TP:T].rearrange("p c (b t) -> p c b t", b=NB)
        ds_ = xx[:, :, TP:T].rearrange("p c (b t) -> p c b t", b=NB)
        shiftT = vecT[:, VEC["state_shift"]:VEC["state_shift"] + 64].rearrange("p (b c) -> p c b", b=NB)
        V.tensor_tensor(xx[:, :, 1:TP], xn2[:, :, 0:TP - 1], xn2[:, :, 1:TP], ALU.subtract)
        V.tensor_scalar(xx[:, :, 0:1], xn2[:, :, 0:1], -1.0, None, ALU.mult)
        for c in range(KC):
            V.tensor_tensor(ds_[:, c, :, 1:TS], xs[:, c, :, 0:TS - 1], xs[:, c, :, 1:TS], ALU.subtract)
        V.tensor_tensor(ds_[:, :, :, 0], shiftT, xs[:, :, :, 0], ALU.subtract).then_inc(xx_ok, 1)
        dve.wait_ge(xx_ok, 1)
        for i, m in enumerate((1, 4, 5, 2, 0, 3)):
            if i == 5:
                dve.wait_ge(job_mm, NIN + 32)
            elif i >= 2:
                dve.wait_ge(lh_mm, i - 1)
            for c in range(KC):
                v_ = VEC["mu"] + KC * m + c
                V.scalar_tensor_tensor(mx[:, i % 2, c], xx[:, c], vecT[:, v_:v_ + 1], xn2[:, c],
                                       ALU.mult, ALU.add).then_inc(mix_ok, 1)
        ka = VEC["rwkv_k_a"]
        pr = slice(0, TP)
        link(V.tensor_scalar(omk[:], vecT[:, ka:ka + KC], -1.0, 1.0, ALU.mult, ALU.add))
        for half in range(2):
            dve.wait_ge(hs_mm, half + 1)
            for c in range(4):
                last = V.tensor_scalar(t2[:, 4 * half + c], bk[(0, 5, 6, 7)[c]][:, 0:T], 1.0e-24, None, ALU.max)
            last.then_inc(nk_ok, 1)
        dve.wait_ge(nsq_ok, 1)
        link(V.reciprocal(t2[:], t2[:]))
        link(V.tensor_tensor(t1[:], t1[:], t2[:], ALU.mult))
        for c in range(KC):
            last = V.tensor_scalar(t3[:, c], aT[:, c], vecT[:, ka + c:ka + c + 1], omk[:, c:c + 1], ALU.mult, ALU.add)
        link(last)
        link(V.tensor_tensor(kT[:], kT[:], t3[:], ALU.mult))
        dve.wait_ge(job_ok, NIN + 40)
        for c in range(KC):
            v_ = VEC["rwkv_r_k"] + c
            last = V.scalar_tensor_tensor(t2[:, c], rT[:, c], vecT[:, v_:v_ + 1], kT[:, c], ALU.mult, ALU.mult)
        last.then_inc(rk_ok, 1)
        V.tensor_tensor(aT[:], t1[:], aT[:], ALU.mult)
        link(V.tensor_scalar(lwT[:], lwT[:], -float(np.exp(np.float64(-0.5))), None, ALU.mult))
        for c in range(KC):
            for k in range(NCH):
                s_ = slice(k * CH, k * CH + CH)
                last = V.tensor_tensor_scan(t3[:, c, s_], C["ones"][:, 0:CH], lwT[:, c, s_], 0.0, ALU.mult, ALU.add)
        last.then_inc(cum_ok, 1)
        dve.wait_ge(cum_ok, 1)
        dve.wait_ge(hs_mm, 3)
        for c in range(KC):
            last = V.tensor_copy(bon[:, c] if c < 7 else ms[:], bk[c][:, 0:T])
        last.then_inc(bn_ok, 1)
        V.tensor_tensor(t2[:, :, pr], t3[:, :, pr], lwT[:, :, pr], ALU.subtract).then_inc(cum_ok, 1)
        dve.wait_ge(e_ok, 1)

        def tok(t):
            return t[:, :, pr].rearrange("p c (k t) -> p c k t", k=NCH)

        V.tensor_copy(PC[:], tok(t4)[:, :, :, CH - 1])
        V.tensor_tensor(AR[:, :, :, 1], tok(rT), tok(t4), ALU.mult).then_inc(ehat_ok, 1)
        dve.wait_ge(e_ok, 2)
        for c in range(KC):
            V.scalar_tensor_tensor(AR[:, c, :, 0], t1[:, c, pr].rearrange("p (k t) -> p k t", k=NCH), -1.0,
                                   t2[:, c, pr].rearrange("p (k t) -> p k t", k=NCH), ALU.mult, ALU.mult)
        dve.wait_ge(e_ok, 4)
        V.tensor_tensor(BK[:, :, :, 0], tok(aT), tok(t4), ALU.mult)
        V.tensor_tensor(BK[:, :, :, 1], tok(kT), tok(t4), ALU.mult).then_inc(arbk_ok, 1)

        def sample_part(n):
            t, third = n // 3, n % 3
            r_, w_, k_, v_, kk_, b_ = (s6[:, t, q] for q in range(6))
            rows_ = slice(POOL_ROWS, HD)
            Sh = S[:, rows_]
            key = lambda x: x.unsqueeze(1).broadcast_to([P, HD - POOL_ROWS, HD])
            val = lambda x: x[:, rows_].unsqueeze(2).broadcast_to([P, HD - POOL_ROWS, HD])
            if n == 0:
                dve.wait_ge(s6_in, 16 * (NB + 1))
            if third == 0:
                link(V.tensor_tensor(dtmp[:], Sh, key(kk_), ALU.mult))
                link(V.tensor_reduce(sa[:, rows_], dtmp[:], AX.X, ALU.add))
                link(V.tensor_tensor(Sh, Sh, key(w_), ALU.mult))
            elif third == 1:
                link(V.tensor_tensor(dtmp[:], val(sa), key(b_), ALU.mult))
                link(V.tensor_tensor(Sh, Sh, dtmp[:], ALU.subtract))
                link(V.tensor_tensor(dtmp[:], val(v_), key(k_), ALU.mult))
            else:
                link(V.tensor_tensor(Sh, Sh, dtmp[:], ALU.add))
                link(V.tensor_tensor(dtmp[:], Sh, key(r_), ALU.mult))
                last = V.tensor_reduce(ys[:, t, rows_], dtmp[:], AX.X, ALU.add)
                if t < TS - 1:
                    link(last)
                else:
                    last.then_inc(ys_ok, 1)

        dve.wait_ge(st_out, 16 * 6)
        for p2 in range(2):
            for gi in range(8):
                cc, par, half = gi // 4, gi // 2 % 2, gi % 2
                dve.wait_ge(g_mm, 8 * p2 + gi + 1)
                V.tensor_tensor(G[:, cc, par, 4 * half:4 * half + 4], bk[gi][:].rearrange("p (h t) -> p h t", h=4),
                                C["delta_mask"].unsqueeze(1).broadcast_to([P, 4, P]), ALU.mult).then_inc(g_ok, 1)

            def add_to(dst, first, other, cc):
                r = slice(CH * cc, CH * cc + CH)
                for par in range(2):
                    last = V.tensor_tensor(dst[r, par], bk[first + 2 * cc + par][r, :].rearrange(
                        "p (h s) -> p h s", h=KC), other(r, par), ALU.add)
                return last

            eye = lambda r, par: C["ident64"][r].unsqueeze(1).broadcast_to([CH, KC, CH])
            def masked(j):
                mask = C["levels"][:, j * CH:(j + 1) * CH].unsqueeze(1).broadcast_to([P, KC, CH])
                for par in range(2):
                    last = V.tensor_tensor(Cj[:, par], L[:, par], mask, ALU.mult)
                last.then_inc(c_ok, 1)

            dve.wait_ge(l_ok, p2 + 1)
            masked(0)
            dve.wait_ge(c_ok, 6 * p2 + 1)
            for par in range(2):
                V.tensor_tensor(X[:, par], Cj[:, par], C["ident64"].unsqueeze(1).broadcast_to([P, KC, CH]), ALU.add)
            for cc in range(2):
                dve.wait_ge(m_mm, 12 * p2 + cc + 1)
                add_to(Y, 0, eye, cc).then_inc(xy_ok, 1)
            dve.wait_ge(xy_ok, 12 * p2 + 2)
            masked(1)
            sample_part(6 * p2)
            for j in range(1, 6):
                if j < 5:
                    dve.wait_ge(m_mm, 12 * p2 + 2 * j + 2)
                    masked(j + 1)
                for cc in range(2):
                    dve.wait_ge(xy_ok, 12 * p2 + 2 * (j - 1) + cc + 1)
                    dve.wait_ge(y_mm, 10 * p2 + 2 * (j - 1) + cc + 1)
                    last = add_to(Y, 4, lambda r, par: Y[r, par], cc)
                    if j < 5:
                        dve.wait_ge(x_mm, 8 * p2 + 2 * (j - 1) + cc + 1)
                        last = add_to(X, 0, lambda r, par: X[r, par], cc)
                    last.then_inc(xy_ok, 1)
                sample_part(6 * p2 + j)
            for cc in range(2):
                c = 2 * p2 + cc
                r = slice(CH * cc, CH * cc + CH)
                if c:
                    dve.wait_ge(w1_ok, p2 + 1)
                    dve.wait_ge(w2_mm, c)
                    for par in range(2):
                        last = V.tensor_tensor(X[r, par], bk[par][r, :].rearrange("p (h s) -> p h s", h=KC),
                                               X[r, par], ALU.add)
                    last.then_inc(w_ok, 1)
                dve.wait_ge(s_mm, c + 1)
                dve.wait_ge(yo_mm, c + 1)
                upd = bk[6][:].rearrange("p (h v) -> p h v", h=KC)
                if c:
                    link(V.tensor_tensor(ST[:], upd, ST[:], ALU.add))
                    upd = ST[:]
                V.tensor_tensor(ST[:], upd, PC[:, :, c:c + 1].broadcast_to([P, KC, CH]), ALU.mult).then_inc(s_ok, 1)
        heads = lambda x, tn, i: x[0:tn, i].rearrange("p (h v) -> p h v", h=RH)
        spread = lambda x, tn, i: x[0:tn, i].unsqueeze(2).broadcast_to([tn, RH, HD])
        for i, (t0, tn) in enumerate(TILES):
            if i < 2:
                dve.wait_ge(yo_ok, 2 * (i + 1))
            else:
                dve.wait_ge(yrow_in, 16)
            y_ = heads(y_rows, tn, i)
            link(V.tensor_reduce(gst[0:tn, i], y_, AX.X, ALU.add))
            link(V.tensor_scalar(gst[0:tn, i], gst[0:tn, i], 1.0 / HD, None, ALU.mult))
            V.tensor_tensor(y_, y_, spread(gst, tn, i), ALU.subtract).then_inc(gn_act, 1)
        for i, (t0, tn) in enumerate(TILES):
            dve.wait_ge(gnq_ok, i + 1)
            link(V.tensor_reduce(gst2[0:tn, i], heads(gsq, tn, i), AX.X, ALU.add))
            V.tensor_scalar(gst2[0:tn, i], gst2[0:tn, i], 1.0 / HD, GN_EPS, ALU.mult, ALU.add).then_inc(gns_ok, 1)
        dve.wait_ge(bonT_in, 16)
        V.tensor_tensor(bonT[:], bonT[:], vT[:], ALU.mult)
        dve.wait_ge(gnq_ok, 4)
        link(V.reciprocal(gst2[:, 0:2], gst2[:, 0:2]))
        dve.wait_ge(gnq_ok, 5)
        link(V.reciprocal(gst2[0:NS, 2], gst2[0:NS, 2]))
        dve.wait_ge(gn_act, 3)
        for i, (t0, tn) in enumerate(TILES):
            V.tensor_tensor(heads(y_rows, tn, i), heads(y_rows, tn, i), spread(gst2, tn, i),
                            ALU.mult).then_inc(gn_ok, 1)
        for c in range(KC):
            dve.wait_ge(yT_mm, c + 1)
            w_, b_ = VEC["rwkv_ln_w"] + c, VEC["rwkv_ln_b"] + c
            link(V.tensor_scalar(oT[:, c], bk[2 + c % 4][:, 0:T], vecT[:, w_:w_ + 1], vecT[:, b_:b_ + 1],
                                 ALU.mult, ALU.add))
            link(V.tensor_tensor(oT[:, c], oT[:, c], bonT[:, c], ALU.add))
            V.tensor_tensor(oT[:, c], oT[:, c], gT[:, c], ALU.mult).then_inc(oT_ok, 1)
        for c in range(KC):
            dve.wait_ge(om_mm, KC + c + 1)
            V.tensor_tensor(xT[:, c], xT[:, c], bk[2 + c % 4][:, 0:T], ALU.add).then_inc(om_ok, 1)

        dve.wait_ge(om_ok, KC + KC)
        rms_dve(dve, link, 3, xT, VEC["norm_ffn_odd"], xn3)
        V.memset(rank[:], -1.0)
        V.memset(share[:], 0.0)
        link(V.memset(ssf[:], 1.0))
        dve.wait_ge(lg_mm, 1)
        for i, (t0, tn) in enumerate(TILES):
            r = slice(0, tn)
            link(V.tensor_copy(lg[r, i], bk[1][r, NE * i:NE * i + NE]))
            link(V.max(top_v[r, i], lg[r, i]))
            link(V.max_index(top_i[r, i], top_v[r, i], lg[r, i]))
            link(V.tensor_copy(top_f[r, i], top_i[r, i]))
            V.tensor_scalar(hot1[r, i], C["slots"][r, 0:NE], top_f[r, i, 0:1], None, ALU.is_equal)
            V.tensor_scalar(hot2[r, i], C["slots"][r, 0:NE], top_f[r, i, 1:2], None, ALU.is_equal)
            link(V.tensor_tensor(gates[r, i, 1:2], top_v[r, i, 1:2], top_v[r, i, 0:1], ALU.subtract))
            last = V.tensor_tensor(sel[r, i], hot1[r, i], hot2[r, i], ALU.add)
        last.then_inc(sel2_ok, 1)
        dve.wait_ge(sel2_ok, 1)
        V.tensor_copy(blocks_f[0:1, 0:1], gates[0:1, 0, 1:2]).then_inc(gx_ok, 1)
        dve.wait_ge(gx_ok, 2)
        for i, (t0, tn) in enumerate(TILES):
            r = slice(0, tn)
            link(V.tensor_scalar(gates[r, i, 0:1], gates[r, i, 1:2], 1.0, None, ALU.add))
            link(V.reciprocal(gates[r, i, 0:1], gates[r, i, 0:1]))
            link(V.tensor_tensor(gates[r, i, 1:2], gates[r, i, 1:2], gates[r, i, 0:1], ALU.mult))
            link(V.tensor_scalar(comb[r, i], hot1[r, i], gates[r, i, 0:1], None, ALU.mult))
            link(V.scalar_tensor_tensor(comb[r, i], hot2[r, i], gates[r, i, 1:2], comb[r, i], ALU.mult, ALU.add))
        dve.wait_ge(rank_mm, 1)
        for i, (t0, tn) in enumerate(TILES):
            r = slice(0, tn)
            link(V.scalar_tensor_tensor(rank[r, i, 0:NE], bk[2][r, NE * i:NE * i + NE], 1.0, sel[r, i], ALU.add, ALU.mult))
            link(V.tensor_scalar(rank[r, i, 0:NE], rank[r, i, 0:NE], -1.0, None, ALU.add))
            for b in range(T // CAP):
                if b:
                    V.tensor_scalar(rank[r, i, NE * b:NE * b + NE], rank[r, i, 0:NE], -float(CAP * b), None, ALU.add)
                link(V.tensor_copy(share[r, i, NE * b:NE * b + NE], comb[r, i]))
        link(V.tensor_reduce(blocks_f[0:1, 0:1], bk[2][0:1, 4 * NE:5 * NE], AX.X, ALU.max))
        link(V.tensor_scalar(blocks_f[0:1, 1:2], blocks_f[0:1, 0:1], float(CAP), 1.0, ALU.is_gt, ALU.add))
        for b in range(2, T // CAP):
            link(V.tensor_scalar(blocks_f[0:1, 2:3], blocks_f[0:1, 0:1], float(CAP * b), None, ALU.is_gt))
            link(V.tensor_tensor(blocks_f[0:1, 1:2], blocks_f[0:1, 1:2], blocks_f[0:1, 2:3], ALU.add))
        V.tensor_copy(blocks[:], blocks_f[0:1, 1:2]).then_inc(blocks_ok, 1)
        for i, (t0, tn) in enumerate(TILES):
            last = V.tensor_scalar(pick[0:tn, i], C["slots"][0:tn, 0:CAP], rank[0:tn, i, 0:1], None, ALU.is_equal)
        last.then_inc(pick_ok, 1)

        def expert(it):
            dve.wait_ge(xg_mm, it + 1)
            dve.wait_ge(down_mm, FC * it + FC)
            for i, (t0, tn) in enumerate(TILES):
                r = slice(0, tn)
                V.tensor_scalar(give[r, i], C["slots"][r, 0:CAP], rank[r, i, bass.ds(it, 1)],
                                share[r, i, bass.ds(it, 1)], ALU.is_equal, ALU.mult)
                last = V.tensor_scalar(pick[r, i], C["slots"][r, 0:CAP], rank[r, i, bass.ds(it + 1, 1)], None,
                                       ALU.is_equal)
            last.then_inc(pick_ok, 1)
            for f in range(FC):
                dve.wait_ge(silu_ok, FC + FC * it + f + 1)
                V.tensor_tensor(hid2[:, f], sg2[:, f % 2], bk[f % 2][:, CAP:2 * CAP], ALU.mult).then_inc(hid_ok, 1)
                if 5 <= f < 11:
                    add_rows(it, f - 5)
            dve.wait_ge(gt_mm, it + 1)
            V.tensor_copy(giveT[:], bk[4][0:CAP, 0:T]).then_inc(gt_ok, 1)

        def add_rows(it, g):
            if g == 0:
                dve.wait_ge(sc_ok, 6 * it + 1)
            i, half = g // 2, g % 2
            tn = TILES[i][1]
            dve.wait_ge(sc_mm, 6 * it + g + 1)
            a = acc[0:tn, i, 512 * half:512 * half + 512]
            V.tensor_tensor(a, a, bk[(4, 5, 2, 3)[g % 4]][0:tn, :], ALU.add).then_inc(sc_ok, 1)

        V.memset(yT[:], 0.0).then_inc(y_ok, 1)
        V.memset(giveT[:], 0.0).then_inc(gt_ok, 1)
        dve.wait_ge(tk_ok, 12)
        V.tensor_copy(blocks_f[0:1, 3:4], blocks_f[0:1, 1:2]).then_inc(sc_ok, 1)
        dve.wait_ge(blocks_ok, 1)
        n_blocks = dve.value_load(blocks[0:1, 0:1], min_val=1, max_val=T // CAP)
        with dve.Fori(0, n_blocks) as blk:
            with dve.Fori(0, NE) as e:
                expert(blk * NE + e)
        for g in range(6):
            add_rows(n_blocks * NE, g)
        dve.wait_ge(sq_ok, 4 * KC + 1)
        V.tensor_scalar(ssf[:], ssf[:], 1.0 / D, EPS, ALU.mult, ALU.add).then_inc(ms_ok, 1)
        dve.wait_ge(sd_ok, 5)
        link(V.reciprocal(ssf[:], ssf[:]))
        dve.wait_ge(rt_in, 32)
        for i, (t0, tn) in enumerate(TILES):
            V.scalar_tensor_tensor(y_out[0:tn, i], acc[0:tn, i], ssf[0:tn, i:i + 1], gain_f[0:tn], ALU.mult,
                                   ALU.mult).then_inc(fin_ok, 1)

    @block.gpsimd
    def _(pool):
        link = chained(pool, pool_chain)
        G = nc.gpsimd
        pool.dma_start(pg_ids[:], I["page_table"].rearrange("b n -> (b n)").unsqueeze(0)).then_inc(ids_in, 16)
        for t in (q_s, iq_s, iw_s):
            link(pool.memset(t[:], 0.0))

        def load_pages(b):
            if b >= 2:
                pool.wait_ge(ikT_mm, b - 1)
            with pool.Fori(SP_IK_PAGES, NPG) as g:
                load_page(pool, b, g, "cache_idx_k", ik_pages[:, b % 2, bass.ds(g, 1)], ik_page_in[b % 2])

        pool.wait_ge(ids_in, 16)
        load_pages(0)
        load_pages(1)
        pool.wait_ge(head_in, HEAD)
        for j in range(8):
            pool.wait_ge(job_ok, j + 1)
            G.tensor_tensor(rp[:, j], raw[:, j], C["cos"], ALU.mult).then_inc(rope_pool, 1)
        pool.wait_ge(rope_ok, 8)
        for g in range(2):
            r = slice(HD * g, HD * g + HD)
            src = rp[r, 4:8, TP:T].rearrange("p j (b t) -> p b j t", b=NB)
            dst = q_s[r, :, 16 * g:16 * g + 16].rearrange("p b (j t) -> p b j t", j=4)
            for b in range(NB):
                last = G.tensor_copy(dst[:, b], src[:, b])
            link(last)
            for h in range(NIH):
                a = HD * (h % 2)
                last = G.tensor_copy(iq_s[r, :, 0:16].rearrange("p b (t h) -> p b t h", h=NIH)[:, :, :, h],
                                     rp[a:a + HD, 2 + h // 2, TP:T].rearrange("p (b t) -> p b t", b=NB))
                if h < NIH - 1:
                    link(last)
            last.then_inc(qs_ok, 2)
            pool.wait_ge(qs_ok, 2 * (g + 1))
        for b in range(NB):
            if b >= 1:
                pool.wait_ge(qk_mm, b)
            G.tensor_copy(keysT[:, 1024:NK], rp[:, 0, TP + TS * b:TP + TS * b + TS]).then_inc(new_ok, 1)
            if b >= 1:
                pool.wait_ge(idx_mm, b)
            G.tensor_copy(ikeysT[:, 512:512 + TS], rp[:, 1, TP + TS * b:TP + TS * b + TS]).then_inc(new_ok, 1)
            if b + 2 < NB:
                load_pages(b + 2)
        pool.wait_ge(vec_ok, 1)
        pool.wait_ge(job_ok, N_ATT + 8)
        pool.wait_ge(turn_mm, 1)
        link(G.memset(u_p[:, :, 0:2], 0.0))
        conv_prev = vecT[:, 256:320].rearrange("p (b j c) -> p c b j", b=NB, j=2)
        for c in range(4):
            G.tensor_copy(u_s[:, c, :, 0:2], conv_prev[:, c])
            G.tensor_tensor(u_p[:, c, 2:2 + TP], ccb[:, 0, c, 0:TP], ccb[:, 1, c, 0:TP], ALU.mult)
            link(G.tensor_tensor(u_s[:, c, :, 2:2 + TS], ccb[:, 0, c, TP:T].rearrange("p (b t) -> p b t", b=NB),
                                 ccb[:, 1, c, TP:T].rearrange("p (b t) -> p b t", b=NB), ALU.mult))
        G.tensor_copy(u_last[:, :, 0:2], u_p[:, :, TP:TP + 2])
        for c in range(4):
            last = G.tensor_copy(u_last[:, c, 2:2 + 2 * NB].rearrange("p (b j) -> p b j", j=2), u_s[:, c, :, TS:TS + 2])
        last.then_inc(conv_ok, 1)
        for c in range(4):
            y_p = mixT[:, 4 + c, 0:TP]
            y_s = mixT[:, 4 + c, TP:T].rearrange("p (b t) -> p b t", b=NB)
            for j in range(3):
                w_ = vecT[:, VEC["conv_w"] + 4 * j + c:VEC["conv_w"] + 4 * j + c + 1]
                if j == 0:
                    G.tensor_scalar(y_p, u_p[:, c, 0:TP], w_, None, ALU.mult)
                    link(G.tensor_scalar(y_s, u_s[:, c, :, 0:TS], w_, None, ALU.mult))
                else:
                    t_p = ccb[:, 0, c, 0:TP]
                    t_s = ccb[:, 0, c, TP:T].rearrange("p (b t) -> p b t", b=NB)
                    G.tensor_scalar(t_p, u_p[:, c, j:j + TP], w_, None, ALU.mult)
                    link(G.tensor_scalar(t_s, u_s[:, c, :, j:j + TS], w_, None, ALU.mult))
                    G.tensor_tensor(y_p, y_p, t_p, ALU.add)
                    link(G.tensor_tensor(y_s, y_s, t_s, ALU.add))
            pool.wait_ge(job_ok, N_ATT + 8 + c + 1)
            G.tensor_tensor(mixT[:, 4 + c], mixT[:, 4 + c], ccb[:, 2, c], ALU.mult).then_inc(conv_ok, 1)

        G_ = nc.gpsimd
        pool.wait_ge(xn_ok, 3 * KC)
        pool.wait_ge(lh_mm, 3)
        pool.wait_ge(job_mm, NIN + 24)
        G_.tensor_copy(e_last[:, :, 0], xn2[:, :, TP - 1]).then_inc(el_ok, 1)
        G_.tensor_copy(e_last[:, :, 1:1 + NB], xn2[:, :, TP:T].rearrange("p c (b t) -> p c b t", b=NB)[:, :, :, TS - 1]
                       ).then_inc(el_ok, 1)
        pool.wait_ge(out_done, 16 * OUT_1)
        for c in range(KC):
            pool.wait_ge(job_ok, NIN + 24 + c + 1)
            v_ = VEC["rwkv_k_k"] + c
            last = G_.tensor_scalar(t1[:, c], kT[:, c], vecT[:, v_:v_ + 1], None, ALU.mult)
        last.then_inc(t1_ok, 1)

        def key_sum(out):
            w = HD // 2
            while w > 1:
                link(G_.tensor_tensor(stmp[:, :, 0:w], stmp[:, :, 0:w], stmp[:, :, w:2 * w], ALU.add))
                w //= 2
            return G_.tensor_tensor(out, stmp[:, :, 0], stmp[:, :, 1], ALU.add)

        def sample_step(t):
            r_, w_, k_, v_, kk_, b_ = (s6[:, t, q] for q in range(6))
            n = POOL_ROWS // 2
            key = lambda x: x.unsqueeze(1).broadcast_to([P, n, HD])
            for half in range(2):
                rows_ = slice(n * half, n * half + n)
                Sh = S[:, rows_]
                val = lambda x: x[:, rows_].unsqueeze(2).broadcast_to([P, n, HD])
                link(G_.tensor_tensor(stmp[:], Sh, key(kk_), ALU.mult))
                link(key_sum(sa[:, rows_]))
                link(G_.tensor_tensor(Sh, Sh, key(w_), ALU.mult))
                link(G_.tensor_tensor(stmp[:], val(sa), key(b_), ALU.mult))
                link(G_.tensor_tensor(Sh, Sh, stmp[:], ALU.subtract))
                link(G_.tensor_tensor(stmp[:], val(v_), key(k_), ALU.mult))
                link(G_.tensor_tensor(Sh, Sh, stmp[:], ALU.add))
                link(G_.tensor_tensor(stmp[:], Sh, key(r_), ALU.mult))
                last = key_sum(ys[:, t, rows_])
                if half and t == TS - 1:
                    last.then_inc(ys_ok, 1)
                else:
                    link(last)

        pool.wait_ge(s6_in, 16 * (NB + 1))
        for t in range(TS):
            sample_step(t)

    ctx.close()


INPUTS = ["x_prompt", "x_sample", "cache_k", "cache_v", "cache_idx_k", "state_conv", "state_shift", "state_wkv",
          "page_table", "norm_mix_even", "w_in_even", "conv_w", "w_out_even", "norm_ffn_even", "ffn_gate", "ffn_up",
          "ffn_down", "norm_mix_odd", "rwkv_mu", "rwkv_w_rkv", "rwkv_w0", "rwkv_w1", "rwkv_w2", "rwkv_a0",
          "rwkv_a1", "rwkv_a2", "rwkv_g1", "rwkv_g2", "rwkv_k_k", "rwkv_k_a", "rwkv_r_k", "rwkv_ln_w", "rwkv_ln_b",
          "rwkv_w_o", "norm_ffn_odd", "moe_router", "moe_gate", "moe_up", "moe_down", "norm_final"]
OUTPUTS = [("y_prompt", (1, TP, D)), ("y_sample", (NB, TS, D)), ("k_prompt", (1, 1, TP, NKV, HD)),
           ("v_prompt", (1, 1, TP, NKV, HD)), ("idx_k_prompt", (1, 1, TP, HD)), ("k_sample", (1, NB, TS, NKV, HD)),
           ("v_sample", (1, NB, TS, NKV, HD)), ("idx_k_sample", (1, NB, TS, HD)), ("conv_prompt", (1, 1, 2, CONV)),
           ("conv_sample", (1, NB, 2, CONV)), ("shift_prompt", (1, 1, D)), ("shift_sample", (1, NB, D)),
           ("wkv_prompt", (1, 1, RH, HD, HD)), ("wkv_sample", (1, NB, RH, HD, HD))]


def kernel(**inputs):
    import concourse.bacc as bacc
    from concourse.bass_utils import run_bass_kernel_spmd

    nc = bacc.Bacc("TRN2", target_bir_lowering=False, num_devices=1)
    arrays, I, O = {}, {}, {}
    for name in INPUTS:
        a = np.ascontiguousarray(inputs[name])
        arrays[f"in_{name}"] = a
        I[name] = nc.dram_tensor(f"in_{name}", a.shape, mybir.dt.from_np(a.dtype), kind="ExternalInput").ap()
    arrays["in_consts"] = np.concatenate([CONSTS[k] for k in COL], 1)
    I["consts"] = nc.dram_tensor("in_consts", arrays["in_consts"].shape, F32, kind="ExternalInput").ap()
    for name, shape in OUTPUTS:
        O[name] = nc.dram_tensor(f"out_{name}", shape, F32, kind="ExternalOutput").ap()
    build(nc, I, O)
    r = run_bass_kernel_spmd(nc, [arrays], core_ids=[0])
    return tuple(r.results[0][f"out_{name}"] for name, _ in OUTPUTS)
```
